# Optimizing a Trainium2 kernel written in Bass

```python
import functools
import jax
import jax.numpy as jnp
from jax import lax
import numpy as np

D_MODEL = 1024
BATCH = 1
SEQ = 512
DEPTH = 1
DEC_BATCH = 8
DEC_SEQ = 8
PAST_LEN = 1024
PAGE_SIZE = 128

N_HEADS = 16
N_KV_HEADS = 2
HEAD_DIM = 64
GROUP = N_HEADS // N_KV_HEADS
WINDOW = 128
ATTN_BLOCK = WINDOW
Q_W = N_HEADS * HEAD_DIM
KV_W = N_KV_HEADS * HEAD_DIM
CONV_DIM = D_MODEL
CONV_WIDTH = 3
IN_SPLITS = (
    Q_W,
    Q_W + KV_W,
    Q_W + 2 * KV_W,
    Q_W + 2 * KV_W + CONV_DIM,
    Q_W + 2 * KV_W + 2 * CONV_DIM,
    Q_W + 2 * KV_W + 3 * CONV_DIM,
    Q_W + 2 * KV_W + 3 * CONV_DIM + D_MODEL,
)
IN_COLS = Q_W + 2 * KV_W + 3 * CONV_DIM + 2 * D_MODEL
N_EXPERTS = 64
TOP_K = 6
N_GROUPS = 8
TOPK_GROUPS = 4
EXPERT_FF = 256
SHARED_FF = 256
ROUTED_SCALE = 2.5
MOE_BLOCK = 128
PLE_DIM = 256
LN_EPS = 1e-5
DN_ALPHA = (2 * DEPTH) ** 0.25
DN_BETA = (8 * DEPTH) ** -0.25

kernel_name = "hybrid_swa_sink_shortconv_moe_deepnorm_step"

def layer_norm(x, g, b):
    xf = x.astype(jnp.float32)
    mu = jnp.mean(xf, axis=-1, keepdims=True)
    xc = xf - mu
    var = jnp.mean(xc * xc, axis=-1, keepdims=True)
    return (xc * lax.rsqrt(var + LN_EPS) * g + b).astype(x.dtype)

def sink_softmax(logits, valid, sinks):
    s = sinks.astype(jnp.float32).reshape(N_KV_HEADS, GROUP)[:, :, None, None]
    logits = jnp.where(valid, logits, -jnp.inf)
    m = jnp.maximum(jnp.max(logits, axis=-1, keepdims=True), s)
    e = jnp.where(valid, jnp.exp(logits - m), 0.0)
    return e / (jnp.sum(e, axis=-1, keepdims=True) + jnp.exp(s - m))

def swa_prompt(q, k, v, sinks):
    n, s = q.shape[:2]
    nb = s // ATTN_BLOCK
    qb = q.reshape(n, nb, ATTN_BLOCK, N_KV_HEADS, GROUP, HEAD_DIM)
    kb = k.reshape(n, nb, ATTN_BLOCK, N_KV_HEADS, HEAD_DIM)
    vb = v.reshape(n, nb, ATTN_BLOCK, N_KV_HEADS, HEAD_DIM)

    def with_prev(t):
        prev = jnp.concatenate([jnp.zeros_like(t[:, :1]), t[:, :-1]], axis=1)
        return jnp.concatenate([prev, t], axis=2)

    kk, vv = with_prev(kb), with_prev(vb)
    logits = jnp.einsum('nbqkgd,nbskd->nbkgqs', qb, kk,
                        preferred_element_type=jnp.float32) * (HEAD_DIM ** -0.5)
    qpos = jnp.arange(ATTN_BLOCK)[:, None] + ATTN_BLOCK
    kpos = jnp.arange(2 * ATTN_BLOCK)[None, :]
    rel = qpos - kpos
    band = (rel >= 0) & (rel < WINDOW)
    real = (jnp.arange(nb)[:, None] > 0) | (kpos >= ATTN_BLOCK)
    valid = (band[None] & real[:, None, :])[None, :, None, None]
    p = sink_softmax(logits, valid, sinks).astype(v.dtype)
    out = jnp.einsum('nbkgqs,nbskd->nbqkgd', p, vv).reshape(n, s, Q_W)
    wc = min(WINDOW, s)
    return out, k[:, s - wc:], v[:, s - wc:]

def swa_sample(q, k, v, sinks, cache_k, cache_v):
    n, s = q.shape[:2]
    wc = cache_k.shape[1]
    kk = jnp.concatenate([cache_k, k], axis=1)
    vv = jnp.concatenate([cache_v, v], axis=1)
    qg = q.reshape(n, s, N_KV_HEADS, GROUP, HEAD_DIM)
    logits = jnp.einsum('nqkgd,nskd->nkgqs', qg, kk,
                        preferred_element_type=jnp.float32) * (HEAD_DIM ** -0.5)
    rel = jnp.arange(s)[:, None] - (jnp.arange(wc + s)[None, :] - wc)
    valid = (rel >= 0) & (rel < WINDOW)
    p = sink_softmax(logits, valid, sinks).astype(v.dtype)
    out = jnp.einsum('nkgqs,nskd->nqkgd', p, vv).reshape(n, s, Q_W)
    return out, kk[:, s:], vv[:, s:]

def short_conv(u, prev, w):
    s = u.shape[1]
    full = jnp.concatenate([prev, u], axis=1)
    y = full[:, 0:s] * w[0]
    for j in range(1, CONV_WIDTH):
        y = y + full[:, j:j + s] * w[j]
    return y, full[:, s:]

def swiglu(x, wg, wu, wd):
    return (jax.nn.silu(x @ wg) * (x @ wu)) @ wd

def route(x2, w_router, router_bias):
    t = x2.shape[0]
    scores = jax.nn.sigmoid((x2 @ w_router).astype(jnp.float32))
    biased = scores + router_bias.astype(jnp.float32)
    grp = biased.reshape(t, N_GROUPS, N_EXPERTS // N_GROUPS)
    grp_score = jnp.sum(lax.top_k(grp, 2)[0], axis=-1)
    _, gidx = lax.top_k(grp_score, TOPK_GROUPS)
    gmask = jnp.sum(jax.nn.one_hot(gidx, N_GROUPS), axis=1) > 0
    emask = jnp.repeat(gmask, N_EXPERTS // N_GROUPS, axis=1)
    _, eidx = lax.top_k(jnp.where(emask, biased, -jnp.inf), TOP_K)
    gw = jnp.take_along_axis(scores, eidx, axis=-1)
    gw = gw / jnp.sum(gw, axis=-1, keepdims=True) * ROUTED_SCALE
    return eidx, gw

def routed_experts(x2, eidx, gw, w_e_gate, w_e_up, w_e_down):
    t, d = x2.shape
    a = t * TOP_K
    flat_e = eidx.reshape(-1)
    flat_tok = jnp.arange(a, dtype=jnp.int32) // TOP_K
    flat_w = gw.reshape(-1)
    order = jnp.argsort(flat_e)
    sorted_e = flat_e[order]
    counts = jnp.bincount(flat_e, length=N_EXPERTS)
    starts = jnp.cumsum(counts) - counts
    padded = (counts + MOE_BLOCK - 1) // MOE_BLOCK * MOE_BLOCK
    pad_end = jnp.cumsum(padded)
    pad_start = pad_end - padded
    dest = pad_start[sorted_e] + jnp.arange(a) - starts[sorted_e]
    n_blocks = -(-(a + N_EXPERTS * (MOE_BLOCK - 1)) // MOE_BLOCK)
    rows = n_blocks * MOE_BLOCK
    row_tok = jnp.full((rows,), t, jnp.int32).at[dest].set(flat_tok[order])
    row_w = jnp.zeros((rows,), jnp.float32).at[dest].set(flat_w[order])
    block_e = jnp.minimum(
        jnp.searchsorted(pad_end, jnp.arange(n_blocks) * MOE_BLOCK, side='right'),
        N_EXPERTS - 1)
    x_pad = jnp.concatenate([x2, jnp.zeros((1, d), x2.dtype)], axis=0)
    xb = x_pad[row_tok].reshape(n_blocks, MOE_BLOCK, d)

    def expert_block(args):
        xblk, e = args
        return swiglu(xblk, w_e_gate[e], w_e_up[e], w_e_down[e])

    yb = lax.map(expert_block, (xb, block_e)).reshape(rows, d)
    y = jax.ops.segment_sum(yb * row_w[:, None].astype(yb.dtype), row_tok, num_segments=t + 1)
    return y[:t].astype(x2.dtype)

def decoder_layer(h, p, attn_fn, conv_prev, lw):
    n, s, _ = h.shape
    z = h @ lw['w_in']
    q, k, v, c_b, c_c, c_h, g_a, g_c = jnp.split(z, IN_SPLITS, axis=-1)
    q = q.reshape(n, s, N_HEADS, HEAD_DIM)
    k = k.reshape(n, s, N_KV_HEADS, HEAD_DIM)
    v = v.reshape(n, s, N_KV_HEADS, HEAD_DIM)
    attn, new_k, new_v = attn_fn(q, k, v, lw['attn_sinks'])
    conv, new_conv = short_conv(c_c * c_h, conv_prev, lw['conv_w'])
    conv = c_b * conv
    merged = (jax.nn.sigmoid(g_a) * (attn @ lw['w_attn_out'])
              + jax.nn.sigmoid(g_c) * (conv @ lw['w_conv_out']))
    mix = merged @ lw['w_o']
    h = layer_norm(DN_ALPHA * h + mix, lw['ln1_g'], lw['ln1_b'])
    x2 = h.reshape(n * s, D_MODEL)
    eidx, gw = route(x2, lw['w_router'], lw['router_bias'])
    ffn = (swiglu(x2, lw['w_s_gate'], lw['w_s_up'], lw['w_s_down'])
           + routed_experts(x2, eidx, gw, lw['w_e_gate'], lw['w_e_up'], lw['w_e_down']))
    ple = jax.nn.sigmoid(h @ lw['w_ple_gate']) * (p @ lw['w_ple_proj'])
    h = layer_norm(DN_ALPHA * h + ffn.reshape(n, s, D_MODEL) + ple, lw['ln2_g'], lw['ln2_b'])
    return h, new_k, new_v, new_conv

def setup_inputs(seed: int = 0) -> dict:
    key = jax.random.key(seed)
    ks = jax.random.split(key, 32)

    def nrm(k, shape, scale):
        return jax.random.normal(k, shape, jnp.float32) * scale

    wc = min(WINDOW, PAST_LEN)
    return {
        'x_prompt': nrm(ks[0], (BATCH, SEQ, D_MODEL), 1.0),
        'x_sample': nrm(ks[1], (DEC_BATCH, DEC_SEQ, D_MODEL), 1.0),
        'p_prompt': nrm(ks[2], (DEPTH, BATCH, SEQ, PLE_DIM), 1.0),
        'p_sample': nrm(ks[3], (DEPTH, DEC_BATCH, DEC_SEQ, PLE_DIM), 1.0),
        'state_win_k': nrm(ks[4], (DEPTH, DEC_BATCH, wc, N_KV_HEADS, HEAD_DIM), 1.0),
        'state_win_v': nrm(ks[5], (DEPTH, DEC_BATCH, wc, N_KV_HEADS, HEAD_DIM), 1.0),
        'state_conv': nrm(ks[6], (DEPTH, DEC_BATCH, CONV_WIDTH - 1, CONV_DIM), 1.0),
        'w_in': nrm(ks[7], (DEPTH, D_MODEL, IN_COLS), D_MODEL ** -0.5),
        'attn_sinks': nrm(ks[8], (DEPTH, N_HEADS), 0.5),
        'conv_w': nrm(ks[9], (DEPTH, CONV_WIDTH, CONV_DIM), CONV_WIDTH ** -0.5),
        'w_attn_out': nrm(ks[10], (DEPTH, Q_W, D_MODEL), Q_W ** -0.5),
        'w_conv_out': nrm(ks[11], (DEPTH, CONV_DIM, D_MODEL), CONV_DIM ** -0.5),
        'w_o': nrm(ks[12], (DEPTH, D_MODEL, D_MODEL), D_MODEL ** -0.5 * DN_BETA),
        'ln1_g': 1.0 + nrm(ks[13], (DEPTH, D_MODEL), 0.01),
        'ln1_b': nrm(ks[14], (DEPTH, D_MODEL), 0.01),
        'w_router': nrm(ks[15], (DEPTH, D_MODEL, N_EXPERTS), D_MODEL ** -0.5),
        'router_bias': nrm(ks[16], (DEPTH, N_EXPERTS), 0.01),
        'w_e_gate': nrm(ks[17], (DEPTH, N_EXPERTS, D_MODEL, EXPERT_FF), D_MODEL ** -0.5),
        'w_e_up': nrm(ks[18], (DEPTH, N_EXPERTS, D_MODEL, EXPERT_FF), D_MODEL ** -0.5),
        'w_e_down': nrm(ks[19], (DEPTH, N_EXPERTS, EXPERT_FF, D_MODEL), EXPERT_FF ** -0.5 * DN_BETA),
        'w_s_gate': nrm(ks[20], (DEPTH, D_MODEL, SHARED_FF), D_MODEL ** -0.5),
        'w_s_up': nrm(ks[21], (DEPTH, D_MODEL, SHARED_FF), D_MODEL ** -0.5),
        'w_s_down': nrm(ks[22], (DEPTH, SHARED_FF, D_MODEL), SHARED_FF ** -0.5 * DN_BETA),
        'w_ple_gate': nrm(ks[23], (DEPTH, D_MODEL, D_MODEL), D_MODEL ** -0.5),
        'w_ple_proj': nrm(ks[24], (DEPTH, PLE_DIM, D_MODEL), PLE_DIM ** -0.5),
        'ln2_g': 1.0 + nrm(ks[25], (DEPTH, D_MODEL), 0.01),
        'ln2_b': nrm(ks[26], (DEPTH, D_MODEL), 0.01),
    }

def reference(x_prompt, x_sample, p_prompt, p_sample, state_win_k, state_win_v, state_conv,
              w_in, attn_sinks, conv_w, w_attn_out, w_conv_out, w_o, ln1_g, ln1_b,
              w_router, router_bias, w_e_gate, w_e_up, w_e_down, w_s_gate, w_s_up, w_s_down,
              w_ple_gate, w_ple_proj, ln2_g, ln2_b):
    hp, hs = x_prompt, x_sample
    kp_l, vp_l, cp_l, ks_l, vs_l, cs_l = [], [], [], [], [], []
    for i in range(DEPTH):
        lw = {
            'w_in': w_in[i], 'attn_sinks': attn_sinks[i], 'conv_w': conv_w[i],
            'w_attn_out': w_attn_out[i], 'w_conv_out': w_conv_out[i], 'w_o': w_o[i],
            'ln1_g': ln1_g[i], 'ln1_b': ln1_b[i], 'w_router': w_router[i],
            'router_bias': router_bias[i], 'w_e_gate': w_e_gate[i], 'w_e_up': w_e_up[i],
            'w_e_down': w_e_down[i], 'w_s_gate': w_s_gate[i], 'w_s_up': w_s_up[i],
            'w_s_down': w_s_down[i], 'w_ple_gate': w_ple_gate[i], 'w_ple_proj': w_ple_proj[i],
            'ln2_g': ln2_g[i], 'ln2_b': ln2_b[i],
        }
        conv0 = jnp.zeros((hp.shape[0], CONV_WIDTH - 1, CONV_DIM), hp.dtype)
        hp, kp, vp, cp = decoder_layer(hp, p_prompt[i], swa_prompt, conv0, lw)
        attn_s = functools.partial(swa_sample, cache_k=state_win_k[i], cache_v=state_win_v[i])
        hs, ks_, vs_, cs_ = decoder_layer(hs, p_sample[i], attn_s, state_conv[i], lw)
        kp_l.append(kp); vp_l.append(vp); cp_l.append(cp)
        ks_l.append(ks_); vs_l.append(vs_); cs_l.append(cs_)
    return (hp, hs, jnp.stack(kp_l), jnp.stack(vp_l), jnp.stack(cp_l),
            jnp.stack(ks_l), jnp.stack(vs_l), jnp.stack(cs_l))


_drawn_inputs = setup_inputs


def setup_inputs(seed=0):
    import zlib

    import numpy as np

    out = dict(_drawn_inputs(seed))
    spreads = {}
    factors = {'attn_sinks': 6.903, 'ln2_g': 5.598, 'ln2_b': 5.604}
    for name, (base, spread) in spreads.items():
        noise = np.random.default_rng([zlib.crc32(name.encode()), seed]).standard_normal(out[name].shape)
        drawn = base * np.exp(spread * noise) if base else spread * noise
        out[name] = jnp.asarray(drawn.astype(out[name].dtype))
    for name, factor in factors.items():
        out[name] = (out[name] * factor).astype(out[name].dtype)
    return out
```

```python
from contextlib import ExitStack

import numpy as np

import concourse.bass as bass
from concourse import mybir

F32 = mybir.dt.float32
F32R = mybir.dt.float32r
BF16 = mybir.dt.bfloat16
I32 = mybir.dt.int32
U32 = mybir.dt.uint32
ALU = mybir.AluOpType
ACT = mybir.ActivationFunctionType
AX = mybir.AxisListType

P = 128
D = 1024
KC = D // P
SEQ, NB_S, S_S = 512, 8, 8
NS = NB_S * S_S
T = SEQ + NS
HALF = T // 2
NT = (T + P - 1) // P
N_HEADS, N_KV, HD = 16, 2, 64
NPAIR_H = N_HEADS // N_KV
WIN = 128
NBLK = SEQ // WIN
KEYS_S = WIN + NS
Q_W, KV_W = N_HEADS * HD, N_KV * HD
PLE = 256
NE, TOPK, NGRP, TOPG = 64, 6, 8, 4
FF = 256
ROUTED_SCALE = 2.5
ALPHA = 2 ** 0.25
LN_EPS = 1e-5
NPE = NE // 2
SLOT = 64
MAXPASS = NPE + T * TOPK // SLOT + 4
BIG = 1e30
PAD_V = 5000.0

COL_K, COL_CB = Q_W, Q_W + 2 * KV_W
COL_CC, COL_CH = COL_CB + D, COL_CB + 2 * D
COL_GA, COL_GC = COL_CB + 3 * D, COL_CB + 4 * D

GW = 256
G_Q, G_GA, G_AO, G_C, G_GC, G_WO, G_PP, G_SG, G_SU, G_PG, G_SD = 1, 5, 9, 13, 25, 33, 37, 38, 39, 40, 44
N_GROUPS_W = 45


def pack_constants():
    neg = -BIG
    ident = np.eye(P, dtype=np.float32)
    q, k = np.arange(P)[:, None] + P, np.arange(2 * P)[None]
    band = (q - k >= 0) & (q - k < WIN)
    first = band & (k >= P)
    mask_p = np.where(np.stack([first, band], 1), 0.0, neg).astype(np.float32).reshape(P, -1)
    row = np.arange(P)
    s_of = row % S_S
    mask_s = np.full((P, NB_S, KEYS_S), neg, np.float32)
    for b in range(NB_S):
        j = np.arange(WIN)[None]
        mask_s[:, b, :WIN] = np.where(j > s_of[:, None], 0.0, neg)
        for s in range(S_S):
            mask_s[:, b, WIN + b * S_S + s] = np.where(s <= s_of, 0.0, neg)
    sel16 = (np.arange(16)[None] == (row[:, None] // 64) * 8 + (row[:, None] % 64) // 8)
    first_part = np.concatenate([ident, mask_p, mask_s.reshape(P, -1), sel16.astype(np.float32)], 1)
    tri = (row[:, None] < row[None, :]).astype(np.float32)
    iota64 = np.tile(np.arange(64, dtype=np.float32), (P, 1))
    iota128 = np.tile(np.arange(128, dtype=np.float32), (P, 1))
    iota_pass = np.tile(np.arange(MAXPASS, dtype=np.float32), (P, 1))
    side = np.tile((np.arange(NE) % 2 * SLOT).astype(np.float32), (P, 1))
    tok = np.arange(NT)[None, :, None] * P + row[:, None, None]
    val = np.where(tok < T, tok * 8 + np.arange(TOPK)[None, None] + 8, 0).astype(np.float32).reshape(P, -1)
    ones = np.ones((P, P), np.float32)
    second_part = np.concatenate([tri, ones, iota64, iota128, iota_pass, side, val], 1)
    return np.ascontiguousarray(first_part, np.float32), np.ascontiguousarray(second_part, np.float32)


C1_W = P + 2 * 2 * P + NB_S * KEYS_S + 16
C2_W = P + P + 64 + P + MAXPASS + 64 + NT * TOPK


class Step:

    def __init__(self, base, it=0, per=0):
        self.base = base
        self.v = base + it * per
        self.par = base % 2
        self.half = base // 2 + it * (per // 2)


def decoder_step(nc, x_prompt, x_sample, p_prompt, p_sample, win_k, win_v, conv_state, w_in, sinks,
                 conv_w, w_ao, w_co, w_o, ln1_g, ln1_b, w_router, router_bias, w_eg, w_eu, w_ed,
                 w_sg, w_su, w_sd, w_pg, w_pp, ln2_g, ln2_b, const1, const2,
                 y_prompt, y_sample, nk_p, nv_p, nconv_p, nk_s, nv_s, nconv_s):
    ctx = ExitStack()
    with ctx:
        base0 = (nc.sbuf_base + 31) // 32 * 32
        def at(name, shape, dt, off):
            return nc.alloc_sbuf_tensor_at(name, shape, dt, offset=base0 + off)

        def sem(name):
            return ctx.enter_context(nc.semaphore(name))

        o_a, o_c, o_ring = 0, 36864, 73728
        o_b, o_d, o_e, o_f = 122880, 141312, 159744, 167936
        h_hi = at("h_hi", [P, KC, T], F32R, o_a)
        h_lo = at("h_lo", [P, KC, T], F32R, o_a + 18432)
        x_tok = at("x_tok", [P, NT, D], F32, o_c)
        mix_hi = at("mix_hi", [P, KC, T], F32R, o_c)
        mix_lo = at("mix_lo", [P, KC, T], F32R, o_c + 18432)
        w_raw = at("w_raw", [P, 2, KC * GW], F32, o_ring)
        w_hi = at("w_hi", [P, 2, KC * GW], F32R, o_ring + 16384)
        w_lo = at("w_lo", [P, 2, KC * GW], F32R, o_ring + 32768)
        q_t = at("q_t", [P, NPAIR_H, T], F32, o_b)
        merged_hi = at("merged_hi", [P, KC, T], F32R, o_b)
        convraw = at("convraw", [16, D], F32, o_d)
        cwraw = at("cwraw", [24, P], F32, o_d + 4096)
        gate_a = at("gate_a", [P, KC, T], F32, o_d)
        merged_lo = at("merged_lo", [P, KC, T], F32R, o_d)
        k_t = at("k_t", [P, WIN + T], F32, o_e)
        v_tok = at("v_tok", [P, 1 + NT, P], F32, o_e + 2816)
        v_t = at("v_t", [P, T], F32, o_e + 5888)
        k_tok = at("k_tok", [P, 2, P], F32, o_e + 5888)
        mask_p = at("mask_p", [P, 2, 2 * P], F32, o_f)
        mask_s = at("mask_s", [P, NB_S, KEYS_S], F32, o_f + 2048)
        cache_k = at("cache_k", [P, NB_S, P], F32, o_f + 8192)
        s_s = at("s_s", [P, NB_S, KEYS_S], F32, o_f + 8192)
        cache_v = at("cache_v", [P, NB_S, P], F32, o_f + 14336)
        o_h = o_f + 18432
        q_blk = [at(f"q_blk{i}", [P, NPAIR_H, P], F32, o_h + 4096 * i) for i in range(2)]
        q_smp = at("q_smp", [P, NB_S, HD], F32, o_h)
        cache_kt = at("cache_kt", [P, NB_S, P], F32, o_h + 4096)
        v_blk = [at(f"v_blk{i}", [P, 2, P], F32, o_h + 8192 + 1024 * i) for i in range(2)]
        k_blk = [at(f"k_blk{i}", [P, 2 * P], F32, o_f + 2048 + 1024 * i) for i in range(2)]
        mask_0 = at("mask_0", [P, 2 * P], F32, o_f + 4096)
        s_p = [at(f"s_p{i}", [P, 2, 2 * P], F32, o_h + 10240 + 2048 * i) for i in range(2)]
        p_t = at("p_t", [P, 2, 2, 4, P], F32, o_h + 14336)
        ps_t = at("ps_t", [P, NB_S, P], F32, o_h + 14336)
        psn_t = at("psn_t", [NS, NB_S, P], F32, o_h + 18432)
        cc_t = at("cc_t", [P, 2, T], F32, o_f)
        u_ext = [at(f"u_ext{i}", [P, 594], F32, o_f + 4608 + 2400 * i) for i in range(2)]
        y_cv = [at(f"y_cv{i}", [P, 594], F32, o_f + 9408 + 2400 * i) for i in range(2)]
        prod = [at(f"prod{i}", [P, T], F32, o_f + 14208 + 2304 * i) for i in range(2)]
        sig_c = at("sig_c", [P, 2, T], F32, o_f)
        cn_tok = at("cn_tok", [18, D], F32, o_h + 4096)

        small = [o_h + 22528]

        def sm(name, shape, dt):
            size = {F32: 4, I32: 4, U32: 4, F32R: 4, BF16: 2}[dt] * int(np.prod(shape[1:]))
            t = at(name, shape, dt, small[0])
            small[0] += (size + 31) // 32 * 32
            return t

        ident = sm("ident", [P, P], F32)
        sink16 = sm("sink16", [P, 16], F32)
        nsink16 = sm("nsink16", [P, 16], F32)
        sel16 = sm("sel16", [P, 16], F32)
        sink_s = sm("sink_s", [P, 1], F32)
        nsink_s = sm("nsink_s", [P, 1], F32)
        cw = sm("cw", [P, 24], F32)
        o_stats = small[0]
        cst = sm("cst", [P, KC, 16], F32)
        cnew = sm("cnew", [P, KC, 18], F32)
        mx = sm("mx", [P, 2, 2], F32)
        nm = sm("nm", [P, 2, 2], F32)
        ds = sm("ds", [P, 2, 2], F32)
        es = sm("es", [P, 2, 2], F32)
        sm_p = sm("sm_p", [P, 2, 2], F32)
        rc = sm("rc", [P, 2, 2], F32)
        mx_s = sm("mx_s", [P, NB_S], F32)
        nm_s = sm("nm_s", [P, NB_S], F32)
        es_s = sm("es_s", [P, NB_S], F32)
        sum_s = sm("sum_s", [P, NB_S], F32)
        eps = sm("eps", [P, 1], F32)
        mv = sm("mv", [P, NT, 2], F32)
        rstd = sm("rstd", [P, NT], F32)
        wj = sm("wj", [P, NT * TOPK], F32)
        tabx = sm("tabx", [P, MAXPASS], U32)
        taby = sm("taby", [P, MAXPASS], U32)
        n_pass = sm("n_pass", [1, NPE], I32)
        cum_pass = sm("cum_pass", [1, NPE], I32)
        half_all = sm("half_all", [1, 1], I32)
        stats = at("stats", [P, NT, 4, 6], F32, o_stats)

        proj = ctx.enter_context(nc.psum_tensor("proj", [P, 4, 512], F32))
        att = ctx.enter_context(nc.psum_tensor("att", [P, 4, 512], F32))

        def slot(i):
            return proj[:, 2 * i:2 * i + 2, 0:HALF]

        ld_x, ld_c1, ld_sink, ld_conv, ld_ck, ld_cv = (sem(n) for n in (
            "ld_x", "ld_c1", "ld_sink", "ld_conv", "ld_ck", "ld_cv"))
        w_dma = [sem(f"w_dma{i}") for i in range(2)]
        hi_done = sem("hi_done")
        w_ready = sem("w_ready")
        mm_ready = [sem(f"mm_ready{i}") for i in range(2)]
        mm_free = [sem(f"mm_free{i}") for i in range(2)]
        zeroed = sem("zeroed")
        tr_x, x_hi, x_lo = sem("tr_x"), sem("x_hi"), sem("x_lo")
        tr_conv, conv_ready = sem("tr_conv"), sem("conv_ready")
        tr_kv, kv_tok_ready, ckt_ready = sem("tr_kv"), sem("kv_tok_ready"), sem("ckt_ready")
        qs_ready = sem("qs_ready")
        sl_ready, sl_read, s_sub, s_exp, s_prob = (sem(n) for n in (
            "sl_ready", "sl_read", "s_sub", "s_exp", "s_prob"))
        s_tr, s_trc, s_pv, s_oh, s_ol = (sem(n) for n in ("s_tr", "s_trc", "s_pv", "s_oh", "s_ol"))
        blk_ready = sem("blk_ready")
        lg_ready, lg_read = sem("lg_ready"), sem("lg_read")
        nm_ready, e_ready, p_ready = sem("nm_ready"), sem("e_ready"), sem("p_ready")
        pt_ready, pt_read = sem("pt_ready"), sem("pt_read")
        pv_ready, o_hi, o_lo = sem("pv_ready"), sem("o_hi"), sem("o_lo")
        sga = sem("sga")
        u_done, pr_ready, cv_hi, cv_lo = sem("u_done"), sem("pr_ready"), sem("cv_hi"), sem("cv_lo")
        mg_ready, mg_hi, mg_lo = sem("mg_ready"), sem("mg_hi"), sem("mg_lo")
        cn_tr, cn_out = sem("cn_tr"), sem("cn_out")
        st_out, win_out = sem("st_out"), sem("win_out")

        res = at("res", [P, NT, D], F32, o_a)
        p_tok = at("p_tok", [P, NT, PLE], F32, o_a + 20480)
        rw_hi = at("rw_hi", [P, KC, NE], F32R, o_a + 20480)
        rw_lo = at("rw_lo", [P, KC, NE], F32R, o_a + 22528)
        pt_hi = at("pt_hi", [P, 2, T], F32R, o_a + 25600)
        pt_lo = at("pt_lo", [P, 2, T], F32R, o_a + 30208)
        hs_f = at("hs_f", [P, 2, T], F32, o_a + 25600)
        rw_raw = at("rw_raw", [P, KC, NE], F32, o_a + 34816)
        xt_hi = at("xt_hi", [P, KC, T], F32R, o_c)
        xt_lo = at("xt_lo", [P, KC, T], F32R, o_c + 18432)
        ppo = at("ppo", [P, NT, D], F32, o_b)
        sgo = at("sgo", [P, NT, D], F32, o_b + 20480)
        cc2 = at("cc2", [P, C2_W], F32, o_b + 40960)
        g1b1 = at("g1b1", [P, 2, D], F32, 172032)
        hs_hi = at("hs_hi", [P, 2, T], F32R, 172032)
        hs_lo = at("hs_lo", [P, 2, T], F32R, 176640)
        tri, ones = cc2[:, 0:P], cc2[:, P:2 * P]
        iota64, iota128 = cc2[:, 2 * P:2 * P + 64], cc2[:, 2 * P + 64:3 * P + 64]
        iota_pass = cc2[:, 3 * P + 64:3 * P + 64 + MAXPASS]
        side, val = cc2[:, 3 * P + 64 + MAXPASS:3 * P + 128 + MAXPASS], cc2[:, 3 * P + 128 + MAXPASS:C2_W]
        NTK = NT * TOPK
        hot = at("hot", [P, NTK, NE], F32, 181248)
        picked = at("picked", [P, NTK, NE], F32, 188928)
        tab_a = at("tab_a", [P, TOPK, P], F32, 196608)
        tab_b = at("tab_b", [P, TOPK, MAXPASS], F32, 199680)
        rt = [201856]
        rt_small = [o_a + 30208]

        def rsm(name, shape, dt, pool=rt):
            size = {F32: 4, I32: 4, U32: 4, BF16: 2}[dt] * int(np.prod(shape[1:]))
            t = at(name, shape, dt, pool[0])
            pool[0] += (size + 31) // 32 * 32
            return t

        scores = rsm("scores", [P, NT, NE], F32)
        biased = rsm("biased", [P, NT, NE], F32)
        slot_map = rsm("slot_map", [P, NT, NE], F32)
        rank_i = rsm("rank_i", [P, NT, NE], I32)
        col_map = rsm("col_map", [P, NT, NE], F32)
        rbias = at("rbias", [P, NE], F32, 208640)
        best8 = rsm("best8", [P, NT * NGRP, 8], F32, rt_small)
        ghot = rsm("ghot", [P, NT, TOPG, NGRP], F32, rt_small)
        sel = rsm("sel", [P, NT, NE], BF16, rt_small)
        gsum = rsm("gsum", [P, NT, NGRP], F32, rt_small)
        gbest = rsm("gbest", [P, NT, 8], F32, rt_small)
        gidx = rsm("gidx", [P, NT, 8], U32, rt_small)
        gidx_f = rsm("gidx_f", [P, NT, TOPG], F32, rt_small)
        gmask = rsm("gmask", [P, NT, NGRP], F32, rt_small)
        ebest = rsm("ebest", [P, NT, 8], F32, rt_small)
        eidx = rsm("eidx", [P, NT, 8], U32, rt_small)
        eidx_f = rsm("eidx_f", [P, NT, TOPK], F32, rt_small)
        xg = at("xg", [P, P, KC], F32, 172032)
        xt = at("xt", [P, KC, P], F32, 180224)
        ysb = [at(f"ysb{i}", [P, D], F32, 184320 + 4096 * i) for i in range(2)]
        sg = at("sg", [P, FF], F32, 192512)
        g_e = at("g_e", [P, FF], F32, 193536)
        h_e = at("h_e", [P, FF], F32, 194560)
        ht_e = at("ht_e", [P, 2, P], F32, 195584)
        w_exp = [at(f"w_exp{i}", [P, 2, 3 * KC * FF], F32, o) for i, o in enumerate((o_c, o_b))]
        y_buf = [at(f"y_buf{i}", [P, TOPK, D], F32, o) for i, o in enumerate((86016, o_b))]
        g2b2 = at("g2b2", [P, 2, D], F32, 110592)
        tri_b = rsm("tri_b", [P, P], BF16, rt_small)
        ones_b = rsm("ones_b", [P, P], BF16, rt_small)
        base64 = rsm("base64", [P, NPE], F32)
        nmax = rsm("nmax", [P, NPE], F32)
        npass_i = rsm("npass_i", [P, NPE], I32)
        npass_f = rsm("npass_f", [P, NPE], F32, rt_small)
        cums = [at(f"cums{i}", [P, NPE], F32, o_a + 30208 + 128 * i) for i in range(2)]
        assert rt[0] <= 208640 and rt_small[0] <= o_a + 34816, (rt[0], rt_small[0] - o_a)
        slot_j, col_j = (at(n, [P, NTK], F32, o_a + 34816 + 128 * i)
                                 for i, n in enumerate(("slot_j", "col_j")))
        ssum = at("ssum", [P, NT], F32, o_a + 34816 + 384)
        tab_f, tab_e = (at(n, [P, MAXPASS], F32, o_a + 34816 + 416 + 384 * i) for i, n in enumerate(("tab_f", "tab_e")))
        tab_i, tab_s = (at(n, [P, MAXPASS], I32, o_a + 34816 + 1184 + 384 * i) for i, n in enumerate(("tab_i", "tab_s")))
        gidx_col = [at(f"gidx_col{i}", [P, 1], U32, o_a + 34816 + 256 + 32 * i) for i in range(2)]
        sidx_col = [at(f"sidx_col{i}", [P, 1], U32, o_a + 34816 + 320 + 32 * i) for i in range(2)]

        x2_d = nc.dram_tensor("x2_rows", [T, D], F32)
        y_d = nc.dram_tensor("expert_rows", [T * TOPK, D], F32)

        def tile_bank(t):
            return proj[:, t, :] if t < 4 else att[:, 0, :]

        def pg_bank(t):
            return proj[:, 2 + t, :] if t < 2 else att[:, t - 2, :]

        ld_p, ld_res, ld_rt, ld_ln1, ld_ln2 = (sem(n) for n in ("ld_p", "ld_res", "ld_rt", "ld_ln1", "ld_ln2"))
        passed = [sem(f"passed{i}") for i in range(5)]
        wo_ready, wo_read = sem("wo_ready"), sem("wo_read")
        p_tr, p_hi, p_lo, pp_ready, pp_read = (sem(n) for n in ("p_tr", "p_hi", "p_lo", "pp_ready", "pp_read"))
        std_ready, var_ready, x2_ready, x2_out = (sem(n) for n in ("std_ready", "var_ready", "x2_ready", "x2_out"))
        x2_tr, x2_hi, x2_lo, rw_h, rw_ready = (sem(n) for n in ("x2_tr", "x2_hi", "x2_lo", "rw_h", "rw_ready"))
        rt_ready, sc_ready, sel_ready, rank_ready, rank_read = (sem(n) for n in (
            "rt_ready", "sc_ready", "sel_ready", "rank_ready", "rank_read"))
        su_ready, ss_ready, hs_ready, hs_hd, hs_ld = (sem(n) for n in ("su_ready", "ss_ready", "hs_ready", "hs_hd", "hs_ld"))
        pg_ready, pg_read = sem("pg_ready"), sem("pg_read")
        tb_ready, tb_used, routed, res_done = (sem(n) for n in ("tb_ready", "tb_used", "routed", "res_done"))
        sd_ready, sd_read = sem("sd_ready"), sem("sd_read")
        x_zero, gathered, idx_ready = sem("x_zero"), sem("gathered"), sem("idx_ready")
        scattered = [sem(f"scattered{i}") for i in range(2)]
        w_exp_in = [sem(f"w_exp_in{i}") for i in range(3)]
        xtr, xt_a, xt_d = sem("xtr"), sem("xt_a"), sem("xt_d")
        gu_ready, sg_ready, h_ready, htr, ht_ready = (sem(n) for n in ("gu_ready", "sg_ready", "h_ready", "htr", "ht_ready"))
        y_mm, y_a, y_dv = sem("y_mm"), sem("y_a"), sem("y_dv")
        ld_y = [sem(f"ld_y{i}") for i in range(2)]
        y_used, y_done, y_out = sem("y_used"), sem("y_done"), sem("y_out")

        block = ctx.enter_context(nc.Block())

        xp = x_prompt[0].rearrange("(t p) n -> p t n", p=P)
        xs = x_sample.rearrange("b s n -> (b s) n")
        QUADS = [(t, c) for t in range(NT) for c in range(2)]
        CHUNKS_AT = [2, 2, 2, 2, 1, 1, 2, 2, 1, 1]

        def ntok(t):
            return P if t < NT - 1 else NS

        def two(ap):
            return ap.rearrange("p (a n) -> p a n", a=2)

        def row(t, m):
            return t[:, bass.ds(m, 1), :].rearrange("p o n -> p (o n)")

        def halves(g):
            for i in range(2):
                raw, hi, lo = (t[:, g.par, :].rearrange("p (c x n) -> p c x n", c=KC, x=4) for t in (w_raw, w_hi, w_lo))
                yield raw[:, :, i:4:2, :], hi[:, :, 2 * i:2 * i + 2, :], lo[:, :, 2 * i:2 * i + 2, :]

        def split_hi(act, g, used=None, count=None):
            act.wait_ge(w_dma[g.par], (g.half + 1) * 32)
            if used is not None:
                act.wait_ge(used, count)
            elif g.base >= 2:
                act.wait_ge(mm_ready[1], g.v - 1)
            if G_Q <= g.base < G_GA:
                for raw, hi, _ in halves(g):
                    last = nc.scalar.activation(hi, raw, ACT.Copy)
                last.then_inc(hi_done, 1)
            else:
                nc.scalar.activation(w_hi[:, g.par, :], w_raw[:, g.par, :], ACT.Copy).then_inc(hi_done, 1)

        def split_lo(dve, g):
            dve.wait_ge(hi_done, g.v + 1)
            if G_Q <= g.base < G_GA:
                for raw, hi, lo in halves(g):
                    last = nc.vector.tensor_tensor(lo, raw, hi.bitcast(F32), ALU.subtract)
                last.then_inc(w_ready, 1)
            else:
                nc.vector.tensor_tensor(w_lo[:, g.par, :], w_raw[:, g.par, :], w_hi[:, g.par, :].bitcast(F32),
                                        ALU.subtract).then_inc(w_ready, 1)

        def past(e, i):
            e.sem_inc(passed[i], 1)

        def pass_counts(e, p, prev=None):
            return e.value_load(n_pass[0:1, bass.ds(p, 1)], min_val=1, max_val=T // SLOT)

        def half_passes(e):
            return e.value_load(half_all[0:1, 0:1], min_val=NPE // 2, max_val=MAXPASS // 2 - 1)

        @block.sync
        def _(sp):
            def load(g, w, c0):
                src = w[0].rearrange("(c p) n -> p c n", p=P)[:, :, bass.ds(c0, GW)]
                if g.base >= 2:
                    sp.wait_ge(w_ready, g.v - 1)
                    if not isinstance(g.v, int):
                        past(nc.sync, 4)
                sp.dma_start(w_raw[:, g.par, :].rearrange("p (c n) -> p c n", c=KC),
                             src).then_inc(w_dma[g.par], 32)

            load(Step(0), w_in, COL_K)
            wq = w_in[0][:, 0:Q_W].rearrange("(c p) (h n) -> p c h n", p=P, h=2)
            for j in range(4):
                g = Step(G_Q + j)
                if j:
                    sp.wait_ge(w_ready, g.v - 1)
                for e in range(2):
                    sp.dma_start(w_raw[:, g.par, :].rearrange("p (c h n) -> p c h n", c=KC, h=2)[:, :, e, :],
                                 wq[:, :, e, j * P:(j + 1) * P]).then_inc(w_dma[g.par], 16)
            with sp.Fori(0, 2) as it:
                for i in range(2):
                    load(Step(G_GA + i, it, 2), w_in, it * 2 * GW + COL_GA + i * GW)
            wao = w_ao[0].rearrange("(g m p) n -> g p m n", g=2, p=HD)
            with sp.Fori(0, 2) as it:
                for i in range(2):
                    g = Step(G_AO + i, it, 2)
                    sp.wait_ge(w_ready, g.v - 1)
                    past(nc.sync, 4)
                    for e in range(2):
                        sp.dma_start(w_raw[e * HD:(e + 1) * HD, g.par, :].rearrange("p (c n) -> p c n", c=KC),
                                     wao[e][:, :, bass.ds(it * 2 * GW + i * GW, GW)]).then_inc(w_dma[g.par], 16)
            with sp.Fori(0, 2) as it:
                for i in range(6):
                    c0 = (COL_CC, COL_CH, COL_CB)[i % 3] + i // 3 * GW
                    load(Step(G_C + i, it, 6), w_in, it * 2 * GW + c0)
            with sp.Fori(0, 4) as it:
                load(Step(G_GC, it, 2), w_in, it * GW + COL_GC)
                load(Step(G_GC + 1, it, 2), w_co, it * GW)
            load(Step(G_WO), w_o, 0)
            for j in range(1, 4):
                load(Step(G_WO + j), w_o, j * GW)
            wide = lambda w: w[0].rearrange("(c p) n -> p c n", p=P)
            def load_wide(g, w):
                sp.wait_ge(w_ready, g.v - 1)
                sp.dma_start(w_raw[:, g.par, :].rearrange("p (c n) -> p c n", c=2), wide(w)).then_inc(w_dma[g.par], 32)
            load_wide(Step(G_PP), w_pp)
            load(Step(G_SG), w_sg, 0)
            load(Step(G_SU), w_su, 0)
            for j in range(4):
                load(Step(G_PG + j), w_pg, j * GW)
            load_wide(Step(G_SD), w_sd)

            def load_part(p, i, n, first=False):
                k, e = ((0, 0), (1, 0), (0, 1), (1, 1), (2, 0), (2, 1))[n]
                w, c = ((w_eg, KC), (w_eu, KC), (w_ed, 2))[k]
                if not (first and n < 3):
                    sp.wait_ge(w_exp_in[n % 3], p * 32 + 16 * (n // 3))
                    if not isinstance(p, int):
                        past(nc.sync, 4)
                src = w[0][bass.ds(p * 2 + e, 1)].rearrange("o (r c) n -> r (o c n)", c=c)
                sp.dma_start(w_exp[i][:, e, k * KC * FF:(k + 1) * KC * FF], src).then_inc(w_exp_in[n % 3], 16)

            sp.wait_ge(pg_ready, 4 * NT + 1)
            sp.wait_ge(w_ready, N_GROUPS_W)
            for n in range(6):
                load_part(0, 0, n, first=True)
            sp.wait_ge(res_done, 1)
            sp.wait_ge(routed, 1)
            for n in range(6):
                load_part(1, 1, n)
            with sp.Fori(0, NPE // 2 - 1) as it:
                for i in range(2):
                    done = sp.value_load(cum_pass[0:1, bass.ds(it * 2 + i, 1)], min_val=1, max_val=MAXPASS - 1)
                    sp.wait_ge(gu_ready, done)
                    past(nc.sync, 4)
                    for n in range(4):
                        load_part(it * 2 + (2 + i), i, n)
                    sp.wait_ge(y_mm, done)
                    past(nc.sync, 4)
                    for n in range(4, 6):
                        load_part(it * 2 + (2 + i), i, n)
            k_half = half_passes(sp)
            for i in range(2):
                sp.wait_ge(scattered[i], k_half * 16 + 16)
                past(nc.sync, 4)
            for t in range(NT):
                w = ntok(t)
                if t >= 2:
                    sp.wait_ge(y_used, t - 1)
                sp.dma_start(y_buf[t % 2][0:w, :, :], y_d[t * P * TOPK:(t * P + w) * TOPK, :]
                             .rearrange("(p j) n -> p j n", j=TOPK)).then_inc(ld_y[t % 2], 16)
            for t in range(NT):
                w = ntok(t)
                sp.wait_ge(y_done, t + 1)
                dst = y_prompt[0, t * P:(t + 1) * P] if t < NT - 1 else y_sample.rearrange("b s n -> (b s) n")
                sp.dma_start(dst, res[0:w, t, :]).then_inc(y_out, 16)
            sp.wait_ge(y_out, NT * 16)

        @block.gpsimd
        def _(pool):
            nc.gpsimd.memset(k_t[:, 0:WIN], 0.0).then_inc(zeroed, 1)
            nc.gpsimd.memset(v_tok[:, 0, :], 0.0).then_inc(zeroed, 1)
            pool.wait_ge(kv_tok_ready, 1)
            pool.dma_start(nk_p[0, 0].rearrange("w g d -> w (g d)"), k_tok[:, 0, :]).then_inc(st_out, 16)
            pool.dma_start(nv_p[0, 0].rearrange("w g d -> w (g d)"), v_tok[:, NT - 1, :]).then_inc(st_out, 16)
            for b in range(NB_S):
                pool.dma_start(nk_s[0, b, WIN - S_S:WIN].rearrange("w g d -> w (g d)"),
                               k_tok[b * S_S:(b + 1) * S_S, 1, :]).then_inc(st_out, 16)
                pool.dma_start(nv_s[0, b, WIN - S_S:WIN].rearrange("w g d -> w (g d)"),
                               v_tok[b * S_S:(b + 1) * S_S, NT, :]).then_inc(st_out, 16)
            pool.wait_ge(cn_out, 1)
            pool.dma_start(nconv_p[0, 0], cn_tok[0:2, :]).then_inc(st_out, 16)
            pool.dma_start(nconv_s[0].rearrange("b j n -> (b j) n"), cn_tok[2:18, :]).then_inc(st_out, 16)
            for g in range(G_SG, N_GROUPS_W):
                pool.wait_ge(w_ready, g)
                pool.wait_ge(hi_done, g + 1)
                nc.gpsimd.tensor_tensor(w_lo[:, g % 2, :], w_raw[:, g % 2, :], w_hi[:, g % 2, :].bitcast(F32),
                                        ALU.subtract).then_inc(w_ready, 1)
            pool.wait_ge(sd_ready, 2 * NT)
            pool.dma_start(g2b2[:, 0, :], ln2_g[0].partition_broadcast(P)).then_inc(scattered[0], 16)
            pool.dma_start(g2b2[:, 1, :], ln2_b[0].partition_broadcast(P)).then_inc(scattered[1], 16)
            nc.gpsimd.memset(xg[:, :, :], 0.0).then_inc(x_zero, 1)
            pool.wait_ge(routed, 1)
            pool.wait_ge(x2_out, 16 * NT)
            pool.wait_ge(x_zero, 1)

            def gather(k, i, n):
                nc.gpsimd.tensor_copy(gidx_col[i][:, :], tabx[:, bass.ds(k, 1)]).then_inc(idx_ready, 1)
                pool.wait_ge(idx_ready, n)
                past(nc.gpsimd, 3)
                pool.indirect_dma_start(out=xg[:, :, :].rearrange("p q c -> p (q c)"), out_offset=None, in_=x2_d[:, :],
                                        in_offset=bass.IndirectOffsetOnAxis(ap=gidx_col[i][:, 0:1], axis=0),
                                        bounds_check=T - 1, oob_is_err=False).then_inc(gathered, 16)

            gather(0, 0, 1)
            pool.wait_ge(xtr, 1)
            gather(1, 1, 2)
            k_half = half_passes(pool)
            with pool.Fori(0, k_half) as it:
                for i in range(2):
                    k = it * 2 + i
                    pool.wait_ge(xtr, k + 2)
                    past(nc.gpsimd, 3)
                    gather(k + 2, i, k * 2 + 3)
                    pool.wait_ge(y_a, k + 2)
                    pool.wait_ge(y_dv, k + 2)
                    past(nc.gpsimd, 3)
                    nc.gpsimd.tensor_copy(sidx_col[i][:, :], taby[:, bass.ds(k, 1)]).then_inc(idx_ready, 1)
                    pool.wait_ge(idx_ready, k * 2 + 4)
                    past(nc.gpsimd, 3)
                    pool.indirect_dma_start(out=y_d[:, :], out_offset=bass.IndirectOffsetOnAxis(ap=sidx_col[i][:, 0:1], axis=0),
                                            in_=ysb[i][:, :], in_offset=None, bounds_check=T * TOPK - 1,
                                            oob_is_err=False).then_inc(scattered[i], 16)
            for i in range(2):
                pool.wait_ge(scattered[i], k_half * 16 + 16)
                past(nc.gpsimd, 3)
            pool.wait_ge(gathered, k_half * 32 + 32)
            past(nc.gpsimd, 3)
            pool.wait_ge(st_out, (2 + 2 * NB_S + 2) * 16)
            pool.wait_ge(win_out, 32)

        @block.scalar
        def _(act):
            act.dma_start(ident[:, :], const1[:, 0:P]).then_inc(ld_x, 16)
            act.dma_start(x_tok[:, 0:NT - 1, :], xp).then_inc(ld_x, 16)
            act.dma_start(x_tok[0:NS, NT - 1, :], xs).then_inc(ld_x, 16)
            act.dma_start(convraw[:, :], conv_state[0].rearrange("b j n -> (b j) n")).then_inc(ld_conv, 16)
            act.dma_start(cwraw[:, :], conv_w[0].rearrange("j (c p) -> (j c) p", p=P)).then_inc(ld_conv, 16)
            act.dma_start(mask_p[:, :, :].rearrange("p a b -> p (a b)"), const1[:, P:5 * P]).then_inc(ld_c1, 16)
            act.dma_start(mask_s[:, :, :].rearrange("p a b -> p (a b)"),
                          const1[:, 5 * P:5 * P + NB_S * KEYS_S]).then_inc(ld_c1, 16)
            act.dma_start(sel16[:, :], const1[:, C1_W - 16:C1_W]).then_inc(ld_sink, 16)
            act.dma_start(sink16[:, :], sinks[0].partition_broadcast(P)).then_inc(ld_sink, 16)
            act.dma_start(cache_k[:, :, :], win_k[0].rearrange("b w g d -> w b (g d)")).then_inc(ld_ck, 16)
            act.dma_start(cache_v[:, :, :], win_v[0].rearrange("b w g d -> w b (g d)")).then_inc(ld_cv, 16)
            act.dma_start(nk_s[0][:, 0:WIN - S_S].rearrange("b w g d -> b (w g d)"),
                          win_k[0][:, S_S:WIN].rearrange("b w g d -> b (w g d)")).then_inc(win_out, 16)
            act.dma_start(nv_s[0][:, 0:WIN - S_S].rearrange("b w g d -> b (w g d)"),
                          win_v[0][:, S_S:WIN].rearrange("b w g d -> b (w g d)")).then_inc(win_out, 16)
            for n, (t, c) in enumerate(QUADS):
                act.wait_ge(tr_x, n + 1)
                w = ntok(t)
                nc.scalar.activation(h_hi[:, 4 * c:4 * c + 4, t * P:t * P + w],
                                     att[:, n % 4, :].rearrange("p (c n) -> p c n", c=4)[:, :, 0:w],
                                     ACT.Copy).then_inc(x_hi, 1)
            split_hi(act, Step(0))
            split_hi(act, Step(1))
            act.wait_ge(mm_ready[0], 1)
            nc.scalar.activation(two(k_t[:, WIN:]), slot(0), ACT.Copy).then_inc(mm_free[0], 1)
            for j in range(4):
                split_hi(act, Step(G_Q + 1 + j))
                act.wait_ge(mm_ready[0], j + 2)
                nc.scalar.activation(two(q_t[:, 2 * j, :]), slot(0), ACT.Copy, scale=HD ** -0.5).then_inc(mm_free[0], 1)
                if j == 0:
                    act.wait_ge(tr_kv, 1)
                    nc.scalar.activation(cache_kt[:, :, :].rearrange("p (a b) n -> p a (b n)", a=2), att[:, 2:4, :],
                                         ACT.Copy).then_inc(ckt_ready, 1)
            act.wait_ge(s_sub, 1)
            nc.scalar.activation(s_s[:, :, :], s_s[:, :, :], ACT.Exp)
            nc.scalar.activation(es_s[:, :], nm_s[:, :], ACT.Exp, bias=sink_s[:, :]).then_inc(s_exp, 1)

            with act.Fori(0, 2) as it:
                for h in range(2):
                    u0, b0, blk = it * 16 + h * 8, it * 4 + h * 2, it * 2 + h
                    for s in range(10):
                        if s < 8:
                            r = s % 2
                            act.wait_ge(nm_ready, u0 + s + 1)
                            for e in range(2):
                                nc.scalar.activation(s_p[r][:, e, :], s_p[r][:, e, :], ACT.Exp,
                                                     bias=nm[:, r, e:e + 1], accum_out=sm_p[:, r, e:e + 1])
                            nc.scalar.activation(es[:, r, :], ds[:, r, :], ACT.Exp).then_inc(e_ready, 1)
                        if s >= 2:
                            m = s - 2
                            if m % 4 == 0:
                                act.wait_ge(pv_ready, b0 + m // 4 + 1)
                            act.wait_ge(pt_ready, u0 + m + 3)
                            nc.scalar.activation(p_t[:, :, :, m % 4, :],
                                                 att[:, 2, :].rearrange("p (g c q) -> p c g q", g=2, c=2),
                                                 ACT.Copy).then_inc(pt_read, 1)
                        if s == 4:
                            split_hi(act, Step(G_GA + h + 1, it, 2))
                        if s == 7 or s == 9:
                            mb = (s - 7) // 2
                            act.wait_ge(pv_ready, b0 + mb + 2)
                            nc.scalar.activation(mix_hi[:, 4 * mb:4 * mb + 4, bass.ds(blk * P, P)],
                                                 att[:, 3, :].rearrange("p (m q) -> p m q", m=4),
                                                 ACT.Copy).then_inc(o_hi, 1)
                    act.wait_ge(mm_ready[1], it * 2 + h + G_GA + 1)
                    nc.scalar.activation(two(row(gate_a, it * 4 + 2 * h + 1)), slot(1), ACT.Copy).then_inc(mm_free[1], 1)
            act.wait_ge(s_tr, 1)
            nc.scalar.activation(ps_t[:, :, :].rearrange("p (a b) n -> p a (b n)", a=2), att[:, 0:2, :],
                                 ACT.Copy).then_inc(s_trc, 1)
            act.wait_ge(s_pv, 1)
            nc.scalar.activation(mix_hi[:, :, SEQ:T].rearrange("p m (b s) -> p b m s", b=NB_S),
                                 att[:, 0, :].rearrange("p (b m s) -> p b m s", b=NB_S, m=8),
                                 ACT.Copy).then_inc(s_oh, 1)
            with act.Fori(0, 2) as it:
                for h in range(2):
                    act.wait_ge(mm_free[0], it * 2 + h + G_GA + 1)
                    act.wait_ge(mm_free[1], it * 2 + h + G_GA + 1)
                    nc.scalar.activation(gate_a[:, bass.ds(it * 4 + 2 * h, 2), :],
                                         gate_a[:, bass.ds(it * 4 + 2 * h, 2), :], ACT.Sigmoid).then_inc(sga, 1)
                    split_hi(act, Step(G_AO + h + 1, it, 2))
            with act.Fori(0, 2) as it:
                for jj in range(2):
                    for k in range(3):
                        gb = G_C + 3 * jj + k
                        split_hi(act, Step(gb + 1, it, 6))
                        for i in range(2):
                            if k == 0:
                                act.wait_ge(mm_ready[i], it * 6 + gb + 1)
                                act.wait_ge(u_done, it * 4 + 2 * jj + 1)
                                nc.scalar.activation(two(cc_t[:, i, :]), slot(i), ACT.Copy).then_inc(mm_free[i], 1)
                            if k == 2:
                                act.wait_ge(pr_ready, it * 4 + 2 * jj + i + 1)
                                act.wait_ge(mm_ready[1], G_AO + 4)
                                nc.scalar.activation(row(mix_hi, it * 4 + 2 * jj + i), prod[i][:, :],
                                                     ACT.Copy).then_inc(cv_hi, 1)
            act.wait_ge(cn_tr, 1)
            nc.scalar.activation(cn_tok[:, :].rearrange("p (a n) -> p a n", a=2), att[0:18, 0:2, :],
                                 ACT.Copy).then_inc(cn_out, 1)
            with act.Fori(0, 4) as it:
                split_hi(act, Step(G_GC + 1, it, 2))
                for i in range(2):
                    act.wait_ge(mm_ready[i], it * 2 + G_GC + 1)
                    act.wait_ge(mg_ready, it * 2 + 1)
                    nc.scalar.activation(two(sig_c[:, i, :]), slot(i), ACT.Sigmoid).then_inc(mm_free[i], 1)
                split_hi(act, Step(G_GC + 2, it, 2))
                for i in range(2):
                    act.wait_ge(mg_ready, it * 2 + 2 + i)
                    nc.scalar.activation(row(merged_hi, it * 2 + i), prod[i][:, :], ACT.Copy).then_inc(mg_hi, 1)
            act.wait_ge(mm_ready[1], G_WO)
            act.wait_ge(mm_ready[0], G_WO)
            act.wait_ge(st_out, (2 + 2 * NB_S + 2) * 16)
            act.dma_start(res[:, 0:NT - 1, :], xp).then_inc(ld_res, 16)
            act.dma_start(res[0:NS, NT - 1, :], xs).then_inc(ld_res, 16)
            act.dma_start(p_tok[:, 0:NT - 1, :], p_prompt[0, 0].rearrange("(t p) n -> p t n", p=P)).then_inc(ld_p, 16)
            act.dma_start(p_tok[0:NS, NT - 1, :], p_sample[0].rearrange("b s n -> (b s) n")).then_inc(ld_p, 16)
            act.dma_start(g1b1[:, 0, :], ln1_g[0].partition_broadcast(P)).then_inc(ld_ln1, 16)
            act.dma_start(g1b1[:, 1, :], ln1_b[0].partition_broadcast(P)).then_inc(ld_ln1, 16)
            act.dma_start(rw_raw[:, :, :], w_router[0].rearrange("(c p) n -> p c n", p=P)).then_inc(ld_rt, 16)
            act.dma_start(rbias[:, :], router_bias[0].partition_broadcast(P)).then_inc(ld_rt, 16)
            act.dma_start(cc2[:, :], const2).then_inc(ld_rt, 16)
            with act.Fori(0, 2) as it:
                for h in range(2):
                    split_hi(act, Step(G_WO + h + 1, it, 2), wo_ready, (it * 2 + h) * NT + 1)
            for t in range(NT):
                w = ntok(t)
                act.wait_ge(p_tr, t + 1)
                nc.scalar.activation(pt_hi[:, :, t * P:t * P + w],
                                     att[:, 1 + t % 3, 0:2 * P].rearrange("p (c n) -> p c n", c=2)[:, :, 0:w],
                                     ACT.Copy).then_inc(p_hi, 1)
            act.wait_ge(ld_rt, 48)
            nc.scalar.activation(rw_hi[:, :, :], rw_raw[:, :, :], ACT.Copy).then_inc(rw_h, 1)
            for r0, r1, t0, t1 in ((0, P, 0, NT - 1), (0, NS, NT - 1, NT)):
                act.wait_ge(var_ready, 1)
                nc.scalar.activation(rstd[r0:r1, t0:t1], mv[r0:r1, t0:t1, 1], ACT.Sqrt,
                                     bias=eps[r0:r1, :]).then_inc(std_ready, 1)
            split_hi(act, Step(G_SG), wo_ready, 4 * NT + 1)
            for n, (t, c) in enumerate(QUADS):
                w = ntok(t)
                act.wait_ge(pp_ready, n + 1)
                nc.scalar.activation(ppo[0:w, t, c * 512:(c + 1) * 512], proj[0:w, n % 4, :], ACT.Copy).then_inc(pp_read, 1)
            split_hi(act, Step(G_SU), pp_ready, 2 * NT)
            for n, (t, c) in enumerate(QUADS):
                w = ntok(t)
                act.wait_ge(x2_tr, n + 1)
                nc.scalar.activation(xt_hi[:, 4 * c:4 * c + 4, t * P:t * P + w],
                                     att[:, n % 4, :].rearrange("p (c n) -> p c n", c=4)[:, :, 0:w],
                                     ACT.Copy).then_inc(x2_hi, 1)
            for t in range(NT):
                w = ntok(t)
                act.dma_start(x2_d[t * P:t * P + w, :], res[0:w, t, :]).then_inc(x2_out, 16)
            act.wait_ge(rt_ready, 1)
            logits = att[:, 3, 0:NT * NE].rearrange("p (t n) -> p t n", t=NT)
            nc.scalar.activation(scores[:, 0:NT - 1, :], logits[:, 0:NT - 1, :], ACT.Sigmoid)
            nc.scalar.activation(scores[0:NS, NT - 1, :], logits[0:NS, NT - 1, :], ACT.Sigmoid).then_inc(sc_ready, 1)
            for m in range(2):
                act.wait_ge(su_ready, m + 1)
                if m == 0:
                    act.wait_ge(pp_ready, 2 * NT)
                nc.scalar.activation(two(hs_f[:, m, :]), (proj, att)[m][:, 0:2, 0:HALF], ACT.Sigmoid).then_inc(ss_ready, 1)
            split_hi(act, Step(G_PG), su_ready, 2)
            with act.Fori(0, 2) as it:
                for h in range(2):
                    split_hi(act, Step(G_PG + h + 1, it, 2), pg_ready, (it * 2 + h) * NT + 1)
                    for t in range(NT):
                        w = ntok(t)
                        act.wait_ge(pg_ready, it * 2 * NT + h * NT + t + 2)
                        past(nc.scalar, 0)
                        nc.scalar.activation(sgo[0:w, t, bass.ds((it * 2 + h) * GW, GW)], pg_bank(t)[0:w, 0:GW],
                                             ACT.Sigmoid).then_inc(pg_read, 1)
            act.wait_ge(hs_ready, 2)
            nc.scalar.activation(hs_hi[:, :, :], hs_f[:, :, :], ACT.Copy).then_inc(hs_hd, 1)
            def xt_half(k):
                act.wait_ge(xtr, k + 1)
                nc.scalar.activation(xt[:, 0:4, :].rearrange("p c n -> p (c n)"), proj[:, 0, :], ACT.Copy).then_inc(xt_a, 1)

            xt_half(0)
            act.wait_ge(routed, 1)
            k_half = half_passes(act)
            with act.Fori(0, k_half) as it:
                for i in range(2):
                    k = it * 2 + i
                    act.wait_ge(gu_ready, k + 1)
                    nc.scalar.activation(sg[:, :], att[:, 0, 0:FF], ACT.Sigmoid).then_inc(sg_ready, 1)
                    xt_half(k + 1)
                    act.wait_ge(htr, k + 1)
                    nc.scalar.activation(ht_e[:, :, :].rearrange("p c n -> p (c n)"), att[:, 1, 0:FF], ACT.Copy).then_inc(ht_ready, 1)
                    act.wait_ge(y_mm, k + 1)
                    act.wait_ge(scattered[i], it * 16 + 16)
                    nc.scalar.activation(ysb[i][:, 0:512], proj[:, 2, :], ACT.Copy).then_inc(y_a, 1)
            for t in range(NT):
                w = ntok(t)
                act.wait_ge(var_ready, 2 + t)
                nc.scalar.activation(rstd[0:w, t:t + 1], mv[0:w, t, 1:2], ACT.Sqrt, bias=eps[0:w, :]).then_inc(std_ready, 1)

        @block.tensor
        def _(pe):
            nc.tensor.sem_inc(lg_read, 1)
            nc.tensor.sem_inc(pt_read, 1)
            nc.tensor.sem_inc(pt_ready, 2)
            nc.tensor.sem_inc(pv_ready, 1)
            nc.tensor.sem_inc(o_lo, 1)
            nc.tensor.sem_inc(u_done, 1)
            nc.tensor.sem_inc(mg_ready, 1)

            def chunk(g, i, c, src_hi, src_lo):
                if c == 0:
                    if i == 0:
                        pe.wait_ge(w_ready, g.v + 1)
                    if g.base >= 1:
                        pe.wait_ge(mm_free[i], g.v)
                for n, (w, x) in enumerate(((w_hi, src_hi), (w_hi, src_lo), (w_lo, src_hi))):
                    lhs = w[:, g.par, :].rearrange("p (c n) -> p c n", c=KC)[:, c, i * P:(i + 1) * P]
                    for a in range(2):
                        last = nc.tensor.matmul(proj[:, 2 * i + a, 0:HALF], lhs, x[:, c, a * HALF:(a + 1) * HALF],
                                                start=(c == 0 and n == 0), stop=(c == KC - 1 and n == 2))
                if c == KC - 1:
                    last.then_inc(mm_ready[i], 1)
                return last

            def group(g, src_hi, src_lo):
                for i in range(2):
                    for c in range(KC):
                        chunk(g, i, c, src_hi, src_lo)

            pe.wait_ge(ld_x, 48)
            for n, (t, c) in enumerate(QUADS):
                if n >= 4:
                    pe.wait_ge(x_lo, n - 3)
                w = ntok(t)
                for j in range(4):
                    k = 4 * c + j
                    last = nc.tensor.transpose(att[:, n % 4, j * P:j * P + w], x_tok[0:w, t, k * P:(k + 1) * P],
                                               ident[0:w, 0:w])
                last.then_inc(tr_x, 1)
            pe.wait_ge(ld_conv, 32)
            for c in range(KC):
                nc.tensor.transpose(proj[:, 0, c * 16:(c + 1) * 16], convraw[:, c * P:(c + 1) * P], ident[0:16, 0:16])
            nc.tensor.transpose(proj[:, 0, P:P + 24], cwraw[:, :], ident[0:24, 0:24]).then_inc(tr_conv, 1)
            pe.wait_ge(x_lo, len(QUADS))
            pe.wait_ge(conv_ready, 1)
            group(Step(0), h_hi, h_lo)
            pe.wait_ge(mm_free[0], 1)
            pe.wait_ge(mm_free[1], 1)
            pe.wait_ge(ld_ck, 16)
            for t in range(NT):
                w = ntok(t)
                nc.tensor.transpose(att[0:w, t // 4, t % 4 * P:(t % 4 + 1) * P], v_t[:, t * P:t * P + w], ident[:, :])
            nc.tensor.transpose(att[:, 1, P:2 * P], k_t[:, WIN + SEQ - P:WIN + SEQ], ident[:, :])
            nc.tensor.transpose(att[0:NS, 1, 2 * P:3 * P], k_t[:, WIN + SEQ:], ident[:, :])
            for b in range(NB_S):
                last = nc.tensor.transpose(att[:, 2 + b // 4, b % 4 * P:(b % 4 + 1) * P], cache_k[:, b, :], ident[:, :])
            last.then_inc(tr_kv, 1)
            for j in range(4):
                group(Step(G_Q + j), h_hi, h_lo)

            pe.wait_ge(qs_ready, 1)
            pe.wait_ge(ckt_ready, 1)
            pe.wait_ge(kv_tok_ready, 1)
            for i in range(NB_S):
                for e in range(2):
                    b = (i + 2 * e) % NB_S
                    r = slice(e * HD, (e + 1) * HD)
                    o = att[r, b // 2, b % 2 * KEYS_S:(b % 2 + 1) * KEYS_S]
                    lhs = q_smp[r, b, :]
                    nc.tensor.matmul(o[:, 0:WIN], lhs, cache_kt[r, b, :], start=True, stop=True)
                    last = nc.tensor.matmul(o[:, WIN:KEYS_S], lhs, k_t[r, WIN + SEQ:], start=True, stop=True)
            last.then_inc(sl_ready, 1)
            pe.wait_ge(sl_read, 1)

            with pe.Fori(0, 2) as it:
                for h in range(2):
                    g = Step(G_GA + h, it, 2)
                    u0, b0, blk = it * 16 + h * 8, it * 4 + h * 2, it * 2 + h
                    todo = [(i, c) for i in range(2) for c in range(KC)]

                    def pv(mb):
                        pe.wait_ge(pt_read, u0 + 4 * mb + 4 + 1)
                        pe.wait_ge(o_lo, b0 + mb + 1)
                        for c in range(2):
                            for e in range(2):
                                r = slice(e * HD, (e + 1) * HD)
                                last = nc.tensor.matmul(att[r, 3, :], v_blk[h][:, c, r],
                                                        p_t[:, c, e, :, :].rearrange("p m q -> p (m q)"),
                                                        start=(c == 0), stop=(c == 1))
                        last.then_inc(pv_ready, 1)

                    for s in range(10):
                        for _ in range(CHUNKS_AT[s]):
                            i, c = todo.pop(0)
                            chunk(g, i, c, h_hi, h_lo)
                        if s < 8:
                            if s == 0:
                                pe.wait_ge(blk_ready, blk + 1)
                            pe.wait_ge(lg_read, u0 + s + 1)
                            for e in range(2):
                                r = slice(e * HD, (e + 1) * HD)
                                last = nc.tensor.matmul(att[:, e, 0:2 * P], q_blk[h][r, s, :],
                                                        k_blk[h][r, :], start=True, stop=True)
                            last.then_inc(lg_ready, 1)
                        if s >= 2:
                            m = s - 2
                            pe.wait_ge(p_ready, u0 + m + 1)
                            pe.wait_ge(pt_read, u0 + m + 1)
                            for e in range(2):
                                for c in range(2):
                                    last = nc.tensor.transpose(att[:, 2, (2 * e + c) * P:(2 * e + c + 1) * P],
                                                               s_p[m % 2][:, e, c * P:(c + 1) * P], ident[:, :])
                            last.then_inc(pt_ready, 1)
                        if s == 6:
                            pv(0)
                        if s == 9:
                            pv(1)
            pe.wait_ge(s_prob, 1)
            pe.wait_ge(o_lo, 2 * NBLK + 1)
            pe.wait_ge(ld_cv, 16)
            for b in range(NB_S):
                nc.tensor.transpose(att[:, b // 4, b % 4 * P:(b % 4 + 1) * P], s_s[:, b, 0:WIN], ident[:, :])
            for b in range(NB_S):
                last = nc.tensor.transpose(att[0:NS, 2 + b // 4, b % 4 * P:(b % 4 + 1) * P], s_s[:, b, WIN:KEYS_S],
                                           ident[:, :])
            last.then_inc(s_tr, 1)
            pe.wait_ge(s_trc, 2)
            for b in range(NB_S):
                for e in range(2):
                    r = slice(e * HD, (e + 1) * HD)
                    o = att[r, 0, b * HD:(b + 1) * HD]
                    nc.tensor.matmul(o, cache_v[:, b, r], ps_t[:, b, r], start=True, stop=False)
                    last = nc.tensor.matmul(o, v_tok[0:NS, NT, r], psn_t[:, b, r], start=False, stop=True)
            last.then_inc(s_pv, 1)
            pe.wait_ge(s_ol, 1)
            with pe.Fori(0, 2) as it:
                for h in range(2):
                    group(Step(G_AO + h, it, 2), mix_hi, mix_lo)
            with pe.Fori(0, 2) as it:
                for i in range(6):
                    group(Step(G_C + i, it, 6), h_hi, h_lo)
            pe.wait_ge(cv_lo, KC)
            for c in range(KC):
                last = nc.tensor.transpose(att[0:18, c // 4, c % 4 * P:(c % 4 + 1) * P], cnew[:, c, :], ident[:, :])
            last.then_inc(cn_tr, 1)
            with pe.Fori(0, 4) as it:
                group(Step(G_GC, it, 2), h_hi, h_lo)
                group(Step(G_GC + 1, it, 2), mix_hi, mix_lo)
            nc.tensor.sem_inc(wo_read, NT)
            nc.tensor.sem_inc(pg_read, NT)
            nc.tensor.sem_inc(wo_ready, 1)
            nc.tensor.sem_inc(pg_ready, 1)
            nc.tensor.sem_inc(tb_used, TOPK)
            nc.tensor.sem_inc(y_a, 1)
            nc.tensor.sem_inc(y_dv, 1)

            def tile_products(g, t, x_hi_, x_lo_, out):
                w = ntok(t)
                whi, wlo = (m[:, g.par, :].rearrange("p (c n) -> p c n", c=KC) for m in (w_hi, w_lo))
                for c in range(KC):
                    for n, (x, v) in enumerate(((x_hi_, whi), (x_hi_, wlo), (x_lo_, whi))):
                        last = nc.tensor.matmul(out, x[:, c, t * P:t * P + w], v[:, c, :],
                                                start=(c == 0 and n == 0), stop=(c == KC - 1 and n == 2))
                return last

            def wide_products(g, t, half, x_hi_, x_lo_, out):
                w = ntok(t)
                whi, wlo = (m[:, g.par, :].rearrange("p (c n) -> p c n", c=2) for m in (w_hi, w_lo))
                for c in range(2):
                    for n, (x, v) in enumerate(((x_hi_, whi), (x_hi_, wlo), (x_lo_, whi))):
                        last = nc.tensor.matmul(out, x[:, c, t * P:t * P + w], v[:, c, half * 512:(half + 1) * 512],
                                                start=(c == 0 and n == 0), stop=(c == 1 and n == 2))
                return last

            pe.wait_ge(mg_lo, KC)
            pe.wait_ge(mm_free[0], G_WO)
            pe.wait_ge(mm_free[1], G_WO)
            pe.wait_ge(cn_out, 1)
            with pe.Fori(0, 2) as it:
                for h in range(2):
                    g = Step(G_WO + h, it, 2)
                    pe.wait_ge(w_ready, g.v + 1)
                    for t in range(NT):
                        pe.wait_ge(wo_read, it * 2 * NT + h * NT + t + 1)
                        last = tile_products(g, t, merged_hi, merged_lo, tile_bank(t)[0:ntok(t), 0:GW])
                        last.then_inc(wo_ready, 1)
            pe.wait_ge(ld_p, 32)
            for t in range(NT):
                w = ntok(t)
                if t >= 3:
                    pe.wait_ge(p_lo, t - 2)
                for c in range(2):
                    last = nc.tensor.transpose(att[:, 1 + t % 3, c * P:c * P + w], p_tok[0:w, t, c * P:(c + 1) * P],
                                               ident[0:w, 0:w])
                last.then_inc(p_tr, 1)
            pe.wait_ge(p_lo, NT)
            pe.wait_ge(w_ready, G_PP + 1)
            pe.wait_ge(wo_read, 5 * NT)
            for n, (t, c) in enumerate(QUADS):
                w = ntok(t)
                if n >= 4:
                    pe.wait_ge(pp_read, n - 3)
                last = wide_products(Step(G_PP), t, c, pt_hi, pt_lo, proj[0:w, n % 4, :])
                last.then_inc(pp_ready, 1)
            for n, (t, c) in enumerate(QUADS):
                w = ntok(t)
                pe.wait_ge(x2_ready, t + 1)
                if n >= 4:
                    pe.wait_ge(x2_lo, n - 3)
                for j in range(4):
                    k = 4 * c + j
                    last = nc.tensor.transpose(att[:, n % 4, j * P:j * P + w], res[0:w, t, k * P:(k + 1) * P],
                                               ident[0:w, 0:w])
                last.then_inc(x2_tr, 1)
            pe.wait_ge(x2_lo, 2 * NT)
            pe.wait_ge(rw_ready, 1)
            for t in range(NT):
                w = ntok(t)
                for c in range(KC):
                    for n, (x, v) in enumerate(((xt_hi, rw_hi), (xt_hi, rw_lo), (xt_lo, rw_hi))):
                        last = nc.tensor.matmul(att[0:w, 3, t * NE:(t + 1) * NE], x[:, c, t * P:t * P + w], v[:, c, :],
                                                start=(c == 0 and n == 0), stop=(c == KC - 1 and n == 2))
            last.then_inc(rt_ready, 1)
            pe.wait_ge(w_ready, G_SU + 1)
            pe.wait_ge(pp_read, 2 * NT)
            pe.wait_ge(sc_ready, 1)
            for m in range(2):
                for k, g in enumerate((Step(G_SG), Step(G_SU))):
                    whi, wlo = (v[:, g.par, :].rearrange("p (c n) -> p c n", c=KC) for v in (w_hi, w_lo))
                    for c in range(KC):
                        for n, (v, x) in enumerate(((whi, xt_hi), (whi, xt_lo), (wlo, xt_hi))):
                            for a in range(2):
                                last = nc.tensor.matmul((proj, att)[m][:, 2 * k + a, 0:HALF], v[:, c, m * P:(m + 1) * P],
                                                        x[:, c, a * HALF:(a + 1) * HALF],
                                                        start=(c == 0 and n == 0), stop=(c == KC - 1 and n == 2))
                last.then_inc(su_ready, 1)
            pe.wait_ge(sel_ready, 1)
            pe.wait_ge(hs_ready, 1)
            for t in range(NT):
                for s in range(t + 1):
                    nc.tensor.matmul(proj[:, 0, t * NE:(t + 1) * NE], (ones_b if s < t else tri_b)[:, :], sel[:, s, :],
                                     start=(s == 0), stop=(s == t))
            for s in range(NT):
                last = nc.tensor.matmul(proj[:, 1, 0:NE], ones_b[:, :], sel[:, s, :], start=(s == 0), stop=(s == NT - 1))
            last.then_inc(rank_ready, 1)
            pe.wait_ge(hs_ready, 2)
            with pe.Fori(0, 2) as it:
                for h in range(2):
                    g = Step(G_PG + h, it, 2)
                    pe.wait_ge(w_ready, g.v + 1)
                    for t in range(NT):
                        pe.wait_ge(pg_read, it * 2 * NT + h * NT + t + 1)
                        last = tile_products(g, t, xt_hi, xt_lo, pg_bank(t)[0:ntok(t), 0:GW])
                        last.then_inc(pg_ready, 1)
            pe.wait_ge(tb_ready, 1)

            def table(it, j, start, stop):
                pe.wait_ge(tb_ready, it * TOPK + j + 1)
                nc.tensor.matmul(att[:, 3, 0:MAXPASS], tab_a[:, j, :], tab_b[:, j, :],
                                 start=start, stop=stop).then_inc(tb_used, 1)

            for j in range(TOPK):
                table(0, j, j == 0, False)
            with pe.Fori(1, NT - 1) as it:
                for j in range(TOPK):
                    table(it, j, False, False)
            for j in range(TOPK):
                table(NT - 1, j, False, j == TOPK - 1)
            pe.wait_ge(w_ready, N_GROUPS_W)
            pe.wait_ge(hs_ld, 1)
            pe.wait_ge(rank_read, 1)
            pe.wait_ge(pg_read, 5 * NT)
            for n, (t, c) in enumerate(QUADS):
                w = ntok(t)
                if n >= 4:
                    pe.wait_ge(sd_read, n - 3)
                wide_products(Step(G_SD), t, c, hs_hi, hs_lo, proj[0:w, n % 4, :]).then_inc(sd_ready, 1)
            pe.wait_ge(sd_read, 2 * NT)

            def turn(k):
                pe.wait_ge(gathered, k * 16 + 16)
                for c in range(KC):
                    last = nc.tensor.transpose(proj[:, c // 4, c % 4 * P:(c % 4 + 1) * P], xg[:, :, c], ident[:, :])
                last.then_inc(xtr, 1)

            pe.wait_ge(routed, 1)
            turn(0)
            count = pe.alloc_register("pass_count")
            pe.reg_mov(count, 0)
            with pe.Fori(0, NPE // 2) as it:
                for i in range(2):
                    n_of_pair = pass_counts(pe, it * 2 + i)
                    gate_up = [w_exp[i][:, e, 0:2 * KC * FF].rearrange("p (k c n) -> p c k n", k=2, c=KC) for e in range(2)]
                    down = [w_exp[i][:, e, 2 * KC * FF:].rearrange("p (c n) -> p c n", c=2) for e in range(2)]
                    for n in range(3):
                        pe.wait_ge(w_exp_in[n], (it * 2 + i) * 32 + (32 if n == 0 else 16))
                    past(nc.tensor, 1)
                    with pe.Fori(0, n_of_pair):
                        k = pe.snap(count, min_val=0, max_val=MAXPASS - 3)
                        pe.wait_ge(xt_a, k + 1)
                        pe.wait_ge(xt_d, k + 1)
                        for c in range(KC):
                            for e in range(2):
                                last = nc.tensor.matmul(att[e * SLOT:(e + 1) * SLOT, 0, :], xt[:, c, e * SLOT:(e + 1) * SLOT],
                                                        gate_up[e][:, c, :, :], start=(c == 0), stop=(c == KC - 1))
                        last.then_inc(gu_ready, 1)
                        turn(k + 1)
                        pe.wait_ge(h_ready, k + 1)
                        for c in range(2):
                            last = nc.tensor.transpose(att[:, 1, c * P:(c + 1) * P], h_e[:, c:FF:2], ident[:, :])
                        last.then_inc(htr, 1)
                        for n in range(1, 3):
                            pe.wait_ge(w_exp_in[n], (it * 2 + i) * 32 + 32)
                        pe.wait_ge(ht_ready, k + 1)
                        pe.wait_ge(y_a, k + 1)
                        pe.wait_ge(y_dv, k + 1)
                        for c in range(2):
                            for half in range(2):
                                for e in range(2):
                                    last = nc.tensor.matmul(proj[e * SLOT:(e + 1) * SLOT, 2 + half, :],
                                                            ht_e[:, c, e * SLOT:(e + 1) * SLOT],
                                                            down[e][:, c, half * 512:(half + 1) * 512],
                                                            start=(c == 0), stop=(c == 1))
                        last.then_inc(y_mm, 1)
                        pe.reg_add(count, count, 1)

        @block.vector
        def _(dve):
            for n, (t, c) in enumerate(QUADS):
                dve.wait_ge(x_hi, n + 1)
                w = ntok(t)
                nc.vector.tensor_tensor(h_lo[:, 4 * c:4 * c + 4, t * P:t * P + w],
                                        att[:, n % 4, :].rearrange("p (c n) -> p c n", c=4)[:, :, 0:w],
                                        h_hi[:, 4 * c:4 * c + 4, t * P:t * P + w].bitcast(F32),
                                        ALU.subtract).then_inc(x_lo, 1)
            dve.wait_ge(tr_conv, 1)
            nc.vector.tensor_copy(cst[:, :, :].rearrange("p c n -> p (c n)"), proj[:, 0, 0:P])
            nc.vector.tensor_copy(cw[:, :], proj[:, 0, P:P + 24]).then_inc(conv_ready, 1)
            split_lo(dve, Step(0))
            split_lo(dve, Step(1))
            dve.wait_ge(ld_sink, 32)
            nc.vector.tensor_scalar(nsink16[:, :], sink16[:, :], -1.0, None, ALU.mult)
            nc.vector.tensor_tensor(sel16[:, :], sel16[:, :], sink16[:, :], ALU.mult)
            dve.drain()
            nc.vector.reduce_sum(sink_s[:, :], sel16[:, :], AX.X)
            dve.drain()
            nc.vector.tensor_scalar(nsink_s[:, :], sink_s[:, :], -1.0, None, ALU.mult)
            dve.drain()
            dve.wait_ge(mm_ready[1], 1)
            nc.vector.tensor_copy(two(v_t[:, :]), slot(1)).then_inc(mm_free[1], 1)
            for j in range(4):
                split_lo(dve, Step(G_Q + 1 + j))
                if j == 0:
                    dve.wait_ge(tr_kv, 1)
                    nc.vector.tensor_copy(v_tok[:, 1:NT, :].rearrange("p a n -> p (a n)"), att[:, 0, :])
                    nc.vector.tensor_copy(v_tok[0:NS, NT, :], att[0:NS, 1, 0:P])
                    nc.vector.tensor_copy(k_tok[:, 0, :], att[:, 1, P:2 * P])
                    nc.vector.tensor_copy(k_tok[0:NS, 1, :], att[0:NS, 1, 2 * P:3 * P]).then_inc(kv_tok_ready, 1)
                dve.wait_ge(mm_ready[1], j + 2)
                nc.vector.tensor_scalar(two(q_t[:, 2 * j + 1, :]), slot(1), HD ** -0.5, None, ALU.mult).then_inc(mm_free[1], 1)
            dve.wait_ge(mm_free[0], G_Q + 4)
            dve.drain()
            nc.vector.tensor_copy(q_smp[:, :, :].rearrange("p b (m s) -> p b m s", s=S_S),
                                  q_t[:, :, SEQ:T].rearrange("p m (b s) -> p b m s", b=NB_S)).then_inc(qs_ready, 1)
            dve.wait_ge(sl_ready, 1)
            dve.wait_ge(ld_c1, 32)
            for n in range(4):
                last = nc.vector.tensor_tensor(s_s[:, 2 * n:2 * n + 2, :].rearrange("p b k -> p (b k)"),
                                               att[:, n, 0:2 * KEYS_S],
                                               mask_s[:, 2 * n:2 * n + 2, :].rearrange("p b k -> p (b k)"), ALU.add)
            last.then_inc(sl_read, 1)
            dve.drain()
            nc.vector.reduce_max(mx_s[:, :], s_s[:, :, :], AX.X)
            dve.drain()
            nc.vector.tensor_scalar(nm_s[:, :], mx_s[:, :], -1.0, nsink_s[:, :], ALU.mult, ALU.min)
            dve.drain()
            nc.vector.tensor_tensor(s_s[:, :, :], s_s[:, :, :], nm_s[:, :].unsqueeze(2).to_broadcast([P, NB_S, KEYS_S]),
                                    ALU.add).then_inc(s_sub, 1)

            dve.wait_ge(zeroed, 2)
            with dve.Fori(0, 2) as it:
                for h in range(2):
                    u0, b0, blk = it * 16 + h * 8, it * 4 + h * 2, it * 2 + h
                    dve.wait_ge(mm_free[0], G_Q + 4)
                    nc.vector.tensor_copy(q_blk[h][:, :, :], q_t[:, :, bass.ds(blk * P, P)])
                    nc.vector.tensor_copy(k_blk[h][:, :], k_t[:, bass.ds(blk * P, 2 * P)])
                    nc.vector.tensor_copy(v_blk[h][:, :, :], v_tok[:, bass.ds(blk, 2), :]).then_inc(blk_ready, 1)
                    if h == 0:
                        nc.vector.tensor_copy(mask_0[:, :], mask_p[:, bass.ds(it, 1), :].rearrange("p o n -> p (o n)"))
                        dve.drain()
                    mk = mask_0[:, :] if h == 0 else mask_p[:, 1, :]
                    for s in range(10):
                        if s < 8:
                            r = s % 2
                            dve.wait_ge(lg_ready, u0 + s + 1)
                            dve.wait_ge(pt_ready, u0 + s + 1)
                            past(nc.vector, 2)
                            for e in range(2):
                                last = nc.vector.tensor_tensor_reduce(s_p[r][:, e, :], att[:, e, 0:2 * P], mk, 1.0, -BIG,
                                                                      ALU.add, ALU.max, mx[:, r, e:e + 1])
                            last.then_inc(lg_read, 1)
                            dve.drain()
                            nc.vector.scalar_tensor_tensor(nm[:, r, :], mx[:, r, :], -1.0, nsink16[:, s:16:8],
                                                           ALU.mult, ALU.min)
                            dve.drain()
                            nc.vector.tensor_tensor(ds[:, r, :], nm[:, r, :], sink16[:, s:16:8], ALU.add).then_inc(nm_ready, 1)
                        if 1 <= s <= 8:
                            r = (s - 1) % 2
                            dve.wait_ge(e_ready, u0 + s)
                            nc.vector.tensor_tensor(rc[:, r, :], sm_p[:, r, :], es[:, r, :], ALU.add)
                            dve.drain()
                            nc.vector.reciprocal(rc[:, r, :], rc[:, r, :])
                            dve.drain()
                            for e in range(2):
                                last = nc.vector.tensor_scalar(s_p[r][:, e, :], s_p[r][:, e, :], rc[:, r, e:e + 1], None, ALU.mult)
                            last.then_inc(p_ready, 1)
                        if s == 5:
                            split_lo(dve, Step(G_GA + h + 1, it, 2))
                        if s == 6:
                            dve.wait_ge(mm_ready[0], it * 2 + h + G_GA + 1)
                            nc.vector.tensor_copy(two(row(gate_a, it * 4 + 2 * h)), slot(0)).then_inc(mm_free[0], 1)
                        if s == 8 or s == 9:
                            mb = s - 8
                            dve.wait_ge(o_hi, b0 + mb + 1)
                            nc.vector.tensor_tensor(mix_lo[:, 4 * mb:4 * mb + 4, bass.ds(blk * P, P)],
                                                    att[:, 3, :].rearrange("p (m q) -> p m q", m=4),
                                                    mix_hi[:, 4 * mb:4 * mb + 4, bass.ds(blk * P, P)].bitcast(F32),
                                                    ALU.subtract).then_inc(o_lo, 1)
            dve.wait_ge(s_exp, 1)
            nc.vector.reduce_sum(sum_s[:, :], s_s[:, :, :], AX.X)
            dve.drain()
            nc.vector.tensor_tensor(sum_s[:, :], sum_s[:, :], es_s[:, :], ALU.add)
            dve.drain()
            nc.vector.reciprocal(sum_s[:, :], sum_s[:, :])
            dve.drain()
            nc.vector.tensor_tensor(s_s[:, :, :], s_s[:, :, :], sum_s[:, :].unsqueeze(2).to_broadcast([P, NB_S, KEYS_S]),
                                    ALU.mult).then_inc(s_prob, 1)
            dve.wait_ge(s_tr, 1)
            nc.vector.tensor_copy(psn_t[:, :, :].rearrange("p (a b) n -> p a (b n)", a=2), att[0:NS, 2:4, :]).then_inc(s_trc, 1)
            dve.wait_ge(s_oh, 1)
            nc.vector.tensor_tensor(mix_lo[:, :, SEQ:T].rearrange("p m (b s) -> p b m s", b=NB_S),
                                    att[:, 0, :].rearrange("p (b m s) -> p b m s", b=NB_S, m=8),
                                    mix_hi[:, :, SEQ:T].rearrange("p m (b s) -> p b m s", b=NB_S).bitcast(F32),
                                    ALU.subtract).then_inc(s_ol, 1)
            with dve.Fori(0, 2) as it:
                for h in range(2):
                    split_lo(dve, Step(G_AO + h + 1, it, 2))
                    dve.wait_ge(sga, it * 2 + h + 1)
                    for i in range(2):
                        dve.wait_ge(mm_ready[i], it * 2 + h + G_AO + 1)
                        m = row(gate_a, it * 4 + 2 * h + i)
                        nc.vector.tensor_tensor(two(m), slot(i), two(m), ALU.mult).then_inc(mm_free[i], 1)
            for i in range(2):
                nc.vector.memset(u_ext[i][:, 0:2], 0.0)
            with dve.Fori(0, 2) as it:
                for jj in range(2):
                    m0 = it * 4 + 2 * jj
                    for k in range(3):
                        gb = G_C + 3 * jj + k
                        split_lo(dve, Step(gb + 1, it, 6))
                        if k == 1:
                            for i in range(2):
                                u = u_ext[i]
                                us = u[:, 514:594].rearrange("p (b n) -> p b n", n=10)
                                dve.wait_ge(mm_free[i], it * 6 + gb)
                                dve.wait_ge(mm_ready[i], it * 6 + gb + 1)
                                nc.vector.tensor_tensor(u[:, 2:2 + HALF], proj[:, 2 * i, 0:HALF], cc_t[:, i, 0:HALF], ALU.mult)
                                nc.vector.tensor_tensor(u[:, 2 + HALF:514], proj[:, 2 * i + 1, 0:SEQ - HALF],
                                                        cc_t[:, i, HALF:SEQ], ALU.mult)
                                nc.vector.tensor_tensor(us[:, :, 2:10],
                                                        proj[:, 2 * i + 1, SEQ - HALF:HALF].rearrange("p (b s) -> p b s", b=NB_S),
                                                        cc_t[:, i, SEQ:T].rearrange("p (b s) -> p b s", b=NB_S),
                                                        ALU.mult).then_inc(mm_free[i], 1)
                                nc.vector.tensor_copy(us[:, :, 0:2],
                                                      row(cst, m0 + i).rearrange("p (b j) -> p b j", j=2)).then_inc(u_done, 1)
                            dve.drain()
                            for i in range(2):
                                u = u_ext[i]
                                us = u[:, 514:594].rearrange("p (b n) -> p b n", n=10)
                                cn = row(cnew, m0 + i)
                                nc.vector.tensor_copy(cn[:, 0:2], u[:, 512:514])
                                nc.vector.tensor_copy(cn[:, 2:18].rearrange("p (b j) -> p b j", j=2), us[:, :, 8:10])
                            for j in range(3):
                                for i in range(2):
                                    wj_ = cw[:, bass.ds(m0 + (j * KC + i), 1)]
                                    u = u_ext[i][:, j:j + 592]
                                    if j == 0:
                                        nc.vector.tensor_scalar(y_cv[i][:, 0:592], u, wj_, None, ALU.mult)
                                    else:
                                        nc.vector.scalar_tensor_tensor(y_cv[i][:, 0:592], u, wj_, y_cv[i][:, 0:592], ALU.mult, ALU.add)
                                dve.drain()
                        if k == 2:
                            for i in range(2):
                                dve.wait_ge(mm_ready[i], it * 6 + gb + 1)
                                nc.vector.tensor_tensor(prod[i][:, 0:HALF], proj[:, 2 * i, 0:HALF], y_cv[i][:, 0:HALF], ALU.mult)
                                nc.vector.tensor_tensor(prod[i][:, HALF:SEQ], proj[:, 2 * i + 1, 0:SEQ - HALF],
                                                        y_cv[i][:, HALF:SEQ], ALU.mult)
                                last = nc.vector.tensor_tensor(
                                    prod[i][:, SEQ:T].rearrange("p (b s) -> p b s", b=NB_S),
                                    proj[:, 2 * i + 1, SEQ - HALF:HALF].rearrange("p (b s) -> p b s", b=NB_S),
                                    y_cv[i][:, 514:594].rearrange("p (b n) -> p b n", n=10)[:, :, 0:S_S], ALU.mult)
                                last.then_inc(mm_free[i], 1)
                                dve.drain().then_inc(pr_ready, 1)
                            for i in range(2):
                                dve.wait_ge(cv_hi, m0 + i + 1)
                                nc.vector.tensor_tensor(row(mix_lo, m0 + i), prod[i][:, :], row(mix_hi, m0 + i).bitcast(F32),
                                                        ALU.subtract).then_inc(cv_lo, 1)
            with dve.Fori(0, 4) as it:
                split_lo(dve, Step(G_GC + 1, it, 2))
                split_lo(dve, Step(G_GC + 2, it, 2))
                for i in range(2):
                    dve.wait_ge(mm_free[i], it * 2 + G_GC + 1)
                    dve.wait_ge(mm_ready[i], it * 2 + G_GC + 2)
                    nc.vector.tensor_tensor(two(prod[i][:, :]), slot(i), two(sig_c[:, i, :]), ALU.mult).then_inc(mm_free[i], 1)
                    dve.drain()
                    nc.vector.tensor_tensor(prod[i][:, :], prod[i][:, :], row(gate_a, it * 2 + i), ALU.add).then_inc(mg_ready, 1)
                for i in range(2):
                    dve.wait_ge(mg_hi, it * 2 + i + 1)
                    nc.vector.tensor_tensor(row(merged_lo, it * 2 + i), prod[i][:, :], row(merged_hi, it * 2 + i).bitcast(F32),
                                            ALU.subtract).then_inc(mg_lo, 1)
            nc.vector.memset(eps[:, :], LN_EPS)
            dve.wait_ge(ld_res, 32)
            with dve.Fori(0, 2) as it:
                for h in range(2):
                    split_lo(dve, Step(G_WO + h + 1, it, 2))
                    for t in range(NT):
                        w = ntok(t)
                        r = res[0:w, t, bass.ds((it * 2 + h) * GW, GW)]
                        dve.wait_ge(wo_ready, it * 2 * NT + h * NT + t + 2)
                        nc.vector.scalar_tensor_tensor(r, r, ALPHA, tile_bank(t)[0:w, 0:GW], ALU.mult, ALU.add).then_inc(wo_read, 1)
                        dve.drain()
                        nc.vector.bn_stats(stats[0:w, t, bass.ds(it * 2 + h, 1), :].rearrange("p o n -> p (o n)"), r)
            for t in range(NT):
                w = ntok(t)
                dve.wait_ge(p_hi, t + 1)
                nc.vector.tensor_tensor(pt_lo[:, :, t * P:t * P + w],
                                        att[:, 1 + t % 3, 0:2 * P].rearrange("p (c n) -> p c n", c=2)[:, :, 0:w],
                                        pt_hi[:, :, t * P:t * P + w].bitcast(F32), ALU.subtract).then_inc(p_lo, 1)
            for t in range(NT):
                w = ntok(t)
                last = nc.vector.bn_aggr(mv[0:w, t, :], stats[0:w, t, :, :])
            last.then_inc(var_ready, 1)
            dve.wait_ge(rw_h, 1)
            nc.vector.tensor_tensor(rw_lo[:, :, :], rw_raw[:, :, :], rw_hi[:, :, :].bitcast(F32), ALU.subtract).then_inc(rw_ready, 1)
            dve.wait_ge(std_ready, 2)
            dve.wait_ge(ld_ln1, 32)

            def normalise(t, gb):
                w = ntok(t)
                nc.vector.tensor_scalar(res[0:w, t, :], res[0:w, t, :], mv[0:w, t, 0:1], rstd[0:w, t:t + 1],
                                        ALU.subtract, ALU.mult)
                dve.drain()
                nc.vector.tensor_tensor(res[0:w, t, :], res[0:w, t, :], gb[0:w, 0, :], ALU.mult)
                dve.drain()
                return nc.vector.tensor_tensor(res[0:w, t, :], res[0:w, t, :], gb[0:w, 1, :], ALU.add)

            nc.vector.reciprocal(rstd[:, 0:NT - 1], rstd[:, 0:NT - 1])
            nc.vector.reciprocal(rstd[0:NS, NT - 1:NT], rstd[0:NS, NT - 1:NT])
            dve.drain()
            for t in range(NT + 1):
                if t < NT:
                    normalise(t, g1b1).then_inc(x2_ready, 1)
                if t >= 1:
                    w = ntok(t - 1)
                    for c in range(2):
                        n = 2 * (t - 1) + c
                        dve.wait_ge(x2_hi, n + 1)
                        nc.vector.tensor_tensor(xt_lo[:, 4 * c:4 * c + 4, (t - 1) * P:(t - 1) * P + w],
                                                att[:, n % 4, :].rearrange("p (c n) -> p c n", c=4)[:, :, 0:w],
                                                xt_hi[:, 4 * c:4 * c + 4, (t - 1) * P:(t - 1) * P + w].bitcast(F32),
                                                ALU.subtract).then_inc(x2_lo, 1)

            dve.wait_ge(rt_ready, 1)
            nc.vector.tensor_copy(tri_b[:, :], tri)
            nc.vector.tensor_copy(ones_b[:, :], ones)
            nc.vector.memset(scores[NS:P, NT - 1, :], 0.0)
            dve.wait_ge(sc_ready, 1)
            dve.drain()
            nc.vector.tensor_tensor(biased[:, :, :], scores[:, :, :], rbias[:, :].unsqueeze(1).to_broadcast([P, NT, NE]), ALU.add)
            dve.drain()
            for t in range(NT):
                for g in range(NGRP):
                    nc.vector.max(best8[:, t * NGRP + g, :], biased[:, t, g * 8:(g + 1) * 8])
            dve.drain()
            nc.vector.tensor_tensor(gsum[:, :, :].rearrange("p t g -> p (t g)"), best8[:, :, 0], best8[:, :, 1], ALU.add)
            dve.drain()
            for t in range(NT):
                nc.vector.max(gbest[:, t, :], gsum[:, t, :])
            dve.drain()
            for t in range(NT):
                nc.vector.max_index(gidx[:, t, :], gbest[:, t, :], gsum[:, t, :])
            dve.drain()
            nc.vector.tensor_copy(gidx_f[:, :, :], gidx[:, :, 0:TOPG])
            dve.drain()
            for t in range(NT):
                nc.vector.tensor_tensor(ghot[:, t, :, :], iota64[:, 0:NGRP].unsqueeze(1).to_broadcast([P, TOPG, NGRP]),
                                        gidx_f[:, t, :].unsqueeze(2).to_broadcast([P, TOPG, NGRP]), ALU.is_equal)
            dve.drain()
            nc.vector.reduce_sum(gmask[:, :, :], ghot[:, :, :, :].rearrange("p t i g -> p t g i"), AX.X)
            dve.drain()
            nc.vector.tensor_scalar(gmask[:, :, :], gmask[:, :, :], BIG, -BIG, ALU.mult, ALU.add)
            dve.drain()
            nc.vector.tensor_tensor(biased[:, :, :].rearrange("p t (g n) -> p (t g) n", n=8),
                                    biased[:, :, :].rearrange("p t (g n) -> p (t g) n", n=8),
                                    gmask[:, :, :].rearrange("p t g -> p (t g)").unsqueeze(2).to_broadcast([P, NT * NGRP, 8]),
                                    ALU.add)
            dve.drain()
            for t in range(NT):
                nc.vector.max(ebest[:, t, :], biased[:, t, :])
            dve.drain()
            for t in range(NT):
                nc.vector.max_index(eidx[:, t, :], ebest[:, t, :], biased[:, t, :])
            dve.drain()
            nc.vector.tensor_copy(eidx_f[:, :, :], eidx[:, :, 0:TOPK])
            dve.drain()
            nc.vector.memset(eidx_f[NS:P, NT - 1, :], -1.0)
            dve.drain()
            nc.vector.tensor_tensor(hot[:, :, :], iota64.unsqueeze(1).to_broadcast([P, NTK, NE]),
                                    eidx_f[:, :, :].rearrange("p t j -> p (t j)").unsqueeze(2).to_broadcast([P, NTK, NE]),
                                    ALU.is_equal)
            dve.drain()
            with nc.allow_low_precision(reason="each sum is 0 or 1, exact in bfloat16"):
                nc.vector.reduce_sum(sel[:, :, :], hot[:, :, :].rearrange("p (t j) e -> p t e j", t=NT), AX.X).then_inc(sel_ready, 1)

            def shared_act(m):
                dve.wait_ge(ss_ready, m + 1)
                ps = (proj, att)[m]
                nc.vector.tensor_tensor(two(hs_f[:, m, :]), ps[:, 0:2, 0:HALF], two(hs_f[:, m, :]), ALU.mult)
                dve.drain()
                nc.vector.tensor_tensor(two(hs_f[:, m, :]), ps[:, 2:4, 0:HALF], two(hs_f[:, m, :]), ALU.mult).then_inc(hs_ready, 1)

            def pick(dst, per_expert):
                for t in range(NT):
                    js = slice(t * TOPK, (t + 1) * TOPK)
                    nc.vector.tensor_tensor(picked[:, js, :], hot[:, js, :],
                                            per_expert[:, t, :].unsqueeze(1).to_broadcast([P, TOPK, NE]), ALU.mult)
                dve.drain()
                nc.vector.reduce_sum(dst, picked[:, :, :], AX.X)
                dve.drain()

            shared_act(0)
            pick(wj[:, :], scores)
            wj3 = wj[:, :].rearrange("p (t j) -> p t j", t=NT)
            nc.vector.reduce_sum(ssum[:, :], wj3, AX.X)
            dve.drain()
            nc.vector.memset(ssum[NS:P, NT - 1:NT], 1.0)
            dve.drain()
            nc.vector.reciprocal(ssum[:, :], ssum[:, :])
            dve.drain()
            nc.vector.tensor_tensor(wj3, wj3, ssum[:, :].unsqueeze(2).to_broadcast([P, NT, TOPK]), ALU.mult)
            dve.drain()
            nc.vector.tensor_scalar(wj[:, :], wj[:, :], ROUTED_SCALE, None, ALU.mult)
            shared_act(1)
            dve.wait_ge(rank_ready, 1)
            nc.vector.tensor_copy(base64[:, :], proj[:, 1, 0:NE:2])
            dve.drain()
            nc.vector.tensor_tensor(nmax[:, :], base64[:, :], proj[:, 1, 1:NE:2], ALU.max)
            dve.drain()
            nc.vector.tensor_scalar(npass_i[:, :], nmax[:, :], SLOT - 1.0, None, ALU.add)
            nc.vector.tensor_copy(rank_i[:, :, :].rearrange("p t e -> p (t e)"), proj[:, 0, 0:NT * NE]).then_inc(rank_read, 1)
            dve.drain()
            nc.vector.tensor_scalar(npass_i[:, :], npass_i[:, :], 6, None, ALU.arith_shift_right)
            dve.drain()
            nc.vector.tensor_scalar(npass_f[:, :], npass_i[:, :], 1.0, None, ALU.max)
            dve.drain()
            cur = npass_f
            for s in range(5):
                nxt = cums[s % 2]
                nc.vector.tensor_copy(nxt[:, 0:1 << s], cur[:, 0:1 << s])
                nc.vector.tensor_tensor(nxt[:, 1 << s:], cur[:, 1 << s:], cur[:, 0:NPE - (1 << s)], ALU.add)
                dve.drain()
                cur = nxt
            nc.vector.tensor_copy(npass_i[:, :], cur[:, :])
            dve.drain()
            nc.vector.tensor_scalar(npass_i[:, :], npass_i[:, :], 1, None, ALU.bitwise_and)
            dve.drain()
            nc.vector.tensor_copy(nmax[:, :], npass_i[:, :])
            dve.drain()
            nc.vector.tensor_copy(n_pass[:, 0:NPE - 1], npass_f[0:1, 0:NPE - 1])
            nc.vector.tensor_tensor(n_pass[:, NPE - 1:NPE], npass_f[0:1, NPE - 1:NPE], nmax[0:1, NPE - 1:NPE], ALU.add)
            nc.vector.tensor_copy(cum_pass[:, 0:NPE - 1], cur[0:1, 0:NPE - 1])
            nc.vector.tensor_tensor(nmax[0:1, 0:1], cur[0:1, NPE - 1:NPE], nmax[0:1, NPE - 1:NPE], ALU.add)
            dve.drain()
            nc.vector.tensor_copy(cum_pass[:, NPE - 1:NPE], nmax[0:1, 0:1])
            nc.vector.tensor_scalar(half_all[:, :], nmax[0:1, 0:1], 0.5, None, ALU.mult)
            nc.vector.tensor_tensor(base64[:, :], cur[:, :], npass_f[:, :], ALU.subtract)
            col_i = col_map[:, :, :].bitcast(I32)
            nc.vector.tensor_scalar(col_i, rank_i[:, :, :], 6, None, ALU.arith_shift_right)
            nc.vector.tensor_scalar(slot_map[:, :, :].bitcast(I32), rank_i[:, :, :], SLOT - 1, None, ALU.bitwise_and)
            dve.drain()
            nc.vector.tensor_copy(col_map[:, :, :], col_i)
            nc.vector.tensor_copy(slot_map[:, :, :], slot_map[:, :, :].bitcast(I32))
            dve.drain()
            for t in range(NT):
                nc.vector.tensor_tensor(col_map[:, t, :].rearrange("p (q e) -> p q e", e=2),
                                        col_map[:, t, :].rearrange("p (q e) -> p q e", e=2),
                                        base64[:, :].unsqueeze(2).to_broadcast([P, NPE, 2]), ALU.add)
            nc.vector.tensor_tensor(slot_map[:, :, :], slot_map[:, :, :], side.unsqueeze(1).to_broadcast([P, NT, NE]), ALU.add)
            dve.drain()
            pick(col_j[:, :], col_map)
            pick(slot_j[:, :], slot_map)
            with dve.Fori(0, NT) as it:
                for j in range(TOPK):
                    n = it * TOPK + j
                    dve.wait_ge(tb_used, n + 1)
                    nc.vector.tensor_scalar(tab_a[:, j, :], iota128, slot_j[:, bass.ds(n, 1)], None, ALU.is_equal)
                    nc.vector.tensor_scalar(tab_b[:, j, :], iota_pass, col_j[:, bass.ds(n, 1)], val[:, bass.ds(n, 1)],
                                            ALU.is_equal, ALU.mult).then_inc(tb_ready, 1)
            dve.wait_ge(tb_used, NTK + TOPK)
            nc.vector.tensor_scalar(tab_e[:, :], att[:, 3, 0:MAXPASS], 0.0, PAD_V, ALU.is_equal, ALU.mult)
            dve.drain()
            nc.vector.tensor_tensor(tab_i[:, :], tab_e[:, :], att[:, 3, 0:MAXPASS], ALU.add)
            dve.drain()
            nc.vector.tensor_scalar(tab_s[:, :], tab_i[:, :], 3, None, ALU.arith_shift_right)
            dve.drain()
            nc.vector.tensor_scalar(tabx[:, :], tab_s[:, :], -1.0, None, ALU.add)
            nc.vector.tensor_scalar(tab_f[:, :], tab_s[:, :], -2.0, -6.0, ALU.mult, ALU.add)
            dve.drain()
            nc.vector.tensor_tensor(taby[:, :], tab_i[:, :], tab_f[:, :], ALU.add)
            dve.drain().then_inc(routed, 1)
            dve.wait_ge(hs_hd, 1)
            nc.vector.tensor_tensor(hs_lo[:, :, :], hs_f[:, :, :], hs_hi[:, :, :].bitcast(F32), ALU.subtract).then_inc(hs_ld, 1)
            dve.wait_ge(pg_read, 5 * NT)
            dve.wait_ge(x2_out, 16 * NT)
            for t in range(NT):
                w = ntok(t)
                nc.vector.tensor_tensor(sgo[0:w, t, :], sgo[0:w, t, :], ppo[0:w, t, :], ALU.mult)
                dve.drain()
                last = nc.vector.scalar_tensor_tensor(res[0:w, t, :], res[0:w, t, :], ALPHA, sgo[0:w, t, :], ALU.mult, ALU.add)
            last.then_inc(res_done, 1)
            for n, (t, c) in enumerate(QUADS):
                w = ntok(t)
                dve.wait_ge(sd_ready, n + 1)
                if n == 0:
                    dve.drain()
                r = res[0:w, t, c * 512:(c + 1) * 512]
                nc.vector.tensor_tensor(r, r, proj[0:w, n % 4, :], ALU.add).then_inc(sd_read, 1)

            def xt_half(k):
                dve.wait_ge(xtr, k + 1)
                nc.vector.tensor_copy(xt[:, 4:8, :].rearrange("p c n -> p (c n)"), proj[:, 1, :]).then_inc(xt_d, 1)

            xt_half(0)
            k_half = half_passes(dve)
            with dve.Fori(0, k_half) as it:
                for i in range(2):
                    k = it * 2 + i
                    dve.wait_ge(sg_ready, k + 1)
                    nc.vector.tensor_tensor(g_e[:, :], sg[:, :], att[:, 0, 0:FF], ALU.mult)
                    dve.drain()
                    nc.vector.tensor_tensor(h_e[:, :], g_e[:, :], att[:, 0, FF:2 * FF], ALU.mult).then_inc(h_ready, 1)
                    xt_half(k + 1)
                    dve.wait_ge(y_mm, k + 1)
                    dve.wait_ge(scattered[i], it * 16 + 16)
                    nc.vector.tensor_copy(ysb[i][:, 512:D], proj[:, 3, :]).then_inc(y_dv, 1)
            def finish(t):
                w = ntok(t)
                dve.wait_ge(std_ready, 3 + t)
                nc.vector.reciprocal(rstd[0:w, t:t + 1], rstd[0:w, t:t + 1])
                dve.drain()
                normalise(t, g2b2).then_inc(y_done, 1)

            for t in range(NT):
                w = ntok(t)
                dve.wait_ge(ld_y[t % 2], 16 * (t // 2 + 1))
                for j in range(TOPK):
                    n = t * TOPK + j
                    dve.drain()
                    last = nc.vector.scalar_tensor_tensor(res[0:w, t, :], y_buf[t % 2][0:w, j, :], wj[0:w, n:n + 1],
                                                          res[0:w, t, :], ALU.mult, ALU.add)
                last.then_inc(y_used, 1)
                dve.drain()
                for c in range(2):
                    nc.vector.bn_stats(stats[0:w, t, c, :], res[0:w, t, c * 512:(c + 1) * 512])
                dve.drain()
                nc.vector.bn_aggr(mv[0:w, t, :], stats[0:w, t, 0:2, :]).then_inc(var_ready, 1)
                if t >= 1:
                    finish(t - 1)
            finish(NT - 1)


_INS = ["x_prompt", "x_sample", "p_prompt", "p_sample", "state_win_k", "state_win_v", "state_conv", "w_in", "attn_sinks",
        "conv_w", "w_attn_out", "w_conv_out", "w_o", "ln1_g", "ln1_b", "w_router", "router_bias", "w_e_gate", "w_e_up",
        "w_e_down", "w_s_gate", "w_s_up", "w_s_down", "w_ple_gate", "w_ple_proj", "ln2_g", "ln2_b"]
_OUTS = [(1, SEQ, D), (NB_S, S_S, D), (1, 1, WIN, N_KV, HD), (1, 1, WIN, N_KV, HD), (1, 1, 2, D),
         (1, NB_S, WIN, N_KV, HD), (1, NB_S, WIN, N_KV, HD), (1, NB_S, 2, D)]


def kernel(**inputs):
    import concourse.bacc as bacc
    from concourse.bass_utils import run_bass_kernel_spmd

    nc = bacc.Bacc("TRN2", target_bir_lowering=False, num_devices=1)
    arrays, args = {}, []
    data = [(name, np.ascontiguousarray(inputs[name])) for name in _INS]
    data += list(zip(("const1", "const2"), pack_constants()))
    for name, a in data:
        arrays[f"in_{name}_dram"] = a
        args.append(nc.dram_tensor(f"in_{name}_dram", a.shape, mybir.dt.from_np(a.dtype), kind="ExternalInput").ap())
    for i, shape in enumerate(_OUTS):
        args.append(nc.dram_tensor(f"out_{i}_dram", shape, F32, kind="ExternalOutput").ap())
    decoder_step(nc, *args)
    r = run_bass_kernel_spmd(nc, [arrays], core_ids=[0])
    return tuple(r.results[0][f"out_{i}_dram"] for i in range(len(_OUTS)))
```

```python
from contextlib import ExitStack

import numpy as np

import concourse.bass as bass
from concourse import mybir

F32 = mybir.dt.float32
F32R = mybir.dt.float32r
BF16 = mybir.dt.bfloat16
I32 = mybir.dt.int32
U32 = mybir.dt.uint32
ALU = mybir.AluOpType
ACT = mybir.ActivationFunctionType
AX = mybir.AxisListType

P = 128
D = 1024
KC = D // P
SEQ, NB_S, S_S = 512, 8, 8
NS = NB_S * S_S
T = SEQ + NS
HALF = T // 2
NT = (T + P - 1) // P
N_HEADS, N_KV, HD = 16, 2, 64
NPAIR_H = N_HEADS // N_KV
WIN = 128
NBLK = SEQ // WIN
KEYS_S = WIN + NS
Q_W, KV_W = N_HEADS * HD, N_KV * HD
PLE = 256
NE, TOPK, NGRP, TOPG = 64, 6, 8, 4
FF = 256
ROUTED_SCALE = 2.5
ALPHA = 2 ** 0.25
LN_EPS = 1e-5
NPE = NE // 2
SLOT = 64
MAXPASS = NPE + T * TOPK // SLOT + 4
BIG = 1e30
PAD_V = 16000.0

COL_K, COL_CB = Q_W, Q_W + 2 * KV_W
COL_CC, COL_CH = COL_CB + D, COL_CB + 2 * D
COL_GA, COL_GC = COL_CB + 3 * D, COL_CB + 4 * D

GW = 256
G_Q, G_GA, G_AO, G_C, G_GC, G_WO, G_SG, G_SU, G_P0, G_SD, G_PP, G_PG = 1, 5, 9, 13, 25, 33, 37, 38, 39, 40, 41, 42
N_GROUPS_W = 45


def pack_constants():
    neg = -BIG
    ident = np.eye(P, dtype=np.float32)
    q, k = np.arange(P)[:, None] + P, np.arange(2 * P)[None]
    band = (q - k >= 0) & (q - k < WIN)
    first = band & (k >= P)
    mask_p = np.where(np.stack([first, band], 1), 0.0, neg).astype(np.float32).reshape(P, -1)
    row = np.arange(P)
    s_of = row % S_S
    mask_s = np.full((P, NB_S, KEYS_S), neg, np.float32)
    for b in range(NB_S):
        j = np.arange(WIN)[None]
        mask_s[:, b, :WIN] = np.where(j > s_of[:, None], 0.0, neg)
        for s in range(S_S):
            mask_s[:, b, WIN + b * S_S + s] = np.where(s <= s_of, 0.0, neg)
    sel16 = (np.arange(16)[None] == (row[:, None] // 64) * 8 + (row[:, None] % 64) // 8)
    first_part = np.concatenate([ident, mask_p, mask_s.reshape(P, -1), sel16.astype(np.float32)], 1)
    tri = (row[:, None] < row[None, :]).astype(np.float32)
    iota64 = np.tile(np.arange(64, dtype=np.float32), (P, 1))
    iota128 = np.tile(np.arange(128, dtype=np.float32), (P, 1))
    iota_pass = np.tile(np.arange(MAXPASS, dtype=np.float32), (P, 1))
    side = np.tile((np.arange(NE) % 2 * SLOT).astype(np.float32), (P, 1))
    tok = np.arange(NT)[None, :, None] * P + row[:, None, None]
    val = np.where(tok < T, tok * 8 + np.arange(TOPK)[None, None] + 8, 0).astype(np.float32).reshape(P, -1)
    ones = np.ones((P, P), np.float32)
    sum_row = np.where(row[:, None] < SLOT, 0, T).astype(np.float32)
    second_part = np.concatenate([tri, ones, iota64, iota128, iota_pass, side, val, sum_row], 1)
    return np.ascontiguousarray(first_part, np.float32), np.ascontiguousarray(second_part, np.float32)


C1_W = P + 2 * 2 * P + NB_S * KEYS_S + 16
C2_W = P + P + 64 + P + MAXPASS + 64 + NT * TOPK + 1


class Step:

    def __init__(self, base, it=0, per=0):
        self.base = base
        self.v = base + it * per
        self.par = base % 2
        self.half = base // 2 + it * (per // 2)


def decoder_step(nc, x_prompt, x_sample, p_prompt, p_sample, win_k, win_v, conv_state, w_in, sinks,
                 conv_w, w_ao, w_co, w_o, ln1_g, ln1_b, w_router, router_bias, w_eg, w_eu, w_ed,
                 w_sg, w_su, w_sd, w_pg, w_pp, ln2_g, ln2_b, const1, const2,
                 y_prompt, y_sample, nk_p, nv_p, nconv_p, nk_s, nv_s, nconv_s):
    ctx = ExitStack()
    with ctx:
        base0 = (nc.sbuf_base + 31) // 32 * 32
        def at(name, shape, dt, off):
            return nc.alloc_sbuf_tensor_at(name, shape, dt, offset=base0 + off)

        def sem(name):
            return ctx.enter_context(nc.semaphore(name))

        o_a, o_c, o_ring = 0, 36864, 73728
        o_b, o_d, o_e, o_f = 122880, 141312, 159744, 167936
        h_hi = at("h_hi", [P, KC, T], F32R, o_a)
        h_lo = at("h_lo", [P, KC, T], F32R, o_a + 18432)
        x_tok = at("x_tok", [P, NT, D], F32, o_c)
        mix_hi = at("mix_hi", [P, KC, T], F32R, o_c)
        mix_lo = at("mix_lo", [P, KC, T], F32R, o_c + 18432)
        w_raw = at("w_raw", [P, 2, KC * GW], F32, o_ring)
        w_hi = at("w_hi", [P, 2, KC * GW], F32R, o_ring + 16384)
        w_lo = at("w_lo", [P, 2, KC * GW], F32R, o_ring + 32768)
        q_t = at("q_t", [P, NPAIR_H, T], F32, o_b)
        merged_hi = at("merged_hi", [P, KC, T], F32R, o_b)
        convraw = at("convraw", [16, D], F32, o_d)
        cwraw = at("cwraw", [24, P], F32, o_d + 4096)
        gate_a = at("gate_a", [P, KC, T], F32, o_d)
        merged_lo = at("merged_lo", [P, KC, T], F32R, o_d)
        k_t = at("k_t", [P, WIN + T], F32, o_e)
        v_tok = at("v_tok", [P, 1 + NT, P], F32, o_e + 2816)
        v_t = at("v_t", [P, T], F32, o_e + 5888)
        k_tok = at("k_tok", [P, 2, P], F32, o_e + 5888)
        mask_p = at("mask_p", [P, 2, 2 * P], F32, o_f)
        mask_s = at("mask_s", [P, NB_S, KEYS_S], F32, o_f + 2048)
        cache_k = at("cache_k", [P, NB_S, P], F32, o_f + 8192)
        s_s = at("s_s", [P, NB_S, KEYS_S], F32, o_f + 8192)
        cache_v = at("cache_v", [P, NB_S, P], F32, o_f + 14336)
        o_h = o_f + 18432
        q_blk = [at(f"q_blk{i}", [P, NPAIR_H, P], F32, o_h + 4096 * i) for i in range(2)]
        q_smp = at("q_smp", [P, NB_S, HD], F32, o_h)
        cache_kt = at("cache_kt", [P, NB_S, P], F32, o_h + 4096)
        v_blk = [at(f"v_blk{i}", [P, 2, P], F32, o_h + 8192 + 1024 * i) for i in range(2)]
        k_blk = [at(f"k_blk{i}", [P, 2 * P], F32, o_f + 2048 + 1024 * i) for i in range(2)]
        mask_0 = at("mask_0", [P, 2 * P], F32, o_f + 4096)
        s_p = [at(f"s_p{i}", [P, 2, 2 * P], F32, o_h + 10240 + 2048 * i) for i in range(2)]
        p_t = at("p_t", [P, 2, 2, 4, P], F32, o_h + 14336)
        ps_t = at("ps_t", [P, NB_S, P], F32, o_h + 14336)
        psn_t = at("psn_t", [NS, NB_S, P], F32, o_h + 18432)
        cc_t = at("cc_t", [P, 2, T], F32, o_f)
        u_ext = [at(f"u_ext{i}", [P, 594], F32, o_f + 4608 + 2400 * i) for i in range(2)]
        y_cv = [at(f"y_cv{i}", [P, 594], F32, o_f + 9408 + 2400 * i) for i in range(2)]
        prod = [at(f"prod{i}", [P, T], F32, o_f + 14208 + 2304 * i) for i in range(2)]
        sig_c = at("sig_c", [P, 2, T], F32, o_f)
        cn_tok = at("cn_tok", [18, D], F32, o_h + 4096)

        small = [o_h + 22528]

        def sm(name, shape, dt):
            size = {F32: 4, I32: 4, U32: 4, F32R: 4, BF16: 2}[dt] * int(np.prod(shape[1:]))
            t = at(name, shape, dt, small[0])
            small[0] += (size + 31) // 32 * 32
            return t

        ident = sm("ident", [P, P], F32)
        sink16 = sm("sink16", [P, 16], F32)
        nsink16 = sm("nsink16", [P, 16], F32)
        sel16 = sm("sel16", [P, 16], F32)
        sink_s = sm("sink_s", [P, 1], F32)
        nsink_s = sm("nsink_s", [P, 1], F32)
        cw = sm("cw", [P, 24], F32)
        o_stats = small[0]
        cst = sm("cst", [P, KC, 16], F32)
        cnew = sm("cnew", [P, KC, 18], F32)
        mx = sm("mx", [P, 2, 2], F32)
        nm = sm("nm", [P, 2, 2], F32)
        ds = sm("ds", [P, 2, 2], F32)
        es = sm("es", [P, 2, 2], F32)
        sm_p = sm("sm_p", [P, 2, 2], F32)
        rc = sm("rc", [P, 2, 2], F32)
        mx_s = sm("mx_s", [P, NB_S], F32)
        nm_s = sm("nm_s", [P, NB_S], F32)
        es_s = sm("es_s", [P, NB_S], F32)
        sum_s = sm("sum_s", [P, NB_S], F32)
        eps = sm("eps", [P, 1], F32)
        mv = sm("mv", [P, NT, 2], F32)
        rstd = sm("rstd", [P, NT], F32)
        wj = sm("wj", [P, NT * TOPK], F32)
        tabx = sm("tabx", [P, MAXPASS], U32)
        tabs = sm("tabs", [P, MAXPASS], U32)
        tabw = sm("tabw", [P, MAXPASS], F32)
        n_pass = sm("n_pass", [1, NPE], I32)
        cum_pass = sm("cum_pass", [1, NPE], I32)
        half_all = sm("half_all", [1, 1], I32)
        stats = at("stats", [P, NT, 4, 6], F32, o_stats)

        proj = ctx.enter_context(nc.psum_tensor("proj", [P, 4, 512], F32))
        att = ctx.enter_context(nc.psum_tensor("att", [P, 4, 512], F32))

        def slot(i):
            return proj[:, 2 * i:2 * i + 2, 0:HALF]

        ld_x, ld_c1, ld_sink, ld_conv, ld_ck, ld_cv = (sem(n) for n in (
            "ld_x", "ld_c1", "ld_sink", "ld_conv", "ld_ck", "ld_cv"))
        w_dma = [sem(f"w_dma{i}") for i in range(2)]
        hi_done = sem("hi_done")
        w_ready = sem("w_ready")
        mm_ready = [sem(f"mm_ready{i}") for i in range(2)]
        mm_free = [sem(f"mm_free{i}") for i in range(2)]
        zeroed = sem("zeroed")
        tr_x, x_hi, x_lo = sem("tr_x"), sem("x_hi"), sem("x_lo")
        tr_conv, conv_ready = sem("tr_conv"), sem("conv_ready")
        tr_kv, kv_tok_ready, ckt_ready = sem("tr_kv"), sem("kv_tok_ready"), sem("ckt_ready")
        qs_ready = sem("qs_ready")
        sl_ready, sl_read, s_sub, s_exp, s_prob = (sem(n) for n in (
            "sl_ready", "sl_read", "s_sub", "s_exp", "s_prob"))
        s_tr, s_trc, s_pv, s_oh, s_ol = (sem(n) for n in ("s_tr", "s_trc", "s_pv", "s_oh", "s_ol"))
        blk_ready = sem("blk_ready")
        lg_ready, lg_read = sem("lg_ready"), sem("lg_read")
        nm_ready, e_ready, p_ready = sem("nm_ready"), sem("e_ready"), sem("p_ready")
        pt_ready, pt_read = sem("pt_ready"), sem("pt_read")
        pv_ready, o_hi, o_lo = sem("pv_ready"), sem("o_hi"), sem("o_lo")
        sga = sem("sga")
        u_done, pr_ready, cv_hi, cv_lo = sem("u_done"), sem("pr_ready"), sem("cv_hi"), sem("cv_lo")
        mg_ready, mg_hi, mg_lo = sem("mg_ready"), sem("mg_hi"), sem("mg_lo")
        cn_tr, cn_out = sem("cn_tr"), sem("cn_out")
        st_out, win_out = sem("st_out"), sem("win_out")

        res = at("res", [P, NT, D], F32, o_a)
        p_tok = at("p_tok", [P, NT, PLE], F32, o_a + 20480)
        pt_hi = at("pt_hi", [P, 2, T], F32R, o_a + 25600)
        pt_lo = at("pt_lo", [P, 2, T], F32R, o_a + 30208)
        hs_f = at("hs_f", [P, 2, T], F32, o_a + 25600)
        rw_hi = at("rw_hi", [P, KC, NE], F32R, o_a + 30208)
        rw_lo = at("rw_lo", [P, KC, NE], F32R, o_a + 32256)
        rw_raw = at("rw_raw", [P, KC, NE], F32, o_a + 34816)
        sig_g = at("sig_g", [P, 2, GW], F32, o_a + 34816)
        xt_hi = at("xt_hi", [P, KC, T], F32R, o_c)
        xt_lo = at("xt_lo", [P, KC, T], F32R, o_c + 18432)
        sdo = at("sdo", [P, NT, D], F32, o_b + 20480)
        cc2 = at("cc2", [P, C2_W], F32, o_b + 40960)
        g1b1 = at("g1b1", [P, 2, D], F32, 172032)
        hs_hi = at("hs_hi", [P, 2, T], F32R, 172032)
        hs_lo = at("hs_lo", [P, 2, T], F32R, 176640)
        tri, ones = cc2[:, 0:P], cc2[:, P:2 * P]
        iota64, iota128 = cc2[:, 2 * P:2 * P + 64], cc2[:, 2 * P + 64:3 * P + 64]
        iota_pass = cc2[:, 3 * P + 64:3 * P + 64 + MAXPASS]
        side, val = cc2[:, 3 * P + 64 + MAXPASS:3 * P + 128 + MAXPASS], cc2[:, 3 * P + 128 + MAXPASS:C2_W - 1]
        sum_row = cc2[:, C2_W - 1:C2_W]
        NTK = NT * TOPK
        TAB_RING = 10
        hot = at("hot", [P, NTK, NE], F32, 181248)
        sig0 = at("sig0", [P, NT, GW], F32, 188928)
        tab_a = at("tab_a", [P, TAB_RING, P], F32, 194048)
        tab_b = at("tab_b", [P, TAB_RING, 2, MAXPASS], F32, 199168)
        zero_rows = at("zero_rows", [P, D], F32, 194560)
        rt_small = [o_b]

        def rsm(name, shape, dt, pool=rt_small):
            size = {F32: 4, I32: 4, U32: 4, BF16: 2}[dt] * int(np.prod(shape[1:]))
            t = at(name, shape, dt, pool[0])
            pool[0] += (size + 31) // 32 * 32
            return t

        picked = rsm("picked", [P, NTK, NE], F32)
        scores = rsm("scores", [P, NT, NE], F32)
        biased = rsm("biased", [P, NT, NE], F32)
        slot_map = rsm("slot_map", [P, NT, NE], F32)
        rank_i = rsm("rank_i", [P, NT, NE], I32)
        col_map = rsm("col_map", [P, NT, NE], F32)
        rbias = at("rbias", [P, NE], F32, 208640)
        best8 = rsm("best8", [P, NT * NGRP, 8], F32)
        ghot = rsm("ghot", [P, NT, TOPG, NGRP], F32)
        sel = rsm("sel", [P, NT, NE], BF16)
        gsum = rsm("gsum", [P, NT, NGRP], F32)
        gbest = rsm("gbest", [P, NT, 8], F32)
        gidx = rsm("gidx", [P, NT, 8], U32)
        gidx_f = rsm("gidx_f", [P, NT, TOPG], F32)
        gmask = rsm("gmask", [P, NT, NGRP], F32)
        ebest = rsm("ebest", [P, NT, 8], F32)
        eidx = rsm("eidx", [P, NT, 8], U32)
        eidx_f = rsm("eidx_f", [P, NT, TOPK], F32)
        xg = at("xg", [P, P, KC], F32, 172032)
        xt = at("xt", [P, KC, P], F32, 176128)
        ysb = [at(f"ysb{i}", [P, D], F32, 180224 + 4096 * i) for i in range(2)]
        sg, g_e, h_e = (at(n, [P, FF], F32, 194560 + 1024 * i) for i, n in enumerate(("sg", "g_e", "h_e")))
        ht_e = at("ht_e", [P, 2, P], F32, 197632)
        w_exp = [at(f"w_exp{i}", [P, 2, 3 * KC * FF], F32, o) for i, o in enumerate((o_ring, o_b))]
        y_all = at("y_all", [P, NT, 2, D], F32, o_b)
        pp_hi = at("pp_hi", [P, 2 * D], F32R, o_b + 40960)
        pp_lo = at("pp_lo", [P, 2 * D], F32R, 172032)
        g2b2 = at("g2b2", [P, 2, D], F32, 200704)
        tri_b = rsm("tri_b", [P, P], BF16)
        ones_b = rsm("ones_b", [P, P], BF16)
        base64 = rsm("base64", [P, NPE], F32)
        nmax = rsm("nmax", [P, NPE], F32)
        npass_i = rsm("npass_i", [P, NPE], I32)
        npass_f = rsm("npass_f", [P, NPE], F32)
        cums = [rsm(f"cums{i}", [P, NPE], F32) for i in range(2)]
        assert rt_small[0] <= o_b + 20480
        slot_j, col_j = (at(n, [P, NTK], F32, o_a + 34816 + 128 * i)
                                 for i, n in enumerate(("slot_j", "col_j")))
        ssum = at("ssum", [P, NT], F32, o_a + 34816 + 384)
        tab_f, tab_e = (at(n, [P, MAXPASS], F32, o_a + 34816 + 416 + 384 * i) for i, n in enumerate(("tab_f", "tab_e")))
        tab_i, tab_s = (at(n, [P, MAXPASS], I32, o_a + 34816 + 1184 + 384 * i) for i, n in enumerate(("tab_i", "tab_s")))
        gidx_col = [at(f"gidx_col{i}", [P, 1], U32, o_h + 22528 + 512 + 32 * i) for i in range(2)]
        sidx_col = [at(f"sidx_col{i}", [P, 1], U32, o_h + 22528 + 576 + 32 * i) for i in range(2)]

        x2_d = nc.dram_tensor("x2_rows", [T, D], F32)
        acc_d = nc.dram_tensor("expert_sums", [2 * T, D], F32)

        def tile_bank(t):
            return proj[:, t, :] if t < 4 else att[:, 0, :]

        def sd_bank(n):
            return proj[:, 2 + n % 4, :] if n % 4 < 2 else att[:, n % 4 - 2, :]

        def g0_bank(t):
            return proj[:, 2 + t, :] if t < 2 else att[:, t - 2, :]

        def p_bank(c):
            return (proj if c == 0 else att)[:, 0:2, :].rearrange("p a n -> p (a n)")[:, 0:T]
        ld_p, ld_res, ld_rt, ld_ln1, ld_ln2 = (sem(n) for n in ("ld_p", "ld_res", "ld_rt", "ld_ln1", "ld_ln2"))
        passed = [sem(f"passed{i}") for i in range(5)]
        wo_ready, wo_read = sem("wo_ready"), sem("wo_read")
        p_tr, p_hi, p_lo, rows_done, y_comb = (sem(n) for n in ("p_tr", "p_hi", "p_lo", "rows_done", "y_comb"))
        std_ready, var_ready, x2_ready, x2_out = (sem(n) for n in ("std_ready", "var_ready", "x2_ready", "x2_out"))
        x2_tr, x2_hi, x2_lo, rw_h, rw_ready = (sem(n) for n in ("x2_tr", "x2_hi", "x2_lo", "rw_h", "rw_ready"))
        sg_used, g0_ready, g0_read = sem("sg_used"), sem("g0_ready"), sem("g0_read")
        rt_ready, sc_ready, sel_ready, rank_ready, rank_read = (sem(n) for n in (
            "rt_ready", "sc_ready", "sel_ready", "rank_ready", "rank_read"))
        su_ready, ss_ready, hs_ready, hs_hd, hs_ld = (sem(n) for n in ("su_ready", "ss_ready", "hs_ready", "hs_hd", "hs_ld"))
        pg_ready, pg_sig, pg_read = sem("pg_ready"), sem("pg_sig"), sem("pg_read")
        tb_ready, tb_used, routed, res_done = (sem(n) for n in ("tb_ready", "tb_used", "routed", "res_done"))
        sd_ready, sd_read = sem("sd_ready"), sem("sd_read")
        x_zero, gathered, scattered, idx_ready = (sem(n) for n in ("x_zero", "gathered", "scattered", "idx_ready"))
        w_exp_in = [sem(f"w_exp_in{i}") for i in range(3)]
        xtr, xt_a, xt_d = sem("xtr"), sem("xt_a"), sem("xt_d")
        gu_ready, sg_ready, h_ready, htr, ht_ready = (sem(n) for n in ("gu_ready", "sg_ready", "h_ready", "htr", "ht_ready"))
        xt_last = sem("xt_last")
        y_mm, y_a, y_dv = sem("y_mm"), sem("y_a"), sem("y_dv")
        ld_y = sem("ld_y")
        acc_zero, zero_ready, y_free = sem("acc_zero"), sem("zero_ready"), sem("y_free")
        y_done, y_out = sem("y_done"), sem("y_out")

        block = ctx.enter_context(nc.Block())

        xp = x_prompt[0].rearrange("(t p) n -> p t n", p=P)
        xs = x_sample.rearrange("b s n -> (b s) n")
        QUADS = [(t, c) for t in range(NT) for c in range(2)]
        CHUNKS_AT = [(2, 0), (2, 0), (1, 0), (1, 1), (1, 0), (1, 1), (1, 0), (1, 1), (2, 0), (1, 0)]

        def ntok(t):
            return P if t < NT - 1 else NS

        def two(ap):
            return ap.rearrange("p (a n) -> p a n", a=2)

        def row(t, m):
            return t[:, bass.ds(m, 1), :].rearrange("p o n -> p (o n)")

        def halves(g):
            for i in range(2):
                raw, hi, lo = (t[:, g.par, :].rearrange("p (c x n) -> p c x n", c=KC, x=4) for t in (w_raw, w_hi, w_lo))
                yield raw[:, :, i:4:2, :], hi[:, :, 2 * i:2 * i + 2, :], lo[:, :, 2 * i:2 * i + 2, :]

        def split_hi(act, g, used=None, count=None):
            act.wait_ge(w_dma[g.par], (g.half + 1) * 32)
            if used is not None:
                act.wait_ge(used, count)
            elif g.base >= 2:
                act.wait_ge(mm_ready[1], g.v - 1)
            if G_Q <= g.base < G_GA:
                for raw, hi, _ in halves(g):
                    last = nc.scalar.activation(hi, raw, ACT.Copy)
                last.then_inc(hi_done, 1)
            else:
                nc.scalar.activation(w_hi[:, g.par, :], w_raw[:, g.par, :], ACT.Copy).then_inc(hi_done, 1)

        def split_lo(dve, g):
            dve.wait_ge(hi_done, g.v + 1)
            if G_Q <= g.base < G_GA:
                for raw, hi, lo in halves(g):
                    last = nc.vector.tensor_tensor(lo, raw, hi.bitcast(F32), ALU.subtract)
                last.then_inc(w_ready, 1)
            else:
                nc.vector.tensor_tensor(w_lo[:, g.par, :], w_raw[:, g.par, :], w_hi[:, g.par, :].bitcast(F32),
                                        ALU.subtract).then_inc(w_ready, 1)

        def past(e, i):
            e.sem_inc(passed[i], 1)

        def pass_counts(e, p, prev=None):
            return e.value_load(n_pass[0:1, bass.ds(p, 1)], min_val=1, max_val=T // SLOT)

        def half_passes(e):
            return e.value_load(half_all[0:1, 0:1], min_val=NPE // 2, max_val=MAXPASS // 2 - 1)

        @block.sync
        def _(sp):
            def load(g, w, c0):
                src = w[0].rearrange("(c p) n -> p c n", p=P)[:, :, bass.ds(c0, GW)]
                if g.base >= 2:
                    sp.wait_ge(w_ready, g.v - 1)
                    if not isinstance(g.v, int):
                        past(nc.sync, 4)
                sp.dma_start(w_raw[:, g.par, :].rearrange("p (c n) -> p c n", c=KC),
                             src).then_inc(w_dma[g.par], 32)

            load(Step(0), w_in, COL_K)
            wq = w_in[0][:, 0:Q_W].rearrange("(c p) (h n) -> p c h n", p=P, h=2)
            for j in range(4):
                g = Step(G_Q + j)
                if j:
                    sp.wait_ge(w_ready, g.v - 1)
                for e in range(2):
                    sp.dma_start(w_raw[:, g.par, :].rearrange("p (c h n) -> p c h n", c=KC, h=2)[:, :, e, :],
                                 wq[:, :, e, j * P:(j + 1) * P]).then_inc(w_dma[g.par], 16)
            with sp.Fori(0, 2) as it:
                for i in range(2):
                    load(Step(G_GA + i, it, 2), w_in, it * 2 * GW + COL_GA + i * GW)
            wao = w_ao[0].rearrange("(g m p) n -> g p m n", g=2, p=HD)
            with sp.Fori(0, 2) as it:
                for i in range(2):
                    g = Step(G_AO + i, it, 2)
                    sp.wait_ge(w_ready, g.v - 1)
                    past(nc.sync, 4)
                    for e in range(2):
                        sp.dma_start(w_raw[e * HD:(e + 1) * HD, g.par, :].rearrange("p (c n) -> p c n", c=KC),
                                     wao[e][:, :, bass.ds(it * 2 * GW + i * GW, GW)]).then_inc(w_dma[g.par], 16)
            with sp.Fori(0, 2) as it:
                for i in range(6):
                    c0 = (COL_CC, COL_CH, COL_CB)[i % 3] + i // 3 * GW
                    load(Step(G_C + i, it, 6), w_in, it * 2 * GW + c0)
            with sp.Fori(0, 4) as it:
                load(Step(G_GC, it, 2), w_in, it * GW + COL_GC)
                load(Step(G_GC + 1, it, 2), w_co, it * GW)
            load(Step(G_WO), w_o, 0)
            for j in range(1, 4):
                load(Step(G_WO + j), w_o, j * GW)
            wide = lambda w: w[0].rearrange("(c p) n -> p c n", p=P)
            def load_wide(g, w):
                sp.wait_ge(w_ready, g.v - 1)
                sp.dma_start(w_raw[:, g.par, :].rearrange("p (c n) -> p c n", c=2), wide(w)).then_inc(w_dma[g.par], 32)
            load(Step(G_SG), w_sg, 0)
            load(Step(G_SU), w_su, 0)
            load(Step(G_P0), w_pg, 0)
            load_wide(Step(G_SD), w_sd)

            def load_part(p, i, n, first=False):
                k, e = ((0, 0), (1, 0), (0, 1), (1, 1), (2, 0), (2, 1))[n]
                w, c = ((w_eg, KC), (w_eu, KC), (w_ed, 2))[k]
                if not (first and n < 3):
                    sp.wait_ge(w_exp_in[n % 3], p * 32 + 16 * (n // 3))
                    if not isinstance(p, int):
                        past(nc.sync, 4)
                src = w[0][bass.ds(p * 2 + e, 1)].rearrange("o (r c) n -> r (o c n)", c=c)
                sp.dma_start(w_exp[i][:, e, k * KC * FF:(k + 1) * KC * FF], src).then_inc(w_exp_in[n % 3], 16)

            sp.wait_ge(w_ready, G_P0 + 1)
            load_part(0, 0, 1, first=True)
            sp.wait_ge(w_ready, G_SD + 1)
            load_part(0, 0, 0, first=True)
            sp.wait_ge(g0_ready, NT)
            load_part(0, 0, 2, first=True)
            load_part(0, 0, 5, first=True)
            sp.wait_ge(sd_ready, 2 * NT)
            load_part(0, 0, 3, first=True)
            load_part(0, 0, 4, first=True)
            sp.wait_ge(res_done, 1)
            sp.wait_ge(routed, 1)
            for n in range(6):
                load_part(1, 1, n)
            with sp.Fori(0, NPE // 2 - 1) as it:
                for i in range(2):
                    done = sp.value_load(cum_pass[0:1, bass.ds(it * 2 + i, 1)], min_val=1, max_val=MAXPASS - 1)
                    sp.wait_ge(gu_ready, done)
                    past(nc.sync, 4)
                    for n in range(4):
                        load_part(it * 2 + (2 + i), i, n)
                    sp.wait_ge(y_mm, done)
                    past(nc.sync, 4)
                    for n in range(4, 6):
                        load_part(it * 2 + (2 + i), i, n)
            done = sp.value_load(cum_pass[0:1, NPE - 2:NPE - 1], min_val=1, max_val=MAXPASS - 1)
            sp.wait_ge(y_mm, done)
            past(nc.sync, 4)
            load_wide(Step(G_PP), w_pp)
            load(Step(G_PG), w_pg, GW)
            k_half = half_passes(sp)
            sp.wait_ge(scattered, k_half * 32 + 32)
            past(nc.sync, 4)
            for i in range(2):
                sp.dma_start(y_all[:, 0:NT - 1, i, :], acc_d[i * T:i * T + SEQ, :].rearrange("(t p) n -> p t n", p=P)).then_inc(ld_y, 16)
                sp.dma_start(y_all[0:NS, NT - 1, i, :], acc_d[i * T + SEQ:(i + 1) * T, :]).then_inc(ld_y, 16)
            for t in range(NT):
                w = ntok(t)
                sp.wait_ge(y_done, t + 1)
                dst = y_prompt[0, t * P:(t + 1) * P] if t < NT - 1 else y_sample.rearrange("b s n -> (b s) n")
                sp.dma_start(dst, res[0:w, t, :]).then_inc(y_out, 16)
            sp.wait_ge(y_out, NT * 16)

        @block.gpsimd
        def _(pool):
            nc.gpsimd.memset(k_t[:, 0:WIN], 0.0).then_inc(zeroed, 1)
            nc.gpsimd.memset(v_tok[:, 0, :], 0.0).then_inc(zeroed, 1)
            pool.wait_ge(kv_tok_ready, 1)
            pool.dma_start(nk_p[0, 0].rearrange("w g d -> w (g d)"), k_tok[:, 0, :]).then_inc(st_out, 16)
            pool.dma_start(nv_p[0, 0].rearrange("w g d -> w (g d)"), v_tok[:, NT - 1, :]).then_inc(st_out, 16)
            for b in range(NB_S):
                pool.dma_start(nk_s[0, b, WIN - S_S:WIN].rearrange("w g d -> w (g d)"),
                               k_tok[b * S_S:(b + 1) * S_S, 1, :]).then_inc(st_out, 16)
                pool.dma_start(nv_s[0, b, WIN - S_S:WIN].rearrange("w g d -> w (g d)"),
                               v_tok[b * S_S:(b + 1) * S_S, NT, :]).then_inc(st_out, 16)
            pool.wait_ge(cn_out, 1)
            pool.dma_start(nconv_p[0, 0], cn_tok[0:2, :]).then_inc(st_out, 16)
            pool.dma_start(nconv_s[0].rearrange("b j n -> (b j) n"), cn_tok[2:18, :]).then_inc(st_out, 16)
            pool.wait_ge(mm_ready[1], G_WO)
            nc.gpsimd.memset(zero_rows[:, :], 0.0).then_inc(zero_ready, 1)
            pool.wait_ge(zero_ready, 1)
            for i in range(2):
                pool.dma_start(acc_d[i * T:i * T + SEQ, :].rearrange("(t p) n -> p t n", p=P),
                               zero_rows[:, :].unsqueeze(1).to_broadcast([P, NT - 1, D])).then_inc(acc_zero, 16)
                pool.dma_start(acc_d[i * T + SEQ:(i + 1) * T, :], zero_rows[0:NS, :]).then_inc(acc_zero, 16)
            for g in (G_SU, G_P0):
                pool.wait_ge(w_ready, g)
                pool.wait_ge(hi_done, g + 1)
                nc.gpsimd.tensor_tensor(w_lo[:, g % 2, :], w_raw[:, g % 2, :], w_hi[:, g % 2, :].bitcast(F32),
                                        ALU.subtract).then_inc(w_ready, 1)
            pool.wait_ge(sd_ready, 2 * NT)
            nc.gpsimd.memset(xg[:, :, :], 0.0).then_inc(x_zero, 1)
            pool.wait_ge(routed, 1)
            pool.wait_ge(x2_out, 16 * NT)
            pool.wait_ge(x_zero, 1)

            def gather(k, i, n):
                nc.gpsimd.tensor_copy(gidx_col[i][:, :], tabx[:, bass.ds(k, 1)]).then_inc(idx_ready, 1)
                pool.wait_ge(idx_ready, n)
                past(nc.gpsimd, 3)
                pool.indirect_dma_start(out=xg[:, :, :].rearrange("p q c -> p (q c)"), out_offset=None, in_=x2_d[:, :],
                                        in_offset=bass.IndirectOffsetOnAxis(ap=gidx_col[i][:, 0:1], axis=0),
                                        bounds_check=T - 1, oob_is_err=False).then_inc(gathered, 16)

            gather(0, 0, 1)
            pool.dma_start(g2b2[:, 0, :], ln2_g[0].partition_broadcast(P)).then_inc(scattered, 16)
            pool.dma_start(g2b2[:, 1, :], ln2_b[0].partition_broadcast(P)).then_inc(scattered, 16)
            pool.wait_ge(xtr, 1)
            gather(1, 1, 2)
            pool.wait_ge(acc_zero, 64)
            k_half = half_passes(pool)
            with pool.Fori(0, k_half) as it:
                for i in range(2):
                    k = it * 2 + i
                    pool.wait_ge(xtr, k + 2)
                    past(nc.gpsimd, 3)
                    gather(k + 2, i, k * 2 + 3)
                    nc.gpsimd.tensor_copy(sidx_col[i][:, :], tabs[:, bass.ds(k, 1)]).then_inc(idx_ready, 1)
                    pool.wait_ge(scattered, k * 16 + 32)
                    past(nc.gpsimd, 3)
                    nc.gpsimd.sem_inc(y_free, 1)
                    pool.wait_ge(idx_ready, k * 2 + 4)
                    pool.wait_ge(y_a, k + 2)
                    pool.wait_ge(y_dv, k + 2)
                    past(nc.gpsimd, 3)
                    pool.indirect_dma_start(out=acc_d[:, :], out_offset=bass.IndirectOffsetOnAxis(ap=sidx_col[i][:, 0:1], axis=0),
                                            in_=ysb[i][:, :], in_offset=None, bounds_check=2 * T - 1, oob_is_err=False,
                                            compute_op=ALU.add).then_inc(scattered, 16)
            pool.wait_ge(gathered, k_half * 32 + 32)
            past(nc.gpsimd, 3)
            nc.gpsimd.sem_inc(rows_done, 1)
            pool.wait_ge(scattered, k_half * 32 + 32)
            past(nc.gpsimd, 3)
            for g in range(G_PG + 1, N_GROUPS_W):
                pool.wait_ge(w_ready, g)
                pool.wait_ge(hi_done, g + 1)
                nc.gpsimd.tensor_tensor(w_lo[:, g % 2, :], w_raw[:, g % 2, :], w_hi[:, g % 2, :].bitcast(F32),
                                        ALU.subtract).then_inc(w_ready, 1)
            pool.wait_ge(st_out, (2 + 2 * NB_S + 2) * 16)
            pool.wait_ge(win_out, 32)

        @block.scalar
        def _(act):
            act.dma_start(ident[:, :], const1[:, 0:P]).then_inc(ld_x, 16)
            act.dma_start(x_tok[:, 0:NT - 1, :], xp).then_inc(ld_x, 16)
            act.dma_start(x_tok[0:NS, NT - 1, :], xs).then_inc(ld_x, 16)
            act.dma_start(convraw[:, :], conv_state[0].rearrange("b j n -> (b j) n")).then_inc(ld_conv, 16)
            act.dma_start(cwraw[:, :], conv_w[0].rearrange("j (c p) -> (j c) p", p=P)).then_inc(ld_conv, 16)
            act.dma_start(mask_p[:, :, :].rearrange("p a b -> p (a b)"), const1[:, P:5 * P]).then_inc(ld_c1, 16)
            act.dma_start(mask_s[:, :, :].rearrange("p a b -> p (a b)"),
                          const1[:, 5 * P:5 * P + NB_S * KEYS_S]).then_inc(ld_c1, 16)
            act.dma_start(sel16[:, :], const1[:, C1_W - 16:C1_W]).then_inc(ld_sink, 16)
            act.dma_start(sink16[:, :], sinks[0].partition_broadcast(P)).then_inc(ld_sink, 16)
            act.dma_start(cache_k[:, :, :], win_k[0].rearrange("b w g d -> w b (g d)")).then_inc(ld_ck, 16)
            act.dma_start(cache_v[:, :, :], win_v[0].rearrange("b w g d -> w b (g d)")).then_inc(ld_cv, 16)
            act.dma_start(nk_s[0][:, 0:WIN - S_S].rearrange("b w g d -> b (w g d)"),
                          win_k[0][:, S_S:WIN].rearrange("b w g d -> b (w g d)")).then_inc(win_out, 16)
            act.dma_start(nv_s[0][:, 0:WIN - S_S].rearrange("b w g d -> b (w g d)"),
                          win_v[0][:, S_S:WIN].rearrange("b w g d -> b (w g d)")).then_inc(win_out, 16)
            for n, (t, c) in enumerate(QUADS):
                act.wait_ge(tr_x, n + 1)
                w = ntok(t)
                nc.scalar.activation(h_hi[:, 4 * c:4 * c + 4, t * P:t * P + w],
                                     att[:, n % 4, :].rearrange("p (c n) -> p c n", c=4)[:, :, 0:w],
                                     ACT.Copy).then_inc(x_hi, 1)
            split_hi(act, Step(0))
            split_hi(act, Step(1))
            act.wait_ge(mm_ready[0], 1)
            nc.scalar.activation(two(k_t[:, WIN:]), slot(0), ACT.Copy).then_inc(mm_free[0], 1)
            for j in range(4):
                split_hi(act, Step(G_Q + 1 + j))
                act.wait_ge(mm_ready[0], j + 2)
                nc.scalar.activation(two(q_t[:, 2 * j, :]), slot(0), ACT.Copy, scale=HD ** -0.5).then_inc(mm_free[0], 1)
                if j == 0:
                    act.wait_ge(tr_kv, 1)
                    nc.scalar.activation(cache_kt[:, :, :].rearrange("p (a b) n -> p a (b n)", a=2), att[:, 2:4, :],
                                         ACT.Copy).then_inc(ckt_ready, 1)
            act.wait_ge(s_sub, 1)
            nc.scalar.activation(s_s[:, :, :], s_s[:, :, :], ACT.Exp)
            nc.scalar.activation(es_s[:, :], nm_s[:, :], ACT.Exp, bias=sink_s[:, :]).then_inc(s_exp, 1)

            with act.Fori(0, 2) as it:
                for h in range(2):
                    u0, b0, blk = it * 16 + h * 8, it * 4 + h * 2, it * 2 + h
                    for s in range(10):
                        if s < 8:
                            r = s % 2
                            act.wait_ge(nm_ready, u0 + s + 1)
                            for e in range(2):
                                nc.scalar.activation(s_p[r][:, e, :], s_p[r][:, e, :], ACT.Exp,
                                                     bias=nm[:, r, e:e + 1], accum_out=sm_p[:, r, e:e + 1])
                            nc.scalar.activation(es[:, r, :], ds[:, r, :], ACT.Exp).then_inc(e_ready, 1)
                        if s >= 2:
                            m = s - 2
                            if m % 4 == 0:
                                act.wait_ge(pv_ready, b0 + m // 4 + 1)
                            act.wait_ge(pt_ready, u0 + m + 3)
                            nc.scalar.activation(p_t[:, :, :, m % 4, :],
                                                 att[:, 2, :].rearrange("p (g c q) -> p c g q", g=2, c=2),
                                                 ACT.Copy).then_inc(pt_read, 1)
                        if s == 4:
                            split_hi(act, Step(G_GA + h + 1, it, 2))
                        if s == 7 or s == 9:
                            mb = (s - 7) // 2
                            act.wait_ge(pv_ready, b0 + mb + 2)
                            nc.scalar.activation(mix_hi[:, 4 * mb:4 * mb + 4, bass.ds(blk * P, P)],
                                                 att[:, 3, :].rearrange("p (m q) -> p m q", m=4),
                                                 ACT.Copy).then_inc(o_hi, 1)
                    act.wait_ge(mm_ready[1], it * 2 + h + G_GA + 1)
                    nc.scalar.activation(two(row(gate_a, it * 4 + 2 * h + 1)), slot(1), ACT.Copy).then_inc(mm_free[1], 1)
            act.wait_ge(s_tr, 1)
            nc.scalar.activation(ps_t[:, :, :].rearrange("p (a b) n -> p a (b n)", a=2), att[:, 0:2, :],
                                 ACT.Copy).then_inc(s_trc, 1)
            act.wait_ge(s_pv, 1)
            nc.scalar.activation(mix_hi[:, :, SEQ:T].rearrange("p m (b s) -> p b m s", b=NB_S),
                                 att[:, 0, :].rearrange("p (b m s) -> p b m s", b=NB_S, m=8),
                                 ACT.Copy).then_inc(s_oh, 1)
            with act.Fori(0, 2) as it:
                for h in range(2):
                    act.wait_ge(mm_free[0], it * 2 + h + G_GA + 1)
                    act.wait_ge(mm_free[1], it * 2 + h + G_GA + 1)
                    nc.scalar.activation(gate_a[:, bass.ds(it * 4 + 2 * h, 2), :],
                                         gate_a[:, bass.ds(it * 4 + 2 * h, 2), :], ACT.Sigmoid).then_inc(sga, 1)
                    split_hi(act, Step(G_AO + h + 1, it, 2))
            with act.Fori(0, 2) as it:
                for jj in range(2):
                    for k in range(3):
                        gb = G_C + 3 * jj + k
                        split_hi(act, Step(gb + 1, it, 6))
                        for i in range(2):
                            if k == 0:
                                act.wait_ge(mm_ready[i], it * 6 + gb + 1)
                                act.wait_ge(u_done, it * 4 + 2 * jj + 1)
                                nc.scalar.activation(two(cc_t[:, i, :]), slot(i), ACT.Copy).then_inc(mm_free[i], 1)
                            if k == 2:
                                act.wait_ge(pr_ready, it * 4 + 2 * jj + i + 1)
                                act.wait_ge(mm_ready[1], G_AO + 4)
                                nc.scalar.activation(row(mix_hi, it * 4 + 2 * jj + i), prod[i][:, :],
                                                     ACT.Copy).then_inc(cv_hi, 1)
            act.wait_ge(cn_tr, 1)
            nc.scalar.activation(cn_tok[:, :].rearrange("p (a n) -> p a n", a=2), att[0:18, 0:2, :],
                                 ACT.Copy).then_inc(cn_out, 1)
            with act.Fori(0, 4) as it:
                split_hi(act, Step(G_GC + 1, it, 2))
                for i in range(2):
                    act.wait_ge(mm_ready[i], it * 2 + G_GC + 1)
                    act.wait_ge(mg_ready, it * 2 + 1)
                    nc.scalar.activation(two(sig_c[:, i, :]), slot(i), ACT.Sigmoid).then_inc(mm_free[i], 1)
                split_hi(act, Step(G_GC + 2, it, 2))
                for i in range(2):
                    act.wait_ge(mg_ready, it * 2 + 2 + i)
                    nc.scalar.activation(row(merged_hi, it * 2 + i), prod[i][:, :], ACT.Copy).then_inc(mg_hi, 1)
            act.wait_ge(mm_ready[1], G_WO)
            act.wait_ge(mm_ready[0], G_WO)
            act.wait_ge(st_out, (2 + 2 * NB_S + 2) * 16)
            act.dma_start(res[:, 0:NT - 1, :], xp).then_inc(ld_res, 16)
            act.dma_start(res[0:NS, NT - 1, :], xs).then_inc(ld_res, 16)
            act.dma_start(p_tok[:, 0:NT - 1, :], p_prompt[0, 0].rearrange("(t p) n -> p t n", p=P)).then_inc(ld_p, 16)
            act.dma_start(p_tok[0:NS, NT - 1, :], p_sample[0].rearrange("b s n -> (b s) n")).then_inc(ld_p, 16)
            act.dma_start(g1b1[:, 0, :], ln1_g[0].partition_broadcast(P)).then_inc(ld_ln1, 16)
            act.dma_start(g1b1[:, 1, :], ln1_b[0].partition_broadcast(P)).then_inc(ld_ln1, 16)
            act.dma_start(rw_raw[:, :, :], w_router[0].rearrange("(c p) n -> p c n", p=P)).then_inc(ld_rt, 16)
            act.dma_start(rbias[:, :], router_bias[0].partition_broadcast(P)).then_inc(ld_rt, 16)
            act.dma_start(cc2[:, :], const2).then_inc(ld_rt, 16)
            with act.Fori(0, 2) as it:
                for h in range(2):
                    split_hi(act, Step(G_WO + h + 1, it, 2), wo_ready, (it * 2 + h) * NT + 1)
            act.wait_ge(ld_rt, 48)
            nc.scalar.activation(rw_hi[:, :, :], rw_raw[:, :, :], ACT.Copy).then_inc(rw_h, 1)

            def root(t):
                w = ntok(t)
                nc.scalar.activation(rstd[0:w, t:t + 1], mv[0:w, t, 1:2], ACT.Sqrt, bias=eps[0:w, :]).then_inc(std_ready, 1)

            for t in range(NT + 2):
                if t < NT:
                    act.wait_ge(var_ready, t + 1)
                    root(t)
                if t == NT - 1:
                    split_hi(act, Step(G_SU), wo_ready, 4 * NT + 1)
                if t >= 2:
                    w = ntok(t - 2)
                    for c in range(2):
                        n = 2 * (t - 2) + c
                        act.wait_ge(x2_tr, n + 1)
                        nc.scalar.activation(xt_hi[:, 4 * c:4 * c + 4, (t - 2) * P:(t - 2) * P + w],
                                             att[:, n % 4, :].rearrange("p (c n) -> p c n", c=4)[:, :, 0:w],
                                             ACT.Copy).then_inc(x2_hi, 1)
                    act.dma_start(x2_d[(t - 2) * P:(t - 2) * P + w, :], res[0:w, t - 2, :]).then_inc(x2_out, 16)
            act.wait_ge(rt_ready, 1)
            logits = att[:, 3, 0:NT * NE].rearrange("p (t n) -> p t n", t=NT)
            nc.scalar.activation(scores[:, 0:NT - 1, :], logits[:, 0:NT - 1, :], ACT.Sigmoid)
            nc.scalar.activation(scores[0:NS, NT - 1, :], logits[0:NS, NT - 1, :], ACT.Sigmoid).then_inc(sc_ready, 1)
            for m in range(2):
                act.wait_ge(su_ready, m + 1)
                nc.scalar.activation(two(hs_f[:, m, :]), (proj, att)[m][:, 0:2, 0:HALF], ACT.Sigmoid).then_inc(ss_ready, 1)
                if m == 0:
                    split_hi(act, Step(G_P0), sg_used, 1)
            split_hi(act, Step(G_SD), su_ready, 2)
            act.wait_ge(hs_ready, 2)
            nc.scalar.activation(hs_hi[:, :, :], hs_f[:, :, :], ACT.Copy).then_inc(hs_hd, 1)
            for t in range(NT):
                w = ntok(t)
                act.wait_ge(g0_ready, t + 1)
                nc.scalar.activation(sig0[0:w, t, :], g0_bank(t)[0:w, 0:GW], ACT.Sigmoid).then_inc(g0_read, 1)
            for n, (t, c) in enumerate(QUADS):
                w = ntok(t)
                act.wait_ge(sd_ready, n + 1)
                nc.scalar.activation(sdo[0:w, t, c * 512:(c + 1) * 512], sd_bank(n)[0:w, :], ACT.Copy).then_inc(sd_read, 1)

            def xt_half(k):
                act.wait_ge(xtr, k + 1)
                nc.scalar.activation(xt[:, 0:4, :].rearrange("p c n -> p (c n)"), proj[:, 0, :], ACT.Copy).then_inc(xt_a, 1)

            xt_half(0)
            act.wait_ge(routed, 1)
            k_half = half_passes(act)
            with act.Fori(0, k_half) as it:
                for i in range(2):
                    k = it * 2 + i
                    act.wait_ge(gu_ready, k + 1)
                    nc.scalar.activation(sg[:, :], att[:, 0, 0:FF], ACT.Sigmoid).then_inc(sg_ready, 1)
                    xt_half(k + 1)
                    act.wait_ge(htr, k + 1)
                    nc.scalar.activation(ht_e[:, :, :].rearrange("p c n -> p (c n)"), att[:, 1, 0:FF], ACT.Copy).then_inc(ht_ready, 1)
                    act.wait_ge(y_mm, k + 1)
                    act.wait_ge(y_free, k + 1)
                    past(nc.scalar, 0)
                    nc.scalar.activation(ysb[i][:, 0:512], proj[:, 2, :], ACT.Copy,
                                         scale=tabw[:, bass.ds(k, 1)]).then_inc(y_a, 1)
            nc.scalar.drain().then_inc(xt_last, 1)
            act.wait_ge(w_dma[G_PP % 2], (G_PP // 2 + 1) * 32)
            nc.scalar.activation(pp_hi[:, :], w_raw[:, G_PP % 2, :], ACT.Copy).then_inc(hi_done, 1)
            split_hi(act, Step(G_PG), sd_ready, 2 * NT)
            act.wait_ge(p_tr, 1)
            for c in range(2):
                last = nc.scalar.activation(pt_hi[:, c, :], p_bank(c), ACT.Copy)
            last.then_inc(p_hi, 1)

            def load_gate(j):
                g = G_PG + j - 1
                act.wait_ge(w_ready, g - 1)
                act.dma_start(w_raw[:, g % 2, :].rearrange("p (c n) -> p c n", c=KC),
                              w_pg[0].rearrange("(c p) n -> p c n", p=P)[:, :, j * GW:(j + 1) * GW]).then_inc(w_dma[g % 2], 32)

            load_gate(2)
            split_hi(act, Step(G_PG + 1), sd_ready, 2 * NT)
            load_gate(3)
            for j in range(1, 4):
                if j == 2:
                    split_hi(act, Step(G_PG + 2), pg_ready, 2 * NT)
                for t in range(NT):
                    w = ntok(t)
                    n = j * NT + t
                    act.wait_ge(pg_ready, n + 1)
                    if n >= NT + 2:
                        act.wait_ge(pg_read, n - 1)
                    nc.scalar.activation(sig_g[0:w, n % 2, :], tile_bank(t)[0:w, 0:GW], ACT.Sigmoid).then_inc(pg_sig, 1)
                    if j == 3 and t >= 1:
                        act.wait_ge(var_ready, NT + t)
                        root(t - 1)
            act.wait_ge(var_ready, 2 * NT)
            root(NT - 1)

        @block.tensor
        def _(pe):
            nc.tensor.sem_inc(lg_read, 1)
            nc.tensor.sem_inc(pt_read, 1)
            nc.tensor.sem_inc(pt_ready, 2)
            nc.tensor.sem_inc(pv_ready, 1)
            nc.tensor.sem_inc(o_lo, 1)
            nc.tensor.sem_inc(u_done, 1)
            nc.tensor.sem_inc(mg_ready, 1)

            def chunk(g, i, c, src_hi, src_lo):
                if c == 0:
                    if i == 0:
                        pe.wait_ge(w_ready, g.v + 1)
                    if g.base >= 1:
                        pe.wait_ge(mm_free[i], g.v)
                for n, (w, x) in enumerate(((w_hi, src_hi), (w_hi, src_lo), (w_lo, src_hi))):
                    lhs = w[:, g.par, :].rearrange("p (c n) -> p c n", c=KC)[:, c, i * P:(i + 1) * P]
                    for a in range(2):
                        last = nc.tensor.matmul(proj[:, 2 * i + a, 0:HALF], lhs, x[:, c, a * HALF:(a + 1) * HALF],
                                                start=(c == 0 and n == 0), stop=(c == KC - 1 and n == 2))
                if c == KC - 1:
                    last.then_inc(mm_ready[i], 1)
                return last

            def group(g, src_hi, src_lo):
                for i in range(2):
                    for c in range(KC):
                        chunk(g, i, c, src_hi, src_lo)

            pe.wait_ge(ld_x, 48)
            for n, (t, c) in enumerate(QUADS):
                if n >= 4:
                    pe.wait_ge(x_lo, n - 3)
                w = ntok(t)
                for j in range(4):
                    k = 4 * c + j
                    last = nc.tensor.transpose(att[:, n % 4, j * P:j * P + w], x_tok[0:w, t, k * P:(k + 1) * P],
                                               ident[0:w, 0:w])
                last.then_inc(tr_x, 1)
            pe.wait_ge(ld_conv, 32)
            for c in range(KC):
                nc.tensor.transpose(proj[:, 0, c * 16:(c + 1) * 16], convraw[:, c * P:(c + 1) * P], ident[0:16, 0:16])
            nc.tensor.transpose(proj[:, 0, P:P + 24], cwraw[:, :], ident[0:24, 0:24]).then_inc(tr_conv, 1)
            pe.wait_ge(x_lo, len(QUADS))
            pe.wait_ge(conv_ready, 1)
            group(Step(0), h_hi, h_lo)
            pe.wait_ge(mm_free[0], 1)
            pe.wait_ge(mm_free[1], 1)
            pe.wait_ge(ld_ck, 16)
            for t in range(NT):
                w = ntok(t)
                nc.tensor.transpose(att[0:w, t // 4, t % 4 * P:(t % 4 + 1) * P], v_t[:, t * P:t * P + w], ident[:, :])
            nc.tensor.transpose(att[:, 1, P:2 * P], k_t[:, WIN + SEQ - P:WIN + SEQ], ident[:, :])
            nc.tensor.transpose(att[0:NS, 1, 2 * P:3 * P], k_t[:, WIN + SEQ:], ident[:, :])
            for b in range(NB_S):
                last = nc.tensor.transpose(att[:, 2 + b // 4, b % 4 * P:(b % 4 + 1) * P], cache_k[:, b, :], ident[:, :])
            last.then_inc(tr_kv, 1)
            for j in range(4):
                group(Step(G_Q + j), h_hi, h_lo)

            pe.wait_ge(qs_ready, 1)
            pe.wait_ge(ckt_ready, 1)
            pe.wait_ge(kv_tok_ready, 1)
            for i in range(NB_S):
                for e in range(2):
                    b = (i + 2 * e) % NB_S
                    r = slice(e * HD, (e + 1) * HD)
                    o = att[r, b // 2, b % 2 * KEYS_S:(b % 2 + 1) * KEYS_S]
                    lhs = q_smp[r, b, :]
                    nc.tensor.matmul(o[:, 0:WIN], lhs, cache_kt[r, b, :], start=True, stop=True)
                    last = nc.tensor.matmul(o[:, WIN:KEYS_S], lhs, k_t[r, WIN + SEQ:], start=True, stop=True)
            last.then_inc(sl_ready, 1)
            pe.wait_ge(sl_read, 1)

            with pe.Fori(0, 2) as it:
                for h in range(2):
                    g = Step(G_GA + h, it, 2)
                    u0, b0, blk = it * 16 + h * 8, it * 4 + h * 2, it * 2 + h
                    todo = [(i, c) for i in range(2) for c in range(KC)]

                    def pv(mb):
                        pe.wait_ge(pt_read, u0 + 4 * mb + 4 + 1)
                        pe.wait_ge(o_lo, b0 + mb + 1)
                        for c in range(2):
                            for e in range(2):
                                r = slice(e * HD, (e + 1) * HD)
                                last = nc.tensor.matmul(att[r, 3, :], v_blk[h][:, c, r],
                                                        p_t[:, c, e, :, :].rearrange("p m q -> p (m q)"),
                                                        start=(c == 0), stop=(c == 1))
                        last.then_inc(pv_ready, 1)

                    for s in range(10):
                        for _ in range(CHUNKS_AT[s][0]):
                            chunk(g, *todo.pop(0), h_hi, h_lo)
                        if s < 8:
                            if s == 0:
                                pe.wait_ge(blk_ready, blk + 1)
                            pe.wait_ge(lg_read, u0 + s + 1)
                            for e in range(2):
                                r = slice(e * HD, (e + 1) * HD)
                                last = nc.tensor.matmul(att[:, e, 0:2 * P], q_blk[h][r, s, :],
                                                        k_blk[h][r, :], start=True, stop=True)
                            last.then_inc(lg_ready, 1)
                        for _ in range(CHUNKS_AT[s][1]):
                            chunk(g, *todo.pop(0), h_hi, h_lo)
                        if s >= 2:
                            m = s - 2
                            pe.wait_ge(p_ready, u0 + m + 1)
                            pe.wait_ge(pt_read, u0 + m + 1)
                            for e in range(2):
                                for c in range(2):
                                    last = nc.tensor.transpose(att[:, 2, (2 * e + c) * P:(2 * e + c + 1) * P],
                                                               s_p[m % 2][:, e, c * P:(c + 1) * P], ident[:, :])
                            last.then_inc(pt_ready, 1)
                        if s == 6:
                            pv(0)
                        if s == 9:
                            pv(1)
            pe.wait_ge(s_prob, 1)
            pe.wait_ge(o_lo, 2 * NBLK + 1)
            pe.wait_ge(ld_cv, 16)
            for b in range(NB_S):
                nc.tensor.transpose(att[:, b // 4, b % 4 * P:(b % 4 + 1) * P], s_s[:, b, 0:WIN], ident[:, :])
            for b in range(NB_S):
                last = nc.tensor.transpose(att[0:NS, 2 + b // 4, b % 4 * P:(b % 4 + 1) * P], s_s[:, b, WIN:KEYS_S],
                                           ident[:, :])
            last.then_inc(s_tr, 1)
            pe.wait_ge(s_trc, 2)
            for b in range(NB_S):
                for e in range(2):
                    r = slice(e * HD, (e + 1) * HD)
                    o = att[r, 0, b * HD:(b + 1) * HD]
                    nc.tensor.matmul(o, cache_v[:, b, r], ps_t[:, b, r], start=True, stop=False)
                    last = nc.tensor.matmul(o, v_tok[0:NS, NT, r], psn_t[:, b, r], start=False, stop=True)
            last.then_inc(s_pv, 1)
            pe.wait_ge(s_ol, 1)
            with pe.Fori(0, 2) as it:
                for h in range(2):
                    group(Step(G_AO + h, it, 2), mix_hi, mix_lo)
            with pe.Fori(0, 2) as it:
                for i in range(6):
                    group(Step(G_C + i, it, 6), h_hi, h_lo)
            pe.wait_ge(cv_lo, KC)
            for c in range(KC):
                last = nc.tensor.transpose(att[0:18, c // 4, c % 4 * P:(c % 4 + 1) * P], cnew[:, c, :], ident[:, :])
            last.then_inc(cn_tr, 1)
            with pe.Fori(0, 4) as it:
                group(Step(G_GC, it, 2), h_hi, h_lo)
                group(Step(G_GC + 1, it, 2), mix_hi, mix_lo)
            nc.tensor.sem_inc(wo_read, NT)
            nc.tensor.sem_inc(wo_ready, 1)
            nc.tensor.sem_inc(y_a, 1)
            nc.tensor.sem_inc(y_free, 1)
            nc.tensor.sem_inc(y_dv, 1)

            def tile_products(g, t, x_hi_, x_lo_, out):
                w = ntok(t)
                whi, wlo = (m[:, g.par, :].rearrange("p (c n) -> p c n", c=KC) for m in (w_hi, w_lo))
                for c in range(KC):
                    for n, (x, v) in enumerate(((x_hi_, whi), (x_hi_, wlo), (x_lo_, whi))):
                        last = nc.tensor.matmul(out, x[:, c, t * P:t * P + w], v[:, c, :],
                                                start=(c == 0 and n == 0), stop=(c == KC - 1 and n == 2))
                return last

            def wide_products(g, t, half, x_hi_, x_lo_, out):
                w = ntok(t)
                whi, wlo = (m[:, g.par, :].rearrange("p (c n) -> p c n", c=2) for m in (w_hi, w_lo))
                for c in range(2):
                    for n, (x, v) in enumerate(((x_hi_, whi), (x_hi_, wlo), (x_lo_, whi))):
                        last = nc.tensor.matmul(out, x[:, c, t * P:t * P + w], v[:, c, half * 512:(half + 1) * 512],
                                                start=(c == 0 and n == 0), stop=(c == 1 and n == 2))
                return last

            pe.wait_ge(mg_lo, KC)
            pe.wait_ge(mm_free[0], G_WO)
            pe.wait_ge(mm_free[1], G_WO)
            pe.wait_ge(cn_out, 1)
            with pe.Fori(0, 2) as it:
                for h in range(2):
                    g = Step(G_WO + h, it, 2)
                    pe.wait_ge(w_ready, g.v + 1)
                    for t in range(NT):
                        pe.wait_ge(wo_read, it * 2 * NT + h * NT + t + 1)
                        last = tile_products(g, t, merged_hi, merged_lo, tile_bank(t)[0:ntok(t), 0:GW])
                        last.then_inc(wo_ready, 1)
            pe.wait_ge(wo_read, 5 * NT)
            for n, (t, c) in enumerate(QUADS):
                w = ntok(t)
                pe.wait_ge(x2_ready, t + 1)
                if n >= 4:
                    pe.wait_ge(x2_lo, n - 3)
                for j in range(4):
                    k = 4 * c + j
                    last = nc.tensor.transpose(att[:, n % 4, j * P:j * P + w], res[0:w, t, k * P:(k + 1) * P],
                                               ident[0:w, 0:w])
                last.then_inc(x2_tr, 1)
            pe.wait_ge(x2_lo, 2 * NT)
            pe.wait_ge(rw_ready, 1)
            for t in range(NT):
                w = ntok(t)
                for c in range(KC):
                    for n, (x, v) in enumerate(((xt_hi, rw_hi), (xt_hi, rw_lo), (xt_lo, rw_hi))):
                        last = nc.tensor.matmul(att[0:w, 3, t * NE:(t + 1) * NE], x[:, c, t * P:t * P + w], v[:, c, :],
                                                start=(c == 0 and n == 0), stop=(c == KC - 1 and n == 2))
            last.then_inc(rt_ready, 1)
            pe.wait_ge(w_ready, G_SU + 1)
            pe.wait_ge(sc_ready, 1)

            def shared_gate_up(m):
                for k, g in enumerate((Step(G_SG), Step(G_SU))):
                    whi, wlo = (v[:, g.par, :].rearrange("p (c n) -> p c n", c=KC) for v in (w_hi, w_lo))
                    for c in range(KC):
                        for n, (v, x) in enumerate(((whi, xt_hi), (whi, xt_lo), (wlo, xt_hi))):
                            for a in range(2):
                                last = nc.tensor.matmul((proj, att)[m][:, 2 * k + a, 0:HALF], v[:, c, m * P:(m + 1) * P],
                                                        x[:, c, a * HALF:(a + 1) * HALF],
                                                        start=(c == 0 and n == 0), stop=(c == KC - 1 and n == 2))
                    if k == 1:
                        last.then_inc(su_ready, 1)
                    elif m == 1:
                        last.then_inc(sg_used, 1)

            shared_gate_up(0)
            pe.wait_ge(sel_ready, 1)
            pe.wait_ge(hs_ready, 1)
            for t in range(NT):
                for s in range(t + 1):
                    nc.tensor.matmul(proj[:, 0, t * NE:(t + 1) * NE], (ones_b if s < t else tri_b)[:, :], sel[:, s, :],
                                     start=(s == 0), stop=(s == t))
            for s in range(NT):
                last = nc.tensor.matmul(proj[:, 1, 0:NE], ones_b[:, :], sel[:, s, :], start=(s == 0), stop=(s == NT - 1))
            last.then_inc(rank_ready, 1)
            shared_gate_up(1)
            pe.wait_ge(w_ready, G_P0 + 1)
            for t in range(NT):
                if t == 2:
                    pe.wait_ge(hs_ready, 2)
                tile_products(Step(G_P0), t, xt_hi, xt_lo, g0_bank(t)[0:ntok(t), 0:GW]).then_inc(g0_ready, 1)
            pe.wait_ge(w_ready, G_SD + 1)
            pe.wait_ge(hs_ld, 1)
            for n, (t, c) in enumerate(QUADS):
                w = ntok(t)
                if n >= 4:
                    pe.wait_ge(sd_read, n - 3)
                else:
                    pe.wait_ge(g0_read, n + 1)
                wide_products(Step(G_SD), t, c, hs_hi, hs_lo, sd_bank(n)[0:w, :]).then_inc(sd_ready, 1)
            for n in range(NTK):
                pe.wait_ge(tb_ready, n + 1)
                nc.tensor.matmul(att[:, 3, 0:2 * MAXPASS], tab_a[:, n % TAB_RING, :],
                                 tab_b[:, n % TAB_RING, :, :].rearrange("p a n -> p (a n)"),
                                 start=(n == 0), stop=(n == NTK - 1)).then_inc(tb_used, 1)
            pe.wait_ge(rank_read, 1)
            pe.wait_ge(sd_read, 2 * NT)

            def turn(k):
                pe.wait_ge(gathered, k * 16 + 16)
                for c in range(KC):
                    last = nc.tensor.transpose(proj[:, c // 4, c % 4 * P:(c % 4 + 1) * P], xg[:, :, c], ident[:, :])
                last.then_inc(xtr, 1)

            pe.wait_ge(routed, 1)
            turn(0)
            count = pe.alloc_register("pass_count")
            pe.reg_mov(count, 0)
            with pe.Fori(0, NPE // 2) as it:
                for i in range(2):
                    n_of_pair = pass_counts(pe, it * 2 + i)
                    gate_up = [w_exp[i][:, e, 0:2 * KC * FF].rearrange("p (k c n) -> p c k n", k=2, c=KC) for e in range(2)]
                    down = [w_exp[i][:, e, 2 * KC * FF:].rearrange("p (c n) -> p c n", c=2) for e in range(2)]
                    for n in range(3):
                        pe.wait_ge(w_exp_in[n], (it * 2 + i) * 32 + (32 if n == 0 else 16))
                    past(nc.tensor, 1)
                    with pe.Fori(0, n_of_pair):
                        k = pe.snap(count, min_val=0, max_val=MAXPASS - 3)
                        pe.wait_ge(xt_a, k + 1)
                        pe.wait_ge(xt_d, k + 1)
                        for c in range(KC):
                            for e in range(2):
                                last = nc.tensor.matmul(att[e * SLOT:(e + 1) * SLOT, 0, :], xt[:, c, e * SLOT:(e + 1) * SLOT],
                                                        gate_up[e][:, c, :, :], start=(c == 0), stop=(c == KC - 1))
                        last.then_inc(gu_ready, 1)
                        turn(k + 1)
                        pe.wait_ge(h_ready, k + 1)
                        for c in range(2):
                            last = nc.tensor.transpose(att[:, 1, c * P:(c + 1) * P], h_e[:, c:FF:2], ident[:, :])
                        last.then_inc(htr, 1)
                        for n in range(1, 3):
                            pe.wait_ge(w_exp_in[n], (it * 2 + i) * 32 + 32)
                        pe.wait_ge(ht_ready, k + 1)
                        pe.wait_ge(y_a, k + 1)
                        pe.wait_ge(y_dv, k + 1)
                        for c in range(2):
                            for half in range(2):
                                for e in range(2):
                                    last = nc.tensor.matmul(proj[e * SLOT:(e + 1) * SLOT, 2 + half, :],
                                                            ht_e[:, c, e * SLOT:(e + 1) * SLOT],
                                                            down[e][:, c, half * 512:(half + 1) * 512],
                                                            start=(c == 0), stop=(c == 1))
                        last.then_inc(y_mm, 1)
                        pe.reg_add(count, count, 1)
            pe.wait_ge(xt_last, 2)
            pe.wait_ge(ld_p, 32)
            for c in range(2):
                for t in range(NT):
                    w = ntok(t)
                    o = (proj if c == 0 else att)[:, 0:2, :].rearrange("p a n -> p (a n)")[:, t * P:t * P + w]
                    last = nc.tensor.transpose(o, p_tok[0:w, t, c * P:(c + 1) * P], ident[0:w, 0:w])
            last.then_inc(p_tr, 1)
            pe.wait_ge(p_lo, 1)
            whi, wlo = (m[:, :].rearrange("p (c n) -> p c n", c=2) for m in (pp_hi, pp_lo))
            for j in range(4):
                if j:
                    pe.wait_ge(w_ready, G_PG + j)
                for t in range(NT):
                    w = ntok(t)
                    if j:
                        pe.wait_ge(pg_read, (j - 1) * NT + t + 1)
                    out = tile_bank(t)[0:w, :]
                    for c in range(2):
                        for n, (x, v) in enumerate(((pt_hi, whi), (pt_hi, wlo), (pt_lo, whi))):
                            last = nc.tensor.matmul(out[:, GW:2 * GW], x[:, c, t * P:t * P + w], v[:, c, j * GW:(j + 1) * GW],
                                             start=(c == 0 and n == 0), stop=(c == 1 and n == 2))
                    if j:
                        last = tile_products(Step(G_PG + j - 1), t, xt_hi, xt_lo, out[:, 0:GW])
                    last.then_inc(pg_ready, 1)

        @block.vector
        def _(dve):
            for n, (t, c) in enumerate(QUADS):
                dve.wait_ge(x_hi, n + 1)
                w = ntok(t)
                nc.vector.tensor_tensor(h_lo[:, 4 * c:4 * c + 4, t * P:t * P + w],
                                        att[:, n % 4, :].rearrange("p (c n) -> p c n", c=4)[:, :, 0:w],
                                        h_hi[:, 4 * c:4 * c + 4, t * P:t * P + w].bitcast(F32),
                                        ALU.subtract).then_inc(x_lo, 1)
            dve.wait_ge(tr_conv, 1)
            nc.vector.tensor_copy(cst[:, :, :].rearrange("p c n -> p (c n)"), proj[:, 0, 0:P])
            nc.vector.tensor_copy(cw[:, :], proj[:, 0, P:P + 24]).then_inc(conv_ready, 1)
            split_lo(dve, Step(0))
            split_lo(dve, Step(1))
            dve.wait_ge(ld_sink, 32)
            nc.vector.tensor_scalar(nsink16[:, :], sink16[:, :], -1.0, None, ALU.mult)
            nc.vector.tensor_tensor(sel16[:, :], sel16[:, :], sink16[:, :], ALU.mult)
            dve.drain()
            nc.vector.reduce_sum(sink_s[:, :], sel16[:, :], AX.X)
            dve.drain()
            nc.vector.tensor_scalar(nsink_s[:, :], sink_s[:, :], -1.0, None, ALU.mult)
            dve.drain()
            dve.wait_ge(mm_ready[1], 1)
            nc.vector.tensor_copy(two(v_t[:, :]), slot(1)).then_inc(mm_free[1], 1)
            for j in range(4):
                split_lo(dve, Step(G_Q + 1 + j))
                if j == 0:
                    dve.wait_ge(tr_kv, 1)
                    nc.vector.tensor_copy(v_tok[:, 1:NT, :].rearrange("p a n -> p (a n)"), att[:, 0, :])
                    nc.vector.tensor_copy(v_tok[0:NS, NT, :], att[0:NS, 1, 0:P])
                    nc.vector.tensor_copy(k_tok[:, 0, :], att[:, 1, P:2 * P])
                    nc.vector.tensor_copy(k_tok[0:NS, 1, :], att[0:NS, 1, 2 * P:3 * P]).then_inc(kv_tok_ready, 1)
                dve.wait_ge(mm_ready[1], j + 2)
                nc.vector.tensor_scalar(two(q_t[:, 2 * j + 1, :]), slot(1), HD ** -0.5, None, ALU.mult).then_inc(mm_free[1], 1)
            dve.wait_ge(mm_free[0], G_Q + 4)
            dve.drain()
            nc.vector.tensor_copy(q_smp[:, :, :].rearrange("p b (m s) -> p b m s", s=S_S),
                                  q_t[:, :, SEQ:T].rearrange("p m (b s) -> p b m s", b=NB_S)).then_inc(qs_ready, 1)
            dve.wait_ge(sl_ready, 1)
            dve.wait_ge(ld_c1, 32)
            for n in range(4):
                last = nc.vector.tensor_tensor(s_s[:, 2 * n:2 * n + 2, :].rearrange("p b k -> p (b k)"),
                                               att[:, n, 0:2 * KEYS_S],
                                               mask_s[:, 2 * n:2 * n + 2, :].rearrange("p b k -> p (b k)"), ALU.add)
            last.then_inc(sl_read, 1)
            dve.drain()
            nc.vector.reduce_max(mx_s[:, :], s_s[:, :, :], AX.X)
            dve.drain()
            nc.vector.tensor_scalar(nm_s[:, :], mx_s[:, :], -1.0, nsink_s[:, :], ALU.mult, ALU.min)
            dve.drain()
            nc.vector.tensor_tensor(s_s[:, :, :], s_s[:, :, :], nm_s[:, :].unsqueeze(2).to_broadcast([P, NB_S, KEYS_S]),
                                    ALU.add).then_inc(s_sub, 1)

            dve.wait_ge(zeroed, 2)
            with dve.Fori(0, 2) as it:
                for h in range(2):
                    u0, b0, blk = it * 16 + h * 8, it * 4 + h * 2, it * 2 + h
                    dve.wait_ge(mm_free[0], G_Q + 4)
                    nc.vector.tensor_copy(q_blk[h][:, :, :], q_t[:, :, bass.ds(blk * P, P)])
                    nc.vector.tensor_copy(k_blk[h][:, :], k_t[:, bass.ds(blk * P, 2 * P)])
                    nc.vector.tensor_copy(v_blk[h][:, :, :], v_tok[:, bass.ds(blk, 2), :]).then_inc(blk_ready, 1)
                    if h == 0:
                        nc.vector.tensor_copy(mask_0[:, :], mask_p[:, bass.ds(it, 1), :].rearrange("p o n -> p (o n)"))
                        dve.drain()
                    mk = mask_0[:, :] if h == 0 else mask_p[:, 1, :]
                    for s in range(10):
                        if s < 8:
                            r = s % 2
                            dve.wait_ge(lg_ready, u0 + s + 1)
                            dve.wait_ge(pt_ready, u0 + s + 1)
                            past(nc.vector, 2)
                            for e in range(2):
                                last = nc.vector.tensor_tensor_reduce(s_p[r][:, e, :], att[:, e, 0:2 * P], mk, 1.0, -BIG,
                                                                      ALU.add, ALU.max, mx[:, r, e:e + 1])
                            last.then_inc(lg_read, 1)
                            dve.drain()
                            nc.vector.scalar_tensor_tensor(nm[:, r, :], mx[:, r, :], -1.0, nsink16[:, s:16:8],
                                                           ALU.mult, ALU.min)
                            dve.drain()
                            nc.vector.tensor_tensor(ds[:, r, :], nm[:, r, :], sink16[:, s:16:8], ALU.add).then_inc(nm_ready, 1)
                        if 1 <= s <= 8:
                            r = (s - 1) % 2
                            dve.wait_ge(e_ready, u0 + s)
                            nc.vector.tensor_tensor(rc[:, r, :], sm_p[:, r, :], es[:, r, :], ALU.add)
                            dve.drain()
                            nc.vector.reciprocal(rc[:, r, :], rc[:, r, :])
                            dve.drain()
                            for e in range(2):
                                last = nc.vector.tensor_scalar(s_p[r][:, e, :], s_p[r][:, e, :], rc[:, r, e:e + 1], None, ALU.mult)
                            last.then_inc(p_ready, 1)
                        if s == 5:
                            split_lo(dve, Step(G_GA + h + 1, it, 2))
                        if s == 6:
                            dve.wait_ge(mm_ready[0], it * 2 + h + G_GA + 1)
                            nc.vector.tensor_copy(two(row(gate_a, it * 4 + 2 * h)), slot(0)).then_inc(mm_free[0], 1)
                        if s == 8 or s == 9:
                            mb = s - 8
                            dve.wait_ge(o_hi, b0 + mb + 1)
                            nc.vector.tensor_tensor(mix_lo[:, 4 * mb:4 * mb + 4, bass.ds(blk * P, P)],
                                                    att[:, 3, :].rearrange("p (m q) -> p m q", m=4),
                                                    mix_hi[:, 4 * mb:4 * mb + 4, bass.ds(blk * P, P)].bitcast(F32),
                                                    ALU.subtract).then_inc(o_lo, 1)
            dve.wait_ge(s_exp, 1)
            nc.vector.reduce_sum(sum_s[:, :], s_s[:, :, :], AX.X)
            dve.drain()
            nc.vector.tensor_tensor(sum_s[:, :], sum_s[:, :], es_s[:, :], ALU.add)
            dve.drain()
            nc.vector.reciprocal(sum_s[:, :], sum_s[:, :])
            dve.drain()
            nc.vector.tensor_tensor(s_s[:, :, :], s_s[:, :, :], sum_s[:, :].unsqueeze(2).to_broadcast([P, NB_S, KEYS_S]),
                                    ALU.mult).then_inc(s_prob, 1)
            dve.wait_ge(s_tr, 1)
            nc.vector.tensor_copy(psn_t[:, :, :].rearrange("p (a b) n -> p a (b n)", a=2), att[0:NS, 2:4, :]).then_inc(s_trc, 1)
            dve.wait_ge(s_oh, 1)
            nc.vector.tensor_tensor(mix_lo[:, :, SEQ:T].rearrange("p m (b s) -> p b m s", b=NB_S),
                                    att[:, 0, :].rearrange("p (b m s) -> p b m s", b=NB_S, m=8),
                                    mix_hi[:, :, SEQ:T].rearrange("p m (b s) -> p b m s", b=NB_S).bitcast(F32),
                                    ALU.subtract).then_inc(s_ol, 1)
            with dve.Fori(0, 2) as it:
                for h in range(2):
                    split_lo(dve, Step(G_AO + h + 1, it, 2))
                    dve.wait_ge(sga, it * 2 + h + 1)
                    for i in range(2):
                        dve.wait_ge(mm_ready[i], it * 2 + h + G_AO + 1)
                        m = row(gate_a, it * 4 + 2 * h + i)
                        nc.vector.tensor_tensor(two(m), slot(i), two(m), ALU.mult).then_inc(mm_free[i], 1)
            for i in range(2):
                nc.vector.memset(u_ext[i][:, 0:2], 0.0)
            with dve.Fori(0, 2) as it:
                for jj in range(2):
                    m0 = it * 4 + 2 * jj
                    for k in range(3):
                        gb = G_C + 3 * jj + k
                        split_lo(dve, Step(gb + 1, it, 6))
                        if k == 1:
                            for i in range(2):
                                u = u_ext[i]
                                us = u[:, 514:594].rearrange("p (b n) -> p b n", n=10)
                                dve.wait_ge(mm_free[i], it * 6 + gb)
                                dve.wait_ge(mm_ready[i], it * 6 + gb + 1)
                                nc.vector.tensor_tensor(u[:, 2:2 + HALF], proj[:, 2 * i, 0:HALF], cc_t[:, i, 0:HALF], ALU.mult)
                                nc.vector.tensor_tensor(u[:, 2 + HALF:514], proj[:, 2 * i + 1, 0:SEQ - HALF],
                                                        cc_t[:, i, HALF:SEQ], ALU.mult)
                                nc.vector.tensor_tensor(us[:, :, 2:10],
                                                        proj[:, 2 * i + 1, SEQ - HALF:HALF].rearrange("p (b s) -> p b s", b=NB_S),
                                                        cc_t[:, i, SEQ:T].rearrange("p (b s) -> p b s", b=NB_S),
                                                        ALU.mult).then_inc(mm_free[i], 1)
                                nc.vector.tensor_copy(us[:, :, 0:2],
                                                      row(cst, m0 + i).rearrange("p (b j) -> p b j", j=2)).then_inc(u_done, 1)
                            dve.drain()
                            for i in range(2):
                                u = u_ext[i]
                                us = u[:, 514:594].rearrange("p (b n) -> p b n", n=10)
                                cn = row(cnew, m0 + i)
                                nc.vector.tensor_copy(cn[:, 0:2], u[:, 512:514])
                                nc.vector.tensor_copy(cn[:, 2:18].rearrange("p (b j) -> p b j", j=2), us[:, :, 8:10])
                            for j in range(3):
                                for i in range(2):
                                    wj_ = cw[:, bass.ds(m0 + (j * KC + i), 1)]
                                    u = u_ext[i][:, j:j + 592]
                                    if j == 0:
                                        nc.vector.tensor_scalar(y_cv[i][:, 0:592], u, wj_, None, ALU.mult)
                                    else:
                                        nc.vector.scalar_tensor_tensor(y_cv[i][:, 0:592], u, wj_, y_cv[i][:, 0:592], ALU.mult, ALU.add)
                                dve.drain()
                        if k == 2:
                            for i in range(2):
                                dve.wait_ge(mm_ready[i], it * 6 + gb + 1)
                                nc.vector.tensor_tensor(prod[i][:, 0:HALF], proj[:, 2 * i, 0:HALF], y_cv[i][:, 0:HALF], ALU.mult)
                                nc.vector.tensor_tensor(prod[i][:, HALF:SEQ], proj[:, 2 * i + 1, 0:SEQ - HALF],
                                                        y_cv[i][:, HALF:SEQ], ALU.mult)
                                last = nc.vector.tensor_tensor(
                                    prod[i][:, SEQ:T].rearrange("p (b s) -> p b s", b=NB_S),
                                    proj[:, 2 * i + 1, SEQ - HALF:HALF].rearrange("p (b s) -> p b s", b=NB_S),
                                    y_cv[i][:, 514:594].rearrange("p (b n) -> p b n", n=10)[:, :, 0:S_S], ALU.mult)
                                last.then_inc(mm_free[i], 1)
                                dve.drain().then_inc(pr_ready, 1)
                            for i in range(2):
                                dve.wait_ge(cv_hi, m0 + i + 1)
                                nc.vector.tensor_tensor(row(mix_lo, m0 + i), prod[i][:, :], row(mix_hi, m0 + i).bitcast(F32),
                                                        ALU.subtract).then_inc(cv_lo, 1)
            with dve.Fori(0, 4) as it:
                split_lo(dve, Step(G_GC + 1, it, 2))
                split_lo(dve, Step(G_GC + 2, it, 2))
                for i in range(2):
                    dve.wait_ge(mm_free[i], it * 2 + G_GC + 1)
                    dve.wait_ge(mm_ready[i], it * 2 + G_GC + 2)
                    nc.vector.tensor_tensor(two(prod[i][:, :]), slot(i), two(sig_c[:, i, :]), ALU.mult).then_inc(mm_free[i], 1)
                    dve.drain()
                    nc.vector.tensor_tensor(prod[i][:, :], prod[i][:, :], row(gate_a, it * 2 + i), ALU.add).then_inc(mg_ready, 1)
                for i in range(2):
                    dve.wait_ge(mg_hi, it * 2 + i + 1)
                    nc.vector.tensor_tensor(row(merged_lo, it * 2 + i), prod[i][:, :], row(merged_hi, it * 2 + i).bitcast(F32),
                                            ALU.subtract).then_inc(mg_lo, 1)
            nc.vector.memset(eps[:, :], LN_EPS)
            dve.wait_ge(ld_res, 32)

            def normalise(t, gb):
                w = ntok(t)
                nc.vector.reciprocal(rstd[0:w, t:t + 1], rstd[0:w, t:t + 1])
                dve.drain()
                nc.vector.tensor_scalar(res[0:w, t, :], res[0:w, t, :], mv[0:w, t, 0:1], rstd[0:w, t:t + 1],
                                        ALU.subtract, ALU.mult)
                dve.drain()
                nc.vector.tensor_tensor(res[0:w, t, :], res[0:w, t, :], gb[0:w, 0, :], ALU.mult)
                dve.drain()
                return nc.vector.tensor_tensor(res[0:w, t, :], res[0:w, t, :], gb[0:w, 1, :], ALU.add)

            def transposed_low(t):
                w = ntok(t)
                for c in range(2):
                    n = 2 * t + c
                    dve.wait_ge(x2_hi, n + 1)
                    nc.vector.tensor_tensor(xt_lo[:, 4 * c:4 * c + 4, t * P:t * P + w],
                                            att[:, n % 4, :].rearrange("p (c n) -> p c n", c=4)[:, :, 0:w],
                                            xt_hi[:, 4 * c:4 * c + 4, t * P:t * P + w].bitcast(F32),
                                            ALU.subtract).then_inc(x2_lo, 1)

            for j in range(4):
                split_lo(dve, Step(G_WO + j + 1))
                for t in range(NT):
                    w = ntok(t)
                    r = res[0:w, t, j * GW:(j + 1) * GW]
                    dve.wait_ge(wo_ready, j * NT + t + 2)
                    nc.vector.scalar_tensor_tensor(r, r, ALPHA, tile_bank(t)[0:w, 0:GW], ALU.mult, ALU.add).then_inc(wo_read, 1)
                    dve.drain()
                    nc.vector.bn_stats(stats[0:w, t, j, :], r)
                    if j == 3:
                        dve.drain()
                        nc.vector.bn_aggr(mv[0:w, t, :], stats[0:w, t, :, :]).then_inc(var_ready, 1)
                        if t == 0:
                            dve.wait_ge(rw_h, 1)
                            nc.vector.tensor_tensor(rw_lo[:, :, :], rw_raw[:, :, :], rw_hi[:, :, :].bitcast(F32),
                                                    ALU.subtract).then_inc(rw_ready, 1)
                            dve.wait_ge(ld_ln1, 32)
                        else:
                            dve.wait_ge(std_ready, t)
                            normalise(t - 1, g1b1).then_inc(x2_ready, 1)
            dve.wait_ge(std_ready, NT)
            normalise(NT - 1, g1b1).then_inc(x2_ready, 1)
            for t in range(NT):
                transposed_low(t)

            dve.wait_ge(rt_ready, 1)
            nc.vector.tensor_copy(tri_b[:, :], tri)
            nc.vector.tensor_copy(ones_b[:, :], ones)
            nc.vector.memset(scores[NS:P, NT - 1, :], 0.0)
            dve.wait_ge(sc_ready, 1)
            dve.drain()
            nc.vector.tensor_tensor(biased[:, :, :], scores[:, :, :], rbias[:, :].unsqueeze(1).to_broadcast([P, NT, NE]), ALU.add)
            dve.drain()
            for t in range(NT):
                for g in range(NGRP):
                    nc.vector.max(best8[:, t * NGRP + g, :], biased[:, t, g * 8:(g + 1) * 8])
            dve.drain()
            nc.vector.tensor_tensor(gsum[:, :, :].rearrange("p t g -> p (t g)"), best8[:, :, 0], best8[:, :, 1], ALU.add)
            dve.drain()
            for t in range(NT):
                nc.vector.max(gbest[:, t, :], gsum[:, t, :])
            dve.drain()
            for t in range(NT):
                nc.vector.max_index(gidx[:, t, :], gbest[:, t, :], gsum[:, t, :])
            dve.drain()
            nc.vector.tensor_copy(gidx_f[:, :, :], gidx[:, :, 0:TOPG])
            dve.drain()
            for t in range(NT):
                nc.vector.tensor_tensor(ghot[:, t, :, :], iota64[:, 0:NGRP].unsqueeze(1).to_broadcast([P, TOPG, NGRP]),
                                        gidx_f[:, t, :].unsqueeze(2).to_broadcast([P, TOPG, NGRP]), ALU.is_equal)
            dve.drain()
            nc.vector.reduce_sum(gmask[:, :, :], ghot[:, :, :, :].rearrange("p t i g -> p t g i"), AX.X)
            dve.drain()
            nc.vector.tensor_scalar(gmask[:, :, :], gmask[:, :, :], BIG, -BIG, ALU.mult, ALU.add)
            dve.drain()
            nc.vector.tensor_tensor(biased[:, :, :].rearrange("p t (g n) -> p (t g) n", n=8),
                                    biased[:, :, :].rearrange("p t (g n) -> p (t g) n", n=8),
                                    gmask[:, :, :].rearrange("p t g -> p (t g)").unsqueeze(2).to_broadcast([P, NT * NGRP, 8]),
                                    ALU.add)
            dve.drain()
            for t in range(NT):
                nc.vector.max(ebest[:, t, :], biased[:, t, :])
            dve.drain()
            for t in range(NT):
                nc.vector.max_index(eidx[:, t, :], ebest[:, t, :], biased[:, t, :])
            dve.drain()
            nc.vector.tensor_copy(eidx_f[:, :, :], eidx[:, :, 0:TOPK])
            dve.drain()
            nc.vector.memset(eidx_f[NS:P, NT - 1, :], -1.0)
            dve.drain()
            nc.vector.tensor_tensor(hot[:, :, :], iota64.unsqueeze(1).to_broadcast([P, NTK, NE]),
                                    eidx_f[:, :, :].rearrange("p t j -> p (t j)").unsqueeze(2).to_broadcast([P, NTK, NE]),
                                    ALU.is_equal)
            dve.drain()
            with nc.allow_low_precision(reason="each sum is 0 or 1, exact in bfloat16"):
                nc.vector.reduce_sum(sel[:, :, :], hot[:, :, :].rearrange("p (t j) e -> p t e j", t=NT), AX.X).then_inc(sel_ready, 1)

            def shared_act(m):
                dve.wait_ge(ss_ready, m + 1)
                ps = (proj, att)[m]
                nc.vector.tensor_tensor(two(hs_f[:, m, :]), ps[:, 0:2, 0:HALF], two(hs_f[:, m, :]), ALU.mult)
                dve.drain()
                nc.vector.tensor_tensor(two(hs_f[:, m, :]), ps[:, 2:4, 0:HALF], two(hs_f[:, m, :]), ALU.mult).then_inc(hs_ready, 1)

            def pick(dst, per_expert):
                for t in range(NT):
                    js = slice(t * TOPK, (t + 1) * TOPK)
                    nc.vector.tensor_tensor(picked[:, js, :], hot[:, js, :],
                                            per_expert[:, t, :].unsqueeze(1).to_broadcast([P, TOPK, NE]), ALU.mult)
                dve.drain()
                nc.vector.reduce_sum(dst, picked[:, :, :], AX.X)
                dve.drain()

            shared_act(0)
            dve.wait_ge(rank_ready, 1)
            nc.vector.tensor_copy(base64[:, :], proj[:, 1, 0:NE:2])
            dve.drain()
            nc.vector.tensor_tensor(nmax[:, :], base64[:, :], proj[:, 1, 1:NE:2], ALU.max)
            dve.drain()
            nc.vector.tensor_scalar(npass_i[:, :], nmax[:, :], SLOT - 1.0, None, ALU.add)
            nc.vector.tensor_copy(rank_i[:, :, :].rearrange("p t e -> p (t e)"), proj[:, 0, 0:NT * NE]).then_inc(rank_read, 1)
            dve.drain()
            nc.vector.tensor_scalar(npass_i[:, :], npass_i[:, :], 6, None, ALU.arith_shift_right)
            dve.drain()
            nc.vector.tensor_scalar(npass_f[:, :], npass_i[:, :], 1.0, None, ALU.max)
            dve.drain()
            cur = npass_f
            for s in range(5):
                nxt = cums[s % 2]
                nc.vector.tensor_copy(nxt[:, 0:1 << s], cur[:, 0:1 << s])
                nc.vector.tensor_tensor(nxt[:, 1 << s:], cur[:, 1 << s:], cur[:, 0:NPE - (1 << s)], ALU.add)
                dve.drain()
                cur = nxt
            nc.vector.tensor_copy(npass_i[:, :], cur[:, :])
            dve.drain()
            nc.vector.tensor_scalar(npass_i[:, :], npass_i[:, :], 1, None, ALU.bitwise_and)
            dve.drain()
            nc.vector.tensor_copy(nmax[:, :], npass_i[:, :])
            dve.drain()
            nc.vector.tensor_copy(n_pass[:, 0:NPE - 1], npass_f[0:1, 0:NPE - 1])
            nc.vector.tensor_tensor(n_pass[:, NPE - 1:NPE], npass_f[0:1, NPE - 1:NPE], nmax[0:1, NPE - 1:NPE], ALU.add)
            nc.vector.tensor_copy(cum_pass[:, 0:NPE - 1], cur[0:1, 0:NPE - 1])
            nc.vector.tensor_tensor(nmax[0:1, 0:1], cur[0:1, NPE - 1:NPE], nmax[0:1, NPE - 1:NPE], ALU.add)
            dve.drain()
            nc.vector.tensor_copy(cum_pass[:, NPE - 1:NPE], nmax[0:1, 0:1])
            nc.vector.tensor_scalar(half_all[:, :], nmax[0:1, 0:1], 0.5, None, ALU.mult)
            nc.vector.tensor_tensor(base64[:, :], cur[:, :], npass_f[:, :], ALU.subtract)
            col_i = col_map[:, :, :].bitcast(I32)
            nc.vector.tensor_scalar(col_i, rank_i[:, :, :], 6, None, ALU.arith_shift_right)
            nc.vector.tensor_scalar(slot_map[:, :, :].bitcast(I32), rank_i[:, :, :], SLOT - 1, None, ALU.bitwise_and)
            dve.drain()
            nc.vector.tensor_copy(col_map[:, :, :], col_i)
            nc.vector.tensor_copy(slot_map[:, :, :], slot_map[:, :, :].bitcast(I32))
            dve.drain()
            for t in range(NT):
                nc.vector.tensor_tensor(col_map[:, t, :].rearrange("p (q e) -> p q e", e=2),
                                        col_map[:, t, :].rearrange("p (q e) -> p q e", e=2),
                                        base64[:, :].unsqueeze(2).to_broadcast([P, NPE, 2]), ALU.add)
            nc.vector.tensor_tensor(slot_map[:, :, :], slot_map[:, :, :], side.unsqueeze(1).to_broadcast([P, NT, NE]), ALU.add)
            dve.drain()
            dve.wait_ge(acc_zero, 64)
            pick(col_j[:, :], col_map)
            shared_act(1)
            dve.wait_ge(w_ready, G_SD)
            split_lo(dve, Step(G_SD))
            dve.wait_ge(hs_hd, 1)
            nc.vector.tensor_tensor(hs_lo[:, :, :], hs_f[:, :, :], hs_hi[:, :, :].bitcast(F32), ALU.subtract).then_inc(hs_ld, 1)
            pick(slot_j[:, :], slot_map)
            pick(wj[:, :], scores)
            wj3 = wj[:, :].rearrange("p (t j) -> p t j", t=NT)
            nc.vector.reduce_sum(ssum[:, :], wj3, AX.X)
            dve.drain()
            nc.vector.memset(ssum[NS:P, NT - 1:NT], 1.0)
            dve.drain()
            nc.vector.reciprocal(ssum[:, :], ssum[:, :])
            dve.drain()
            nc.vector.tensor_tensor(wj3, wj3, ssum[:, :].unsqueeze(2).to_broadcast([P, NT, TOPK]), ALU.mult)
            dve.drain()
            nc.vector.tensor_scalar(wj[:, :], wj[:, :], ROUTED_SCALE, None, ALU.mult)
            dve.drain()
            for n in range(NTK):
                j = n % TAB_RING
                if n >= TAB_RING:
                    dve.wait_ge(tb_used, n - TAB_RING + 1)
                nc.vector.tensor_scalar(tab_a[:, j, :], iota128, slot_j[:, n:n + 1], None, ALU.is_equal)
                for i, v in enumerate((val, wj)):
                    last = nc.vector.tensor_scalar(tab_b[:, j, i, :], iota_pass, col_j[:, n:n + 1], v[:, n:n + 1],
                                                   ALU.is_equal, ALU.mult)
                last.then_inc(tb_ready, 1)
            dve.wait_ge(tb_used, NTK)
            nc.vector.tensor_scalar(tab_e[:, :], att[:, 3, 0:MAXPASS], 0.0, PAD_V, ALU.is_equal, ALU.mult)
            dve.drain()
            nc.vector.tensor_tensor(tab_i[:, :], tab_e[:, :], att[:, 3, 0:MAXPASS], ALU.add)
            dve.drain()
            nc.vector.tensor_scalar(tab_s[:, :], tab_i[:, :], 3, None, ALU.arith_shift_right)
            dve.drain()
            nc.vector.tensor_scalar(tabx[:, :], tab_s[:, :], -1.0, None, ALU.add)
            nc.vector.tensor_scalar(tabs[:, :], tab_s[:, :], sum_row, -1.0, ALU.add, ALU.add)
            nc.vector.tensor_copy(tabw[:, :], att[:, 3, MAXPASS:2 * MAXPASS])
            dve.drain().then_inc(routed, 1)
            dve.wait_ge(x2_out, 16 * NT)
            dve.wait_ge(sd_read, 2 * NT)
            for t in range(NT):
                w = ntok(t)
                last = nc.vector.scalar_tensor_tensor(res[0:w, t, :], res[0:w, t, :], ALPHA, sdo[0:w, t, :], ALU.mult, ALU.add)
            last.then_inc(res_done, 1)

            def xt_half(k):
                dve.wait_ge(xtr, k + 1)
                nc.vector.tensor_copy(xt[:, 4:8, :].rearrange("p c n -> p (c n)"), proj[:, 1, :]).then_inc(xt_d, 1)

            xt_half(0)
            k_half = half_passes(dve)
            with dve.Fori(0, k_half) as it:
                for i in range(2):
                    k = it * 2 + i
                    dve.wait_ge(sg_ready, k + 1)
                    nc.vector.tensor_tensor(g_e[:, :], sg[:, :], att[:, 0, 0:FF], ALU.mult)
                    dve.drain()
                    nc.vector.tensor_tensor(h_e[:, :], g_e[:, :], att[:, 0, FF:2 * FF], ALU.mult).then_inc(h_ready, 1)
                    xt_half(k + 1)
                    dve.wait_ge(y_mm, k + 1)
                    dve.wait_ge(y_free, k + 1)
                    nc.vector.tensor_scalar(ysb[i][:, 512:D], proj[:, 3, :], tabw[:, bass.ds(k, 1)], None, ALU.mult).then_inc(y_dv, 1)
            dve.drain().then_inc(xt_last, 1)
            dve.wait_ge(hi_done, G_PP + 1)
            dve.wait_ge(rows_done, 1)
            nc.vector.tensor_tensor(pp_lo[:, :], w_raw[:, G_PP % 2, :], pp_hi[:, :].bitcast(F32), ALU.subtract).then_inc(w_ready, 1)
            split_lo(dve, Step(G_PG))
            dve.wait_ge(p_hi, 1)
            for c in range(2):
                last = nc.vector.tensor_tensor(pt_lo[:, c, :], p_bank(c), pt_hi[:, c, :].bitcast(F32), ALU.subtract)
            last.then_inc(p_lo, 1)

            def combine(t):
                w = ntok(t)
                for i in range(2):
                    dve.drain()
                    nc.vector.tensor_tensor(res[0:w, t, :], res[0:w, t, :], y_all[0:w, t, i, :], ALU.add)

            def finish(t):
                dve.wait_ge(std_ready, NT + t + 1)
                normalise(t, g2b2).then_inc(y_done, 1)

            for j in range(4):
                for t in range(NT):
                    w = ntok(t)
                    n = j * NT + t
                    if j == 0:
                        dve.wait_ge(pg_ready, n + 1)
                        gate = sig0[0:w, t, :]
                    else:
                        dve.wait_ge(pg_sig, n - NT + 1)
                        gate = sig_g[0:w, n % 2, :]
                    nc.vector.tensor_tensor(gate, gate, tile_bank(t)[0:w, GW:2 * GW], ALU.mult)
                    dve.drain()
                    r = res[0:w, t, j * GW:(j + 1) * GW]
                    nc.vector.tensor_tensor(r, r, gate, ALU.add).then_inc(pg_read, 1)
                    if j == 1:
                        if t == 0:
                            dve.wait_ge(ld_y, 64)
                        combine(t)
                    if j >= 2:
                        dve.drain()
                        for q in range(3) if j == 2 else (3,):
                            nc.vector.bn_stats(stats[0:w, t, q, :], res[0:w, t, q * GW:(q + 1) * GW])
                    if j == 3:
                        dve.drain()
                        nc.vector.bn_aggr(mv[0:w, t, :], stats[0:w, t, :, :]).then_inc(var_ready, 1)
                        if t >= 1:
                            finish(t - 1)
            finish(NT - 1)


_INS = ["x_prompt", "x_sample", "p_prompt", "p_sample", "state_win_k", "state_win_v", "state_conv", "w_in", "attn_sinks",
        "conv_w", "w_attn_out", "w_conv_out", "w_o", "ln1_g", "ln1_b", "w_router", "router_bias", "w_e_gate", "w_e_up",
        "w_e_down", "w_s_gate", "w_s_up", "w_s_down", "w_ple_gate", "w_ple_proj", "ln2_g", "ln2_b"]
_OUTS = [(1, SEQ, D), (NB_S, S_S, D), (1, 1, WIN, N_KV, HD), (1, 1, WIN, N_KV, HD), (1, 1, 2, D),
         (1, NB_S, WIN, N_KV, HD), (1, NB_S, WIN, N_KV, HD), (1, NB_S, 2, D)]


def kernel(**inputs):
    import concourse.bacc as bacc
    from concourse.bass_utils import run_bass_kernel_spmd

    nc = bacc.Bacc("TRN2", target_bir_lowering=False, num_devices=1)
    arrays, args = {}, []
    data = [(name, np.ascontiguousarray(inputs[name])) for name in _INS]
    data += list(zip(("const1", "const2"), pack_constants()))
    for name, a in data:
        arrays[f"in_{name}_dram"] = a
        args.append(nc.dram_tensor(f"in_{name}_dram", a.shape, mybir.dt.from_np(a.dtype), kind="ExternalInput").ap())
    for i, shape in enumerate(_OUTS):
        args.append(nc.dram_tensor(f"out_{i}_dram", shape, F32, kind="ExternalOutput").ap())
    decoder_step(nc, *args)
    r = run_bass_kernel_spmd(nc, [arrays], core_ids=[0])
    return tuple(r.results[0][f"out_{i}_dram"] for i in range(len(_OUTS)))
```
